# Optimizing a Trainium2 kernel written in Bass

```python
import math
import jax, jax.numpy as jnp
from jax import lax
import numpy as np

D_MODEL = 1024
BATCH = 1
SEQ = 512
DEPTH = 2
DEC_BATCH = 8
DEC_SEQ = 8
PAST_LEN = 1024
PAGE_SIZE = 128

N_MIXERS = 2
N_ATTN_LAYERS = (DEPTH + 1) // 2
N_RWKV_LAYERS = DEPTH // 2
HEAD_DIM = 64
N_HEADS = D_MODEL // HEAD_DIM
N_KV_HEADS = 4
GROUP = N_HEADS // N_KV_HEADS
WINDOW = 128
BLOCK = WINDOW
N_BUCKETS = 32
MAX_DISTANCE = 128
RWKV_HEAD = 64
RWKV_HEADS = D_MODEL // RWKV_HEAD
LORA_DECAY = 64
LORA_AAA = 64
LORA_MV = 32
LORA_GATE = 160
GN_EPS = 64e-5
D_FF = -(-8 * D_MODEL // (3 * 256)) * 256
ALPHA = (2 * DEPTH) ** 0.25
BETA = (8 * DEPTH) ** -0.25
LN_EPS = 1e-5

kernel_name = 'hybrid_swa_sink_rwkv7_deepnorm_step'

def layer_norm(x, g, b):
    xf = x.astype(jnp.float32)
    mu = xf.mean(-1, keepdims=True)
    var = jnp.square(xf - mu).mean(-1, keepdims=True)
    return ((xf - mu) * lax.rsqrt(var + LN_EPS) * g + b).astype(x.dtype)

def t5_bucket(d):
    d = jnp.maximum(d, 0)
    exact = N_BUCKETS // 2
    df = jnp.maximum(d, 1).astype(jnp.float32)
    large = exact + (jnp.log(df / exact) / math.log(MAX_DISTANCE / exact)
                     * (N_BUCKETS - exact)).astype(jnp.int32)
    return jnp.where(d < exact, d, jnp.minimum(large, N_BUCKETS - 1))

def rel_bias_for(d, rel_bias):
    b = rel_bias[t5_bucket(d)]
    return jnp.moveaxis(b, -1, 0).reshape((N_KV_HEADS, GROUP) + d.shape)

def sink_attention(q, k, v, d, valid, sinks, rel_bias):
    s = jnp.einsum('...qkgd,...skd->...kgqs', q, k).astype(jnp.float32) * HEAD_DIM ** -0.5
    s = s + rel_bias_for(d, rel_bias).astype(jnp.float32)
    s = jnp.where(valid, s, -jnp.inf)
    sink = jnp.broadcast_to(sinks.astype(jnp.float32).reshape(N_KV_HEADS, GROUP, 1, 1),
                            s.shape[:-1] + (1,))
    p = jax.nn.softmax(jnp.concatenate([s, sink], axis=-1), axis=-1)[..., :-1]
    return jnp.einsum('...kgqs,...skd->...qkgd', p.astype(v.dtype), v)

def qkv_proj(x, w_qkv, b_qkv):
    lead = x.shape[:-1]
    qkv = x @ w_qkv + b_qkv
    nq, nk = N_HEADS * HEAD_DIM, N_KV_HEADS * HEAD_DIM
    q = qkv[..., :nq].reshape(lead + (N_KV_HEADS, GROUP, HEAD_DIM))
    k = qkv[..., nq:nq + nk].reshape(lead + (N_KV_HEADS, HEAD_DIM))
    v = qkv[..., nq + nk:].reshape(lead + (N_KV_HEADS, HEAD_DIM))
    return q, k, v

def swa_prompt(x, w_qkv, b_qkv, w_o, b_o, sinks, rel_bias):
    B, T, _ = x.shape
    nb = T // BLOCK
    q, k, v = qkv_proj(x, w_qkv, b_qkv)

    def band(t):
        prev = jnp.pad(t[:, :T - BLOCK], ((0, 0), (BLOCK, 0), (0, 0), (0, 0)))
        return jnp.concatenate([prev.reshape(B, nb, BLOCK, N_KV_HEADS, HEAD_DIM),
                                t.reshape(B, nb, BLOCK, N_KV_HEADS, HEAD_DIM)], axis=2)

    qi = jnp.arange(BLOCK)[:, None]
    sj = jnp.arange(2 * BLOCK)[None, :]
    d = qi + BLOCK - sj
    blk = jnp.arange(nb)[:, None, None]
    valid = (d >= 0) & (d < WINDOW) & (blk * BLOCK + sj - BLOCK >= 0)
    o = sink_attention(q.reshape(B, nb, BLOCK, N_KV_HEADS, GROUP, HEAD_DIM), band(k), band(v),
                       d, valid[:, None, None], sinks, rel_bias)
    y = o.reshape(B, T, N_HEADS * HEAD_DIM) @ w_o + b_o
    return y, k[:, T - WINDOW:], v[:, T - WINDOW:]

def swa_sample(x, ck, cv, w_qkv, b_qkv, w_o, b_o, sinks, rel_bias):
    B, T, _ = x.shape
    L = ck.shape[1]
    q, k, v = qkv_proj(x, w_qkv, b_qkv)
    keys = jnp.concatenate([ck, k.astype(ck.dtype)], axis=1)
    vals = jnp.concatenate([cv, v.astype(cv.dtype)], axis=1)
    d = jnp.arange(T)[:, None] + L - jnp.arange(L + T)[None, :]
    valid = (d >= 0) & (d < WINDOW)
    o = sink_attention(q, keys, vals, d, valid, sinks, rel_bias)
    y = o.reshape(B, T, N_HEADS * HEAD_DIM) @ w_o + b_o
    return y, keys[:, T:], vals[:, T:]

def rwkv7_time_mix(x, x_prev, s0, v_first, mix, w_rkv, w0, w1, w2, a0, a1, a2,
                   g1, g2, k_k, k_a, r_k, ln_w, ln_b, w_o, vres):
    B, T, D = x.shape
    xx = jnp.concatenate([x_prev[:, None].astype(x.dtype), x[:, :-1]], axis=1) - x
    xr, xw, xk, xv, xa, xg = (x + xx * mix[c] for c in range(6))
    r = xr @ w_rkv[0]
    k = xk @ w_rkv[1]
    v = xv @ w_rkv[2]
    w = -jax.nn.softplus(-(w0 + jnp.tanh(xw @ w1) @ w2)) - 0.5
    if vres is None:
        v_first = v
    else:
        v0, v1, v2 = vres
        v = v + (v_first - v) * jax.nn.sigmoid(v0 + (xv @ v1) @ v2)
    a = jax.nn.sigmoid(a0 + (xa @ a1) @ a2)
    g = jax.nn.sigmoid(xg @ g1) @ g2

    def heads(t):
        return t.reshape(B, T, RWKV_HEADS, RWKV_HEAD).astype(jnp.float32)

    kk = heads(k * k_k)
    kk = kk / jnp.maximum(jnp.sqrt(jnp.sum(kk * kk, axis=-1, keepdims=True)), 1e-12)
    k = k * (1 + (a - 1) * k_a)
    rh, kh, vh, ah = heads(r), heads(k), heads(v), heads(a)
    decay = jnp.exp(-jnp.exp(heads(w)))

    def step(S, inp):
        r_t, d_t, k_t, v_t, kk_t, a_t = inp
        sa = jnp.einsum('bhvk,bhk->bhv', S, -kk_t)
        S = (S * d_t[:, :, None, :] + sa[..., None] * (kk_t * a_t)[:, :, None, :]
             + v_t[..., None] * k_t[:, :, None, :])
        return S, jnp.einsum('bhvk,bhk->bhv', S, r_t)

    seq = tuple(jnp.moveaxis(t, 1, 0) for t in (rh, decay, kh, vh, kk, ah))
    S, o = lax.scan(step, s0.astype(jnp.float32), seq)
    o = jnp.moveaxis(o, 0, 1)
    mu = o.mean(-1, keepdims=True)
    var = jnp.square(o - mu).mean(-1, keepdims=True)
    o = ((o - mu) * lax.rsqrt(var + GN_EPS)).reshape(B, T, D) * ln_w + ln_b
    bonus = (jnp.sum(rh * kh * r_k.astype(jnp.float32), axis=-1, keepdims=True) * vh).reshape(B, T, D)
    y = ((o + bonus) * g).astype(x.dtype) @ w_o
    return y, v_first, S.astype(s0.dtype), x[:, -1]

def swiglu(x, w_gu, w_down):
    gu = x @ w_gu
    return (jax.nn.silu(gu[..., :D_FF]) * gu[..., D_FF:]) @ w_down

def trunk(x, win_k, win_v, shift, wkv, P):
    prompt = win_k is None
    B = x.shape[0]
    v_first = None
    nk, nv, ns, nw = [], [], [], []
    for i in range(DEPTH):
        j = i // N_MIXERS
        if i % N_MIXERS == 0:
            args = (P['attn_w_qkv'][j], P['attn_b_qkv'][j], P['attn_w_o'][j], P['attn_b_o'][j],
                    P['attn_sinks'][j], P['rel_bias'])
            if prompt:
                h, k_buf, v_buf = swa_prompt(x, *args)
            else:
                h, k_buf, v_buf = swa_sample(x, win_k[j], win_v[j], *args)
            nk.append(k_buf)
            nv.append(v_buf)
        else:
            if prompt:
                x_prev = jnp.zeros((B, D_MODEL), x.dtype)
                s0 = jnp.zeros((B, RWKV_HEADS, RWKV_HEAD, RWKV_HEAD), x.dtype)
            else:
                x_prev, s0 = shift[j], wkv[j]
            vres = None if j == 0 else (P['rwkv_v0'][j - 1], P['rwkv_v1'][j - 1], P['rwkv_v2'][j - 1])
            h, v_first, s_new, last = rwkv7_time_mix(
                x, x_prev, s0, v_first, P['rwkv_mix'][j], P['rwkv_w_rkv'][j],
                P['rwkv_w0'][j], P['rwkv_w1'][j], P['rwkv_w2'][j],
                P['rwkv_a0'][j], P['rwkv_a1'][j], P['rwkv_a2'][j],
                P['rwkv_g1'][j], P['rwkv_g2'][j], P['rwkv_k_k'][j], P['rwkv_k_a'][j],
                P['rwkv_r_k'][j], P['rwkv_ln_w'][j], P['rwkv_ln_b'][j], P['rwkv_w_o'][j], vres)
            ns.append(last)
            nw.append(s_new)
        x = layer_norm(ALPHA * x + h, P['ln_g'][i, 0], P['ln_b'][i, 0])
        x = layer_norm(ALPHA * x + swiglu(x, P['ffn_w_gu'][i], P['ffn_w_down'][i]),
                       P['ln_g'][i, 1], P['ln_b'][i, 1])
    return x, jnp.stack(nk), jnp.stack(nv), jnp.stack(ns), jnp.stack(nw)

def setup_inputs(seed: int = 0) -> dict:
    key = jax.random.key(seed)
    keys = jax.random.split(key, 48)
    it = (keys[i] for i in range(48))

    def nrm(shape, scale):
        return scale * jax.random.normal(next(it), shape, jnp.float32)

    def uni(shape, lo, hi):
        return jax.random.uniform(next(it), shape, jnp.float32, lo, hi)

    NA, NR, D = N_ATTN_LAYERS, N_RWKV_LAYERS, D_MODEL
    QKV = (N_HEADS + 2 * N_KV_HEADS) * HEAD_DIM
    win_rows = min(WINDOW, PAST_LEN)
    return {
        'x_prompt': nrm((BATCH, SEQ, D), 1.0),
        'x_sample': nrm((DEC_BATCH, DEC_SEQ, D), 1.0),
        'cache_win_k': nrm((NA, DEC_BATCH, win_rows, N_KV_HEADS, HEAD_DIM), 1.0),
        'cache_win_v': nrm((NA, DEC_BATCH, win_rows, N_KV_HEADS, HEAD_DIM), 1.0),
        'state_shift': nrm((NR, DEC_BATCH, D), 1.0),
        'state_wkv': nrm((NR, DEC_BATCH, RWKV_HEADS, RWKV_HEAD, RWKV_HEAD), 0.3),
        'rel_bias': nrm((N_BUCKETS, N_HEADS), 0.5),
        'ln_g': 1.0 + nrm((DEPTH, 2, D), 0.05),
        'ln_b': nrm((DEPTH, 2, D), 0.02),
        'attn_w_qkv': nrm((NA, D, QKV), D ** -0.5),
        'attn_b_qkv': nrm((NA, QKV), 0.02),
        'attn_w_o': nrm((NA, N_HEADS * HEAD_DIM, D), BETA * (N_HEADS * HEAD_DIM) ** -0.5),
        'attn_b_o': nrm((NA, D), 0.02),
        'attn_sinks': nrm((NA, N_HEADS), 1.0),
        'rwkv_mix': uni((NR, 6, D), 0.0, 1.0),
        'rwkv_w_rkv': nrm((NR, 3, D, D), D ** -0.5),
        'rwkv_w0': uni((NR, D), -6.0, -1.0),
        'rwkv_w1': nrm((NR, D, LORA_DECAY), D ** -0.5),
        'rwkv_w2': nrm((NR, LORA_DECAY, D), 0.1 * LORA_DECAY ** -0.5),
        'rwkv_a0': nrm((NR, D), 0.1),
        'rwkv_a1': nrm((NR, D, LORA_AAA), D ** -0.5),
        'rwkv_a2': nrm((NR, LORA_AAA, D), LORA_AAA ** -0.5),
        'rwkv_v0': nrm((NR - 1, D), 0.1),
        'rwkv_v1': nrm((NR - 1, D, LORA_MV), D ** -0.5),
        'rwkv_v2': nrm((NR - 1, LORA_MV, D), LORA_MV ** -0.5),
        'rwkv_g1': nrm((NR, D, LORA_GATE), D ** -0.5),
        'rwkv_g2': nrm((NR, LORA_GATE, D), LORA_GATE ** -0.5),
        'rwkv_k_k': 0.85 + nrm((NR, D), 0.05),
        'rwkv_k_a': 1.0 + nrm((NR, D), 0.05),
        'rwkv_r_k': nrm((NR, RWKV_HEADS, RWKV_HEAD), 0.1),
        'rwkv_ln_w': 1.0 + nrm((NR, D), 0.05),
        'rwkv_ln_b': nrm((NR, D), 0.02),
        'rwkv_w_o': nrm((NR, D, D), BETA * D ** -0.5),
        'ffn_w_gu': nrm((DEPTH, D, 2 * D_FF), D ** -0.5),
        'ffn_w_down': nrm((DEPTH, D_FF, D), BETA * D_FF ** -0.5),
    }

def reference(x_prompt, x_sample, cache_win_k, cache_win_v, state_shift, state_wkv,
              rel_bias, ln_g, ln_b, attn_w_qkv, attn_b_qkv, attn_w_o, attn_b_o, attn_sinks,
              rwkv_mix, rwkv_w_rkv, rwkv_w0, rwkv_w1, rwkv_w2, rwkv_a0, rwkv_a1, rwkv_a2,
              rwkv_v0, rwkv_v1, rwkv_v2, rwkv_g1, rwkv_g2, rwkv_k_k, rwkv_k_a, rwkv_r_k,
              rwkv_ln_w, rwkv_ln_b, rwkv_w_o, ffn_w_gu, ffn_w_down):
    P = dict(rel_bias=rel_bias, ln_g=ln_g, ln_b=ln_b,
             attn_w_qkv=attn_w_qkv, attn_b_qkv=attn_b_qkv, attn_w_o=attn_w_o,
             attn_b_o=attn_b_o, attn_sinks=attn_sinks,
             rwkv_mix=rwkv_mix, rwkv_w_rkv=rwkv_w_rkv, rwkv_w0=rwkv_w0, rwkv_w1=rwkv_w1,
             rwkv_w2=rwkv_w2, rwkv_a0=rwkv_a0, rwkv_a1=rwkv_a1, rwkv_a2=rwkv_a2,
             rwkv_v0=rwkv_v0, rwkv_v1=rwkv_v1, rwkv_v2=rwkv_v2, rwkv_g1=rwkv_g1,
             rwkv_g2=rwkv_g2, rwkv_k_k=rwkv_k_k, rwkv_k_a=rwkv_k_a, rwkv_r_k=rwkv_r_k,
             rwkv_ln_w=rwkv_ln_w, rwkv_ln_b=rwkv_ln_b, rwkv_w_o=rwkv_w_o,
             ffn_w_gu=ffn_w_gu, ffn_w_down=ffn_w_down)
    y_prompt, pk, pv, ps, pw = trunk(x_prompt, None, None, None, None, P)
    y_sample, sk, sv, ss, sw = trunk(x_sample, cache_win_k, cache_win_v, state_shift, state_wkv, P)
    return (y_prompt, y_sample, pk, pv, ps, pw, sk, sv, ss, sw)


_drawn_inputs = setup_inputs


def setup_inputs(seed=0):
    import zlib

    import numpy as np

    out = dict(_drawn_inputs(seed))
    spreads = {}
    factors = {'attn_b_qkv': 2.895,
     'attn_sinks': 8.0,
     'rwkv_w1': 8.0,
     'rwkv_w2': 8.0,
     'rwkv_ln_w': 5.71,
     'rwkv_ln_b': 21.649}
    for name, (base, spread) in spreads.items():
        noise = np.random.default_rng([zlib.crc32(name.encode()), seed]).standard_normal(out[name].shape)
        drawn = base * np.exp(spread * noise) if base else spread * noise
        out[name] = __import__('jax').numpy.asarray(drawn.astype(out[name].dtype))
    for name, factor in factors.items():
        out[name] = (out[name] * factor).astype(out[name].dtype)
    return out
```

```python
from contextlib import ExitStack

import numpy as np

import concourse.bass as bass
from concourse import mybir
from concourse.alu_op_type import AluOpType as ALU

F32 = mybir.dt.float32
F32R = mybir.dt.float32r
ACT = mybir.ActivationFunctionType
AX_X = mybir.AxisListType.X

P = 128
D = 1024
KB = D // P
SEQ = 512
DB, DT = 8, 8
NS = DB * DT
T = SEQ + NS
TH = T // 2
HEADS = 16
KV = 4
GROUP = HEADS // KV
HD = 64
WIN = 128
NBUCKET = 32
FF = 2816
FB = FF // P
QKV = (HEADS + 2 * KV) * HD
QB = QKV // P
KEYS = WIN + DT
CH = 64
NCH = SEQ // CH
PADP = NCH * (CH + 1)
PADT = PADP + DB * (DT + 1)
NPAIR = HEADS // 2
LEVELS = 6
L_DECAY, L_AAA, L_GATE = 64, 64, 160
ALPHA = 4 ** 0.25
KAPPA = float(np.exp(-0.5))
NEG = -1e30
TOEP = 384

(R_LNG, R_LNB, R_BQ, R_BKV, R_BO, R_MIX, R_W0, R_A0, R_KK, R_KA, R_RK, R_GW, R_GB, R_SHIFT) = (
    0, 4, 8, 9, 10, 11, 17, 18, 19, 20, 21, 22, 23, 24)
NROW = 32


def constant_layout():
    sizes = [("ident", P), ("ident2", HD), ("bdones", P), ("mean", P), ("strict_p", P), ("incl_p", HD),
             ("strict_s", P), ("incl_s", HD), ("levels", LEVELS * P), ("level0", HD), ("seqmask", DB), ("headmask", 2),
             ("eps", 2), ("reset", PADT)]
    at, out = 0, {}
    for name, n in sizes:
        out[name] = (at, at + n)
        at += n
    return out, at


def t5_bucket(d):
    exact = NBUCKET // 2
    df = np.maximum(d, 1).astype(np.float32)
    large = exact + (np.log(df / np.float32(exact)) / np.float32(np.log(WIN / exact))
                     * np.float32(NBUCKET - exact)).astype(np.int32)
    return np.where(d < exact, d, np.minimum(large, NBUCKET - 1))


def constants():
    cols, width = constant_layout()
    c = np.zeros((P, width), np.float32)

    def put(name, a):
        lo, hi = cols[name]
        c[:a.shape[0], lo:hi] = a.reshape(a.shape[0], -1)

    p, q = np.arange(P)[:, None], np.arange(P)[None, :]
    s, t = p % HD, q % HD
    same_head = (p // HD) == (q // HD)
    same_seq = (s // DT) == (t // DT)
    tc = np.arange(HD)[None, :]
    put("ident", np.eye(P))
    put("ident2", (s == tc))
    put("bdones", same_head)
    put("mean", np.full((P, P), 1.0 / D))
    put("strict_p", same_head & (s < t))
    put("incl_p", s <= tc)
    put("strict_s", same_head & (s < t) & same_seq)
    put("incl_s", (s <= tc) & ((s // DT) == (tc // DT)))
    lv = np.zeros((P, LEVELS, P))
    for level in range(LEVELS):
        b = 1 << level
        lv[:, level] = same_head & (s // (2 * b) == t // (2 * b)) & ((s // b) % 2 == 0) & ((t // b) % 2 == 1)
    put("levels", lv)
    put("level0", (s // 2 == tc // 2) & (s % 2 == 0) & (tc % 2 == 1))
    put("seqmask", (s // DT) == np.arange(DB)[None, :])
    put("headmask", (p // HD) == np.arange(2)[None, :])
    put("eps", np.tile([1e-5, 64e-5], (P, 1)))
    reset = np.ones(PADT)
    reset[0:PADP:CH + 1] = 0
    reset[PADP:PADT:DT + 1] = 0
    put("reset", np.tile(reset, (P, 1)))
    return c


def bucket_table():
    onehot = np.zeros((NBUCKET + 1, TOEP), np.float32)
    for y in range(TOEP):
        d = 2 * WIN - 1 - y
        onehot[t5_bucket(np.array(d)) if 0 <= d < WIN else NBUCKET, y] = 1
    return onehot


def build_program(nc, ins, outs, scratch):
    cols, width = constant_layout()
    ctx = ExitStack()
    with ctx:
        def sb(name, shape, dt=F32):
            return ctx.enter_context(nc.sbuf_tensor(name, shape, dt))

        def sem(name):
            return ctx.enter_context(nc.semaphore(name))

        def region(*tensors):
            with ExitStack() as scope:
                return [scope.enter_context(nc.sbuf_tensor(n, s, d)) for n, s, d in tensors]

        cst = sb("cst", [P, width])

        def const(name):
            lo, hi = cols[name]
            return cst[:, lo:hi]

        prm = sb("prm", [P, KB, NROW])
        bqkv = sb("bqkv", [P, QB])
        sink = sb("sink", [P, HEADS])
        sink_s = sb("sink_s", [P, 1])
        credit = sb("credit", [P, 6])
        omka = sb("omka", [P, KB])

        KMAX = FB // 2
        dense = [("x", [P, KB, T], F32), ("raw", [P, 2, KMAX, P], F32), ("wh", [P, 2, KMAX, P], F32R),
                 ("wl", [P, 2, KMAX, P], F32R), ("xh", [P, KB, T], F32R), ("xl", [P, KB, T], F32R),
                 ("lnw", [P, 5, T], F32)]
        NP2 = NPAIR // 2
        wkv1 = [("kk", [P, KB, T], F32), ("bb", [P, KB, T], F32), ("cc", [P, KB, PADT], F32),
                ("zr", [P, NPAIR, 2, CH], F32), ("zbd", [P, NPAIR, 2, CH], F32), ("bbd", [P, NPAIR, 2, CH], F32),
                ("kbd", [P, NPAIR, 2, CH], F32), ("vbd", [P, NPAIR, 2, CH], F32),
                ("btm", [P, NPAIR, P], F32), ("ktm", [P, NPAIR, P], F32), ("vtm", [P, NPAIR, P], F32),
                ("vtc", [P, NPAIR, CH], F32), ("lzb", [P, NPAIR, 2, CH], F32), ("lzk", [P, NPAIR, 2, CH], F32)]
        kk, bb, cc, zr, zbd, bbd, kbd, vbd, btm, ktm, vtm, vtc, lzb, lzk = region(*wkv1)
        x, raw, wh, wl, xh, xl, lnw = [ctx.enter_context(nc.sbuf_tensor(n, s, d)) for n, s, d in dense]
        w1s, a1s, g1s = lnw[:, 0, 0:512].rearrange("p (k n) -> p k n", k=KB), \
            lnw[:, 1, 0:512].rearrange("p (k n) -> p k n", k=KB), \
            lnw[:, 2:5, :].rearrange("p a n -> p (a n)")[:, 0:KB * L_GATE].rearrange("p (k n) -> p k n", k=KB)

        vnb = lnw.rearrange("p a n -> p (a n)")[0:DT, 0:DB * KV * HD].rearrange("p (b n) -> p b n", b=DB)

        xnat, prow, relb, onehot, toep_sb = region(("xnat", [P, 5, D], F32), ("prow", [P, D], F32),
                                           ("relb", [P, HEADS], F32), ("onehot", [NBUCKET + 1, TOEP], F32), ("toep_sb", [HEADS, TOEP], F32))
        (qkvT, biasT, bias_s, S, PT, vtok, ktok, kvnew, ck, cv, ckT, qs, stat) = region(
            ("qkvT", [P, QB, T], F32), ("biasT", [P, HEADS, 2 * WIN], F32), ("bias_s", [P, KEYS], F32),
            ("S", [P, 2, 8 * KEYS], F32), ("PT", [P, 2, 8 * P], F32), ("vtok", [P, 4, KV * HD], F32),
            ("ktok", [P, KV * HD], F32), ("kvnew", [NS, 2, KV * HD], F32), ("ck", [P, DB, KV * HD], F32),
            ("cv", [P, DB, KV * HD], F32), ("ckT", [P, 2, DB, KEYS], F32), ("qs", [P, 2, DB, GROUP * DT], F32), ("stat", [P, 2, 5, 8], F32))
        hh, hl = region(("hh", [P, FB, T], F32R), ("hl", [P, FB, T], F32R))
        gbuf, hbuf = lnw[:, 0:2, :], lnw[:, 2:4, :]
        yout, = region(("yout", [P, 5, D], F32))
        rr, kx, vv, sg = [ctx.enter_context(nc.sbuf_tensor(n, s, F32)) for n, s in (
            ("rr", [P, KB, T]), ("kx", [P, KB, T]), ("vv", [P, KB, T]), ("sg", [P, 2, T]))]
        xx, mf, mt, twa, wa2, shc, sho = region(
            ("xx", [P, KB, T], F32), ("mf", [P, 2, T], F32), ("mt", [P, 2, T], F32), ("twa", [P, T], F32),
            ("wa2", [P, D], F32), ("shc", [P, KB, 9], F32), ("sho", [9, D], F32))
        g2a, g2b, fin = region(("g2a", [P, D], F32), ("g2b", [L_GATE - P, D], F32), ("fin", [P, 6, T], F32))
        lrb, lrk, ef, pc, kt, stat_out = [ctx.enter_context(nc.sbuf_tensor(n, s, F32)) for n, s in (
            ("lrb", [P, NPAIR, CH]), ("lrk", [P, NPAIR, CH]), ("ef", [P, 3, KB, CH]), ("pc", [P, NPAIR, DB]), ("kt", [P, NPAIR, CH]), ("stat_out", [P, NPAIR, HD]))]
        spc = bb[:, :, 0:SEQ].rearrange("p a (b k) -> p a b k", b=DB)
        lm, xc, xtb, yc, ybd, S_c, sbd = region(
            ("lm", [P, NPAIR, P], F32), ("xc", [P, 2, 2, NP2, CH], F32), ("xtb", [P, NPAIR, 2, CH], F32),
            ("yc", [P, NPAIR, CH], F32), ("ybd", [P, NPAIR, 2, CH], F32), ("S_c", [P, NPAIR, HD], F32),
            ("sbd", [P, NPAIR, 2, HD], F32))
        n0bd, s0bd, dpc = region(("n0bd", [P, 2, DB, 2, HD], F32), ("s0bd", [P, 2, DB, P], F32),
                                 ("dpc", [P, 2, DB, HD], F32))
        uc, sac, sabd = yc, yc, ybd
        ef2 = ef[:].rearrange("p a k n -> p (a k n)")[:, 0:2 * T].rearrange("p (a n) -> p a n", a=2)
        nrm = [t.rearrange("p a b -> p (a b)")[:, 0:T] for t in (lm[:], xtb[:].rearrange("p a h n -> p a (h n)"))]

        def bkm(p, which):
            return n0bd[:, p % 2, :, which, :]

        ps = ctx.enter_context(nc.psum_tensor("ps", [P, 8, 512], F32))
        halves = [(0, 0), (1, TH)]
        top, low = slice(0, HD), slice(HD, P)

        def two(ap):
            return ap.rearrange("p a (h n) -> p (a h) n", h=2)

        def acc(a):
            return ps[:, 2 * a:2 * a + 2, 0:TH]

        def col(row, j):
            return prm[:, j, row:row + 1]

        class Phase:
            def __init__(self, name, slabs, kblocks, dmas=1):
                self.name, self.slabs, self.kb, self.dmas = name, slabs, kblocks, dmas
                self.ffn_up, self.ffn_down = name.startswith("gu"), name.startswith("dn")

        PH = {p.name: p for p in (
            Phase("qkv", QB, KB, 2), Phase("wo", KB, KB, 4), Phase("gu0", 2 * FB, KB), Phase("dn0", 2 * KB, KMAX),
            Phase("r", KB, KB), Phase("k", KB, KB), Phase("v", KB, KB),
            Phase("ro", KB, KB), Phase("gu1", 2 * FB, KB), Phase("dn1", 2 * KB, KMAX))}
        order = list(PH.values())
        n = m = g = r = 0
        for ph in order:
            ph.n0, ph.m0, ph.g0, ph.r0 = n, m, g, r
            n += ph.slabs
            r += 16 * ph.dmas * (ph.slabs // 2)
            if ph.ffn_up:
                g += FB
            else:
                m += ph.slabs // (2 if ph.ffn_down else 1)
            ph.n1, ph.m1 = n, m

        def after(name):
            return order[[p.name for p in order].index(name) + 1]

        raw_in = [sem("raw_in0"), sem("raw_in1")]
        raw_free = sem("raw_free")
        hi_done = sem("hi_done")
        wslot_free = sem("wslot_free")
        acc_free = sem("acc_free")
        gate_free = sem("gate_free")
        up_free = sem("up_free")
        hid_hi = sem("hid_hi")
        hid_lo = sem("hid_lo")
        op_hi = sem("op_hi")
        op_ready = sem("op_ready")
        stored = sem("stored")
        sems = {}

        def ev(name):
            if name not in sems:
                sems[name] = sem(name)
            return sems[name]

        KV_STORES = 16 * (2 + 2 * DB)
        STATE_STORES = 16 * (2 + 2 * NPAIR)
        outs_stored = [0]
        OP = {"x0": 0, "f0": 1, "r": 2, "k": 3, "v": 4, "z": 5, "f1": 6}
        block = ctx.enter_context(nc.Block())

        @block.sync
        def _(sp):
            sp.dma_start(xnat[:, 0:4, :], ins["x_prompt"].rearrange("o (t p) d -> p (o t) d", p=P)).then_inc(ev("x_in"), 16)
            sp.dma_start(xnat[0:NS, 4, :], ins["x_sample"].rearrange("b t d -> (b t) d")).then_inc(ev("x_in"), 16)
            sp.dma_start(cst[:], ins["constants"]).then_inc(ev("c_in"), 16)
            sp.wait_ge(ev("row_zero"), 2)
            rows = [(R_LNG, 4, ins["ln_g"].rearrange("a b d -> (a b) d")), (R_LNB, 4, ins["ln_b"].rearrange("a b d -> (a b) d")),
                    (R_BO, 1, ins["attn_b_o"]), (R_MIX, 6, ins["rwkv_mix"].rearrange("a c d -> (a c) d")),
                    (R_W0, 1, ins["rwkv_w0"]), (R_A0, 1, ins["rwkv_a0"]), (R_KK, 1, ins["rwkv_k_k"]),
                    (R_KA, 1, ins["rwkv_k_a"]), (R_RK, 1, ins["rwkv_r_k"].rearrange("a h d -> a (h d)")),
                    (R_GW, 1, ins["rwkv_ln_w"]), (R_GB, 1, ins["rwkv_ln_b"]),
                    (R_SHIFT, DB, ins["state_shift"].rearrange("a b d -> (a b) d"))]
            for at, count, src in rows:
                sp.dma_start(prow[at:at + count, :], src).then_inc(ev("p_in"), 16)
            for G in range(2):
                sp.dma_start(prow[R_BQ:R_BQ + 1, G * 512:(G + 1) * 512].rearrange("p (i h d) -> p i h d", i=GROUP, h=2),
                             ins["attn_b_qkv"][:, G * 512:(G + 1) * 512].rearrange("a (h i d) -> a i h d", h=2, i=GROUP)
                             ).then_inc(ev("p_in"), 16)
            sp.dma_start(prow[R_BKV:R_BKV + 1, 0:512], ins["attn_b_qkv"][:, D:QKV]).then_inc(ev("p_in"), 16)
            sp.dma_start(relb[0:NBUCKET, :], ins["rel_bias"]).then_inc(ev("b_in"), 16)
            sp.dma_start(onehot[:], ins["onehot"]).then_inc(ev("b_in"), 16)
            sp.dma_start(sink[:], bass.AP(tensor=ins["attn_sinks"].tensor, offset=0, ap=[[0, P], [1, HEADS]])).then_inc(ev("s_in"), 16)
            sp.dma_start(sink_s[:], bass.AP(tensor=ins["attn_sinks"].tensor, offset=0, ap=[[1, HEADS], [0, DT], [1, 1]])
                         ).then_inc(ev("s_in"), 16)

            sp.dma_start(ck[:], ins["cache_win_k"].rearrange("a b w h d -> w (a b) (h d)")).then_inc(ev("cache_in"), 16)
            sp.dma_start(cv[:], ins["cache_win_v"].rearrange("a b w h d -> w (a b) (h d)")).then_inc(ev("cache_in"), 16)

            wq = ins["attn_w_qkv"].rearrange("a (k p) n -> p (a k) n", p=P)
            for G in range(2):
                heads = wq[:, :, G * 512:(G + 1) * 512].rearrange("p k (h i d) -> p k h (i d)", h=2, i=GROUP)
                with nc.sync.Fori(0, 2) as i:
                    for s in range(2):
                        sp.wait_ge(raw_free, 2 * i + (4 * G + s + 1))
                        for h in range(2):
                            sp.dma_start(raw[:, s, 0:KB, h * HD:(h + 1) * HD],
                                         heads[:, :, h, bass.ds((2 * i + s) * HD, HD)]).then_inc(raw_in[s], 16)
            with nc.sync.Fori(0, 2) as i:
                for s in range(2):
                    sp.wait_ge(raw_free, 2 * i + (KB + s + 1))
                    for h in range(2):
                        sp.dma_start(raw[:, s, 0:KB, h * HD:(h + 1) * HD],
                                     wq[:, :, bass.ds((2 * i + s) * P + (D + h * HD), HD)]).then_inc(raw_in[s], 16)

            wo = ins["attn_w_o"].rearrange("a (G h i d) n -> h d (a G) i n", G=2, h=2, i=GROUP)
            with nc.sync.Fori(0, KB // 2) as i:
                for s in range(2):
                    sp.wait_ge(raw_free, 2 * i + (PH["wo"].n0 + s + 1))
                    for h in range(2):
                        for G in range(2):
                            sp.dma_start(raw[h * HD:(h + 1) * HD, s, G * GROUP:(G + 1) * GROUP, :],
                                         wo[h, :, G, :, bass.ds((2 * i + s) * P, P)]).then_inc(raw_in[s], 16)

            def ffn(up, down, layer):
                wgu = ins["ffn_w_gu"][layer].rearrange("(k p) (u n) -> u p k n", p=P, u=2)
                with nc.sync.Fori(0, FB) as i:
                    for s in range(2):
                        sp.wait_ge(raw_free, 2 * i + (up.n0 + s + 1))
                        sp.dma_start(raw[:, s, 0:KB, :], wgu[s, :, :, bass.ds(i * P, P)]).then_inc(raw_in[s], 16)
                wd = ins["ffn_w_down"][layer].rearrange("(u k p) n -> u p k n", p=P, u=2)
                with nc.sync.Fori(0, KB) as i:
                    for s in range(2):
                        sp.wait_ge(raw_free, 2 * i + (down.n0 + s + 1))
                        sp.dma_start(raw[:, s, :, :], wd[s, :, :, bass.ds(i * P, P)]).then_inc(raw_in[s], 16)

            ffn(PH["gu0"], PH["dn0"], 0)

            def square(ph, w):
                v = w.rearrange("(k p) n -> p k n", p=P)
                with nc.sync.Fori(0, KB // 2) as i:
                    for s in range(2):
                        sp.wait_ge(raw_free, 2 * i + (ph.n0 + s + 1))
                        sp.dma_start(raw[:, s, 0:KB, :], v[:, :, bass.ds((2 * i + s) * P, P)]).then_inc(raw_in[s], 16)

            for name, c in (("r", 0), ("k", 1), ("v", 2)):
                square(PH[name], ins["rwkv_w_rkv"][0, c])
            sp.wait_ge(ev("state_kept"), STATE_STORES)
            square(PH["ro"], ins["rwkv_w_o"][0])
            ffn(PH["gu1"], PH["dn1"], 1)

        @block.gpsimd
        def _(pool):
            nc.gpsimd.memset(prow[:], 0.0).then_inc(ev("row_zero"), 1)
            nc.gpsimd.memset(relb[:], NEG).then_inc(ev("row_zero"), 1)
            for at, free in enumerate((raw_free, wslot_free, acc_free, gate_free, up_free, hid_hi)):
                nc.gpsimd.memset(credit[:, at:at + 1], 0.0).then_inc(free, 2)

            def split_low(ph):
                with nc.gpsimd.Fori(0, ph.slabs // 2) as i:
                    for s in range(2):
                        pool.wait_ge(hi_done, 2 * i + (ph.n0 + s + 1))
                        nc.gpsimd.tensor_tensor(wl[:, s, 0:ph.kb, :], raw[:, s, 0:ph.kb, :],
                                                wh[:, s, 0:ph.kb, :].bitcast(F32), ALU.subtract).then_inc(raw_free, 1)

            for name in ("qkv", "wo", "gu0", "dn0", "r", "k", "v"):
                split_low(PH[name])

            pool.wait_ge(ev("prep"), KB)
            pool.wait_ge(ev("shift_kept"), 32)
            for t in (ybd, xtb, bbd):
                nc.gpsimd.memset(t[:], 0.0)
            nc.gpsimd.memset(zbd[:], 0.0).then_inc(ev("sup"), 2)
            nc.gpsimd.memset(S_c[:], 0.0).then_inc(ev("c_kv"), 1)
            for g in range(2):
                nc.gpsimd.memset(sbd[:, g * NP2:(g + 1) * NP2], 0.0).then_inc(ev(f"sbd{g}"), 1)
            nc.gpsimd.memset(pc[:], 0.0).then_inc(ev("wkv_zero"), 1)

            def chunk(c, sample):
                tok = bass.ds(c * CH, CH)
                pool.wait_ge(ev("c_exp"), c + 1)
                pool.wait_ge(ev("sup"), 2 * c + 2)
                own = const("headmask").unsqueeze(1).unsqueeze(3).to_broadcast([P, NPAIR, 2, CH])
                nc.gpsimd.tensor_tensor(kt[:], kx[:, :, tok], ef[:, 2], ALU.mult).then_inc(ev("kt"), 1)
                nc.gpsimd.tensor_tensor(vbd[:], vv[:, :, tok].unsqueeze(2).to_broadcast([P, NPAIR, 2, CH]), own, ALU.mult)
                pool.wait_ge(ev("kt"), c + 1)
                nc.gpsimd.tensor_tensor(kbd[:], kt[:].unsqueeze(2).to_broadcast([P, NPAIR, 2, CH]), own, ALU.mult
                                        ).then_inc(ev("c_kv"), 1)
                for level in range(3 if sample else LEVELS):
                    for g in range(2):
                        if level == 0:
                            pool.wait_ge(ev("gram_b"), 2 * c + (g + 1))
                        else:
                            pool.wait_ge(ev(f"y{g}"), c * LEVELS + level)
                        pr = slice(g * NP2, (g + 1) * NP2)
                        nc.gpsimd.tensor_tensor(
                            lm[:, pr, :], lzb[:, pr].rearrange("p a h t -> p a (h t)"),
                            const("levels")[:, level * P:(level + 1) * P].unsqueeze(1).to_broadcast([P, NP2, P]),
                            ALU.mult).then_inc(ev(f"lm{g}"), 1)

            with nc.gpsimd.Fori(0, NCH) as c:
                chunk(c, False)
            pool.wait_ge(ev("state_out"), 1)
            nc.gpsimd.memset(n0bd[:], 0.0).then_inc(ev("n0_zero"), 1)
            pool.wait_ge(ev("s0_done"), 4)
            nc.gpsimd.memset(ybd[:], 0.0)
            nc.gpsimd.memset(xtb[:], 0.0).then_inc(ev("wkv_zero"), 1)
            chunk(NCH, True)

            for name in ("ro", "gu1", "dn1"):
                split_low(PH[name])

        @block.tensor
        def _(pe):
            mm = nc.tensor.matmul
            ident = const("ident")

            def slab(a, s, kb, high, low_, k0, first, last):
                for k in range(kb):
                    for w, o in ((wh, high), (wh, low_), (wl, high)):
                        for b, t0 in halves:
                            out = mm(ps[:, 2 * a + b, 0:TH], w[:, s, k, :], o[:, k0 + k, t0:t0 + TH],
                                     start=(first and k == 0 and w is wh and o is high),
                                     stop=(last and k == kb - 1 and w is wl))
                out.then_inc(wslot_free, 1)

            def product(name, high, low_):
                ph = PH[name]
                with nc.tensor.Fori(0, ph.slabs // 2) as i:
                    for s in range(2):
                        pe.wait_ge(raw_free, 2 * i + (ph.n0 + s + 3))
                        pe.wait_ge(acc_free, 2 * i + (ph.m0 + s + 1))
                        slab(s, s, ph.kb, high, low_, 0, True, True)

            def operand(name):
                pe.wait_ge(op_ready, KB * (OP[name] + 1))

            def ffn(i_ffn):
                up, down = PH[f"gu{i_ffn}"], PH[f"dn{i_ffn}"]
                operand(f"f{i_ffn}")
                with nc.tensor.Fori(0, FB // 2) as i:
                    for q in range(2):
                        for s, free in ((0, gate_free), (1, up_free)):
                            pe.wait_ge(raw_free, 4 * i + (up.n0 + 2 * q + s + 3))
                            pe.wait_ge(free, 2 * i + (up.g0 + q + 1))
                            slab(2 * q + s, s, KB, xh, xl, 0, True, True)
                pe.wait_ge(hid_lo, FB * (i_ffn + 1))
                with nc.tensor.Fori(0, KB // 2) as i:
                    for q in range(2):
                        pe.wait_ge(acc_free, 2 * i + (down.m0 + q + 1))
                        for s in range(2):
                            pe.wait_ge(raw_free, 4 * i + (down.n0 + 2 * q + s + 3))
                            slab(q, s, KMAX, hh, hl, s * KMAX, s == 0, s == 1)

            def norm(i_ln, ph):
                pe.wait_ge(acc_free, ph.m1 + 2)
                for j in range(KB):
                    for b, t0 in halves:
                        out = mm(ps[:, 4 + b, 0:TH], const("mean"), x[:, j, t0:t0 + TH], start=(j == 0), stop=(j == KB - 1))
                out.then_inc(ev("ln_mean"), 1)
                for j in range(KB):
                    pe.wait_ge(ev("ln_sq"), KB * i_ln + j + 1)
                    for b, t0 in halves:
                        out = mm(ps[:, 6 + b, 0:TH], const("mean"), lnw[:, 3 + j % 2, t0:t0 + TH], start=(j == 0), stop=(j == KB - 1))
                    out.then_inc(ev("ln_sum"), 1)

            pe.wait_ge(ev("c_in"), 16)
            pe.wait_ge(ev("x_in"), 32)
            for j in range(KB):
                if j >= 4:
                    pe.wait_ge(ev("xT_taken"), j - 3)
                for t in range(4):
                    out = nc.tensor.transpose(ps[:, j % 4, t * P:(t + 1) * P], xnat[:, t, j * P:(j + 1) * P], ident)
                out.then_inc(ev("xT"), 1)
            for j in range(KB):
                out = nc.tensor.transpose(ps[:, 4, j * NS:(j + 1) * NS], xnat[0:NS, 4, j * P:(j + 1) * P], ident[0:NS, 0:NS])
            out.then_inc(ev("xsT"), 1)
            pe.wait_ge(ev("p_in"), 16 * 15)
            for j in range(KB):
                out = nc.tensor.transpose(ps[:, 5, j * NROW:(j + 1) * NROW], prow[0:NROW, j * P:(j + 1) * P], ident[0:NROW, 0:NROW])
            out.then_inc(ev("pT"), 1)
            pe.wait_ge(ev("b_in"), 32)
            mm(ps[0:HEADS, 6, 0:TOEP], relb[0:NBUCKET + 1, :], onehot[:],
               start=True, stop=True).then_inc(ev("toep"), 1)

            pe.wait_ge(ev("setup_taken"), 2)
            operand("x0")
            product("qkv", xh, xl)

            pe.wait_ge(acc_free, PH["qkv"].m1 + 2)
            for G in range(2):
                for kv in range(2):
                    nc.tensor.transpose(ps[0:NS, 4, (kv * 2 + G) * P:(kv * 2 + G + 1) * P],
                                        qkvT[:, KB + 2 * kv + G, SEQ:T], ident)
            for G in range(2):
                out = nc.tensor.transpose(ps[:, 5, G * P:(G + 1) * P], qkvT[:, KB + G, SEQ - WIN:SEQ], ident)
            for t in range(4):
                for G in range(2):
                    out = nc.tensor.transpose(ps[:, 6 + t // 2, (t % 2) * 256 + G * P:(t % 2) * 256 + (G + 1) * P],
                                              qkvT[:, KB + 2 + G, t * P:(t + 1) * P], ident)
            out.then_inc(ev("kv_tok"), 1)

            units = [(qb, g) for qb in range(SEQ // WIN) for g in range(KV)]
            U = len(units)
            pe.wait_ge(ev("tok_taken"), 1)
            for t in range(U + 2):
                if t < U:
                    qb, g = units[t]
                    W = WIN if qb == 0 else 2 * WIN
                    part, G = (top, low)[g % 2], g // 2
                    if t >= 2:
                        pe.wait_ge(ev("s_taken"), t - 1)
                    for i in range(GROUP):
                        out = mm(ps[:, 2 * (t % 2) + i // 2, (i % 2) * W:(i % 2 + 1) * W],
                                 qkvT[part, G * GROUP + i, qb * WIN:(qb + 1) * WIN],
                                 qkvT[part, KB + G, (qb + 1) * WIN - W:(qb + 1) * WIN], start=True, stop=True)
                    out.then_inc(ev("s_mm"), 1)
                if 1 <= t <= U:
                    u = t - 1
                    nkb = 1 if units[u][0] == 0 else 2
                    pe.wait_ge(ev("probs"), u + 1)
                    if u >= 1:
                        pe.wait_ge(ev("pt_taken"), u)
                    for kb in range(nkb):
                        for i in range(GROUP):
                            W = nkb * WIN
                            out = nc.tensor.transpose(ps[:, 4 + kb, i * P:(i + 1) * P],
                                                      S[:, u % 2, i * W + kb * P:i * W + (kb + 1) * P], ident)
                    out.then_inc(ev("pt_mm"), 1)
                if t >= 2:
                    u = t - 2
                    qb, g = units[u]
                    nkb = 1 if qb == 0 else 2
                    part, pair = (top, low)[g % 2], u // 2
                    pe.wait_ge(ev("pt_taken"), u + 1)
                    if g % 2 == 0 and pair >= 2:
                        pe.wait_ge(ev("o_taken"), pair - 1)
                    for kb in range(nkb):
                        out = mm(ps[part, 6 + pair % 2, :], vtok[:, qb - nkb + 1 + kb, g * HD:(g + 1) * HD],
                                 PT[:, u % 2, kb * 512:(kb + 1) * 512], start=(kb == 0), stop=(kb == nkb - 1))
                    out.then_inc(ev("o_mm"), 1)

            pe.wait_ge(ev("cache_in"), 32)
            pe.wait_ge(ev("s_taken"), U)
            for G in range(2):
                for b in range(DB):
                    out = nc.tensor.transpose(ps[:, 2 * G + b // 4, (b % 4) * P:(b % 4 + 1) * P], ck[:, b, G * P:(G + 1) * P], ident)
            out.then_inc(ev("ckT_mm"), 1)
            pe.wait_ge(ev("ckT"), 1)
            pe.wait_ge(ev("ckT_new"), 1)
            pe.wait_ge(ev("o_taken"), U // 2)
            for b in range(DB):
                for g in range(KV):
                    part, G = (top, low)[g % 2], g // 2
                    out = mm(ps[32 * g:32 * (g + 1), 4 + b // 3, (b % 3) * KEYS:(b % 3 + 1) * KEYS],
                             qs[part, G, b, :],
                             ckT[part, G, b, :], start=True, stop=True)
            out.then_inc(ev("ss_mm"), 1)
            pe.wait_ge(ev("s_probs"), 1)
            for b in range(DB):
                nc.tensor.transpose(ps[:, b // 4, (b % 4) * P:(b % 4 + 1) * P], S[:, 0, b * KEYS:b * KEYS + WIN], ident)
                out = nc.tensor.transpose(ps[0:DT, 2 + b // 4, (b % 4) * P:(b % 4 + 1) * P],
                                          S[:, 0, b * KEYS + WIN:(b + 1) * KEYS], ident)
            out.then_inc(ev("spt_mm"), 1)
            pe.wait_ge(ev("spt"), 1)
            pe.wait_ge(ev("vnb_in"), 16 * DB)
            o_s = ps[:, 7, :].rearrange("p (G i b t) -> p G i b t", G=2, i=GROUP, b=DB)
            for b in range(DB):
                for g in range(KV):
                    part, G = (top, low)[g % 2], g // 2
                    mm(o_s[part, G, :, b, :], cv[:, b, g * HD:(g + 1) * HD], PT[:, 0, b * P + 32 * g:b * P + 32 * (g + 1)],
                       start=True, stop=False)
                    out = mm(o_s[part, G, :, b, :], vnb[:, b, g * HD:(g + 1) * HD],
                             PT[0:DT, 1, b * P + 32 * g:b * P + 32 * (g + 1)], start=False, stop=True)
            out.then_inc(ev("so_mm"), 1)
            pe.wait_ge(ev("att_ready"), 1)
            product("wo", xh, xl)

            norm(0, PH["wo"])
            ffn(0)
            norm(1, PH["dn0"])

            def lora_in(step, products):
                for k in range(KB):
                    pe.wait_ge(ev("mf"), KB * step + k + 1)
                    for w, part, bank in products:
                        for b, t0 in halves:
                            out = mm(ps[part, bank + b, 0:TH], w(k), mf[:, k % 2, t0:t0 + TH], start=(k == 0), stop=(k == KB - 1))
                    out.then_inc(ev("mf_used"), 1)

            pe.wait_ge(ev("shc"), 1)
            for j in range(KB):
                out = nc.tensor.transpose(ps[0:9, 6 + j // 4, (j % 4) * P:(j % 4 + 1) * P], shc[:, j, :], ident)
            out.then_inc(ev("sh_mm"), 1)
            operand("r")
            product("r", xh, xl)
            pe.wait_ge(ev("lora_w_in"), 16 * 5)
            lora_in(0, [(lambda k: w1s[:, k, :], top, 4)])
            operand("k")
            product("k", xh, xl)
            pe.wait_ge(ev("lora_out"), 1)
            lora_in(1, [(lambda k: a1s[:, k, :], low, 4)])
            operand("v")
            product("v", xh, xl)
            pe.wait_ge(ev("lora_out"), 2)
            pe.wait_ge(ev("sh_taken"), 1)
            lora_in(2, [(lambda k: g1s[:, k, 0:P], slice(0, P), 4), (lambda k: g1s[:, k, P:L_GATE], slice(0, L_GATE - P), 6)])

            pe.wait_ge(ev("proj_taken"), 1)
            pe.wait_ge(acc_free, PH["v"].m1 + 2)
            for i_l, part in enumerate((top, low)):
                for j in range(KB):
                    q = i_l * KB + j
                    if q >= 2:
                        pe.wait_ge(ev("lora2_taken"), q - 1)
                    b = 2 * (j % 2)
                    mm(ps[:, b, :], wa2[part, j * P:(j + 1) * P], twa[part, 0:SEQ], start=True, stop=True)
                    mm(ps[:, b + 1, 0:NS], wa2[part, j * P:(j + 1) * P], twa[part, SEQ:T], start=True, stop=True).then_inc(ev("lora2_mm"), 1)
            for j in range(KB):
                pe.wait_ge(ev("kk_sq"), j + 1)
                if j >= 2:
                    pe.wait_ge(ev("kk_norm"), j - 1)
                for b, t0 in halves:
                    out = mm(ps[:, 4 + 2 * (j % 2) + b, 0:TH], const("bdones"), ef2[:, j % 2, t0:t0 + TH], start=True, stop=True)
                out.then_inc(ev("kk_sum"), 1)

            def chunk(c, sample):
                levels = 3 if sample else LEVELS
                pairs = [range(g * NP2, (g + 1) * NP2) for g in range(2)]
                pe.wait_ge(ev("c_pre"), c + 1)
                pe.wait_ge(ev("c_kv"), c + 2)
                pe.wait_ge(ev("sup"), 2 * c + 2)
                for g in range(2):
                    pe.wait_ge(ev(f"sbd{g}"), c + 1)
                for q, (src, name) in enumerate(((bbd, "gb"), (kbd, "gk"))):
                    for g in range(2):
                        for n_, p in enumerate(pairs[g]):
                            out = mm(ps[:, 2 * q + g, n_ * P:(n_ + 1) * P], src[:, p].rearrange("p h t -> p (h t)"),
                                     zr[:, p].rearrange("p z t -> p (z t)"), start=True, stop=True)
                        out.then_inc(ev(name), 1)
                if sample:
                    pe.wait_ge(ev("hats"), 1)
                for q, (src, name) in enumerate(((bbd, "tb"), (kbd, "tk"), (vbd, "tv"))):
                    for g in range(2):
                        if name == "tv":
                            pe.wait_ge(ev("gram_b"), 2 * c + (g + 1))
                        for n_, p in enumerate(pairs[g]):
                            out = nc.tensor.transpose(ps[:, (4, 6, 0)[q] + g, n_ * P:(n_ + 1) * P],
                                                      src[:, p].rearrange("p h t -> p (h t)"), ident)
                        out.then_inc(ev(name), 1)
                for level in range(levels):
                    for g in range(2):
                        pe.wait_ge(ev(f"lm{g}"), c * LEVELS + level + 1)
                        if level == 0:
                            pe.wait_ge(ev("tok_b"), 2 * c + g + 1)
                        else:
                            pe.wait_ge(ev(f"xup{g}"), c * LEVELS + level)
                            if level > 1:
                                pe.wait_ge(ev(f"yc{g}"), c * (LEVELS - 1) + level - 1)
                        for n_, p in enumerate(pairs[g]):
                            out = mm(ps[:, 4 + g, n_ * CH:(n_ + 1) * CH], lm[:, p, :],
                                     const("ident2") if level == 0 else xc[:, g, 0, n_, :], start=True, stop=True)
                        out.then_inc(ev(f"y{g}"), 1)
                    if level == 0:
                        continue
                    for g in range(2):
                        pe.wait_ge(ev(f"yc{g}"), c * (LEVELS - 1) + level)
                        pe.wait_ge(ev(f"ybd{g}"), c * (LEVELS - 1) + level)
                        pe.wait_ge(ev(f"xtb{g}"), c * LEVELS + level)
                        if level == 1:
                            pe.wait_ge(ev("tok_k"), 2 * c + g + 1)
                        for n_, p in enumerate(pairs[g]):
                            if level < levels - 1:
                                mm(ps[:, 6 + g, n_ * CH:(n_ + 1) * CH], xtb[:, p].rearrange("p h t -> p (h t)"),
                                   yc[:, p, :], start=True, stop=True)
                            out = mm(ps[:, 6 + g, 256 + n_ * CH:256 + (n_ + 1) * CH], ybd[:, p].rearrange("p h t -> p (h t)"),
                                     xc[:, g, 1, n_, :], start=True, stop=True)
                        out.then_inc(ev(f"xm{g}"), 1)
                for g in range(2):
                    pe.wait_ge(ev("gram_k"), 2 * c + (g + 1))
                    pe.wait_ge(ev("tok_v"), 2 * c + g + 1)
                    for n_, p in enumerate(pairs[g]):
                        o = ps[:, 2 + g, n_ * HD:(n_ + 1) * HD]
                        if sample:
                            mm(o, sbd[:, p].rearrange("p h t -> p (h t)"), const("ident2"), start=True, stop=False)
                        else:
                            mm(o, zbd[:, p].rearrange("p h t -> p (h t)"), S_c[:, p, :], start=True, stop=False)
                        out = mm(o, lzk[:, p].rearrange("p h t -> p (h t)"), vtc[:, p, :], start=False, stop=True)
                    out.then_inc(ev("u"), 1)
                for g in range(2):
                    pe.wait_ge(ev("uc"), 2 * c + (g + 1))
                    pe.wait_ge(ev(f"xtb{g}"), c * LEVELS + levels)
                    for n_, p in enumerate(pairs[g]):
                        out = mm(ps[:, g, n_ * HD:(n_ + 1) * HD], xtb[:, p].rearrange("p h t -> p (h t)"), uc[:, p, :],
                                 start=True, stop=True)
                    out.then_inc(ev("sa"), 1)
                for g in range(2):
                    pe.wait_ge(ev("sac"), 2 * c + (g + 1))
                    for n_, p in enumerate(pairs[g]):
                        o = ps[:, 4 + g, n_ * CH:(n_ + 1) * CH]
                        if not sample:
                            mm(o, sbd[:, p].rearrange("p h v -> p (h v)"), zr[:, p, 1, :], start=True, stop=False)
                        mm(o, sabd[:, p].rearrange("p h v -> p (h v)"), lrb[:, p, :], start=sample, stop=False)
                        out = mm(o, vtm[:, p, :], lrk[:, p, :], start=False, stop=True)
                    out.then_inc(ev("o"), 1)
                if sample:
                    return
                for g in range(2):
                    for n_, p in enumerate(pairs[g]):
                        o = ps[:, 6 + g, n_ * HD:(n_ + 1) * HD]
                        mm(o, btm[:, p, :], sac[:, p, :], start=True, stop=False)
                        out = mm(o, ktm[:, p, :], vtc[:, p, :], start=False, stop=True)
                    out.then_inc(ev("st"), 1)

            pe.wait_ge(ev("wkv_zero"), 1)
            with nc.tensor.Fori(0, NCH) as c:
                chunk(c, False)
            for g in range(2):
                pe.wait_ge(ev(f"sbd{g}"), NCH + 1)
            for p in range(NPAIR):
                out = mm(ps[:, 0, p * HD:(p + 1) * HD], sbd[:, p].rearrange("p h v -> p (h v)"), const("ident2"), start=True, stop=True)
            out.then_inc(ev("state_mm"), 1)
            pe.wait_ge(ev("c_pre"), NCH + 1)
            for h in range(4):
                pe.wait_ge(ev("n0_in"), 64 * (h + 1))
                if h >= 1:
                    pe.wait_ge(ev("s0_done"), h)
                else:
                    pe.wait_ge(ev("sup"), 2 * NCH + 2)
                for a in range(2):
                    for b in range(DB):
                        out = nc.tensor.transpose(ps[:, 4 + 2 * a + b // 4, (b % 4) * P:(b % 4 + 1) * P],
                                                  n0bd[:, a, b].rearrange("p h v -> p (h v)"), ident)
                out.then_inc(ev("s0_mm"), 1)
                pe.wait_ge(ev("s0bd"), h + 1)
                for a in range(2):
                    p = 2 * h + a
                    for b in range(DB):
                        out = mm(ps[:, 1, (a * DB + b) * 2 * DT:(a * DB + b + 1) * 2 * DT].rearrange("p (z t) -> p z t", z=2),
                                 s0bd[:, a, b, :], zr[:, p, :, b * DT:(b + 1) * DT], start=True, stop=True)
                out.then_inc(ev("zs_mm"), 1)
                pe.wait_ge(ev("dpc"), h + 1)
                for a in range(2):
                    for b in range(DB):
                        out = mm(ps[:, 2 + a, b * HD:(b + 1) * HD], s0bd[:, a, b, :], dpc[:, a, b, :], start=True, stop=True)
                out.then_inc(ev("sp_mm"), 1)
            pe.wait_ge(ev("s0_done"), 4)
            chunk(NCH, True)
            for p in range(NPAIR):
                pe.wait_ge(ev("bkm"), p + 1)
                if p >= 2:
                    pe.wait_ge(ev("sst"), p - 1)
                o = ps[:, 6 + p % 2, :].rearrange("p (b k) -> p b k", b=DB)
                mm(o, sabd[:, p].rearrange("p h v -> p (h v)"), bkm(p, 0), start=True, stop=False)
                mm(o, vtm[:, p, :], bkm(p, 1), start=False, stop=True).then_inc(ev("sst_mm"), 1)

            for j in range(KB):
                pe.wait_ge(ev("f_rk"), j + 1)
                for b, t0 in halves:
                    mm(ps[:, b, 0:TH], const("bdones"), fin[:, 0, t0:t0 + TH], start=True, stop=True)
                for b, t0 in halves:
                    out = mm(ps[:, 2 + b, 0:TH], const("bdones"), kk[:, j, t0:t0 + TH], start=True, stop=True)
                out.then_inc(ev("f_sums"), 1)
                if j == 0:
                    pe.wait_ge(ev("g2_in"), 32)
                for b, t0 in halves:
                    mm(ps[:, 6 + b, 0:TH], g2a[:, j * P:(j + 1) * P], sg[:, 0, t0:t0 + TH], start=True, stop=False)
                    out = mm(ps[:, 6 + b, 0:TH], g2b[:, j * P:(j + 1) * P], sg[0:L_GATE - P, 1, t0:t0 + TH], start=False, stop=True)
                out.then_inc(ev("f_gate"), 1)
                pe.wait_ge(ev("f_sq"), j + 1)
                for b, t0 in halves:
                    out = mm(ps[:, 4 + b, 0:TH], const("bdones"), fin[:, 2, t0:t0 + TH], start=True, stop=True)
                out.then_inc(ev("f_var"), 1)
                pe.wait_ge(op_ready, KB * OP["z"] + j + 1)

            operand("z")
            product("ro", xh, xl)
            norm(2, PH["ro"])
            ffn(1)
            norm(3, PH["dn1"])
            for t in range(5):
                n_ = P if t < 4 else NS
                if t == 0:
                    pe.wait_ge(ev("ln_x"), 4 * KB)
                if t >= 2:
                    pe.wait_ge(ev("y_taken"), t - 1)
                for j in range(KB):
                    out = nc.tensor.transpose(ps[0:n_, 2 * (t % 2) + j // 4, (j % 4) * P:(j % 4 + 1) * P],
                                              x[:, j, t * P:t * P + n_], ident)
                out.then_inc(ev("y_mm"), 1)

        @block.scalar
        def _(act):
            A = nc.scalar.activation

            def split_high(ph, t, s):
                act.wait_ge(raw_in[s], ph.r0 + 16 * ph.dmas * (t // 2 + 1) if isinstance(t, int)
                            else (t - s) * (8 * ph.dmas) + (ph.r0 + 16 * ph.dmas))
                act.wait_ge(wslot_free, t + (ph.n0 + 1))
                nc.scalar.copy(wh[:, s, 0:ph.kb, :], raw[:, s, 0:ph.kb, :]).then_inc(hi_done, 1)

            def high_ahead(ph, t, s, last):
                if last:
                    if ph.name in ("v", "dn1"):
                        return
                    split_high(after(ph.name), s, s)
                else:
                    split_high(ph, t + 2, s)

            def product(name, take=None):
                ph = PH[name]
                rounds = ph.slabs // 2

                def body(i, last):
                    for s in range(2):
                        high_ahead(ph, 2 * i + s, s, last)
                        if take:
                            act.wait_ge(wslot_free, 2 * i + (ph.n0 + s + 3))
                            take(2 * i + s, s)
                with nc.scalar.Fori(0, rounds - 1) as i:
                    body(i, False)
                body(rounds - 1, True)

            def ffn(i_ffn):
                up = PH[f"gu{i_ffn}"]

                def body(i, last):
                    for q in range(2):
                        for s in range(2):
                            high_ahead(up, 4 * i + 2 * q + s, s, last and q == 1)
                            if s == 0:
                                act.wait_ge(wslot_free, 4 * i + (up.n0 + 2 * q + 3))
                                act.wait_ge(up_free, 2 * i + (up.g0 + q + 1))
                                A(gbuf[:, q, :].rearrange("p (h n) -> p h n", h=2), acc(2 * q), ACT.Silu).then_inc(gate_free, 1)
                        act.wait_ge(up_free, 2 * i + (up.g0 + q + 3))
                        A(hh[:, bass.ds(2 * i + q, 1), :], hbuf[:, q:q + 1, :], ACT.Copy).then_inc(hid_hi, 1)
                with nc.scalar.Fori(0, FB // 2 - 1) as i:
                    body(i, False)
                body(FB // 2 - 1, True)
                product(f"dn{i_ffn}")

            def scale_x(i, bias=None):
                if bias is None:
                    nc.scalar.mul(x[:], x[:], ALPHA).then_inc(ev("x_scaled"), 1)
                else:
                    for j in range(KB):
                        out = A(x[:, j, :], x[:, j, :], ACT.Identity, bias=col(bias, j), scale=ALPHA)
                    out.then_inc(ev("x_scaled"), 1)

            def norm(i_ln, ph, gain, shift_row):
                act.wait_ge(acc_free, ph.m1 + 2)
                for j in range(KB):
                    if i_ln or j >= 2:
                        act.wait_ge(ev("ln_sum"), KB * i_ln + j - 1 if j >= 2 else KB * i_ln)
                    A(lnw[:, 3 + j % 2, :], x[:, j, :], ACT.Square).then_inc(ev("ln_sq"), 1)
                act.wait_ge(ev("ln_var"), i_ln + 1)
                A(lnw[:, 1, :], lnw[:, 1, :], ACT.Sqrt, bias=const("eps")[:, 0:1]).then_inc(ev("ln_sd"), 1)
                for j in range(KB):
                    act.wait_ge(ev("ln_hat"), KB * i_ln + j + 1)
                    A(x[:, j, :], x[:, j, :], ACT.Identity, bias=col(shift_row, j), scale=col(gain, j)).then_inc(ev("ln_x"), 1)
                    if i_ln in (0, 2):
                        act.wait_ge(ev("ln_x"), KB * i_ln + j + 1)
                        A(xh[:, j, :], x[:, j, :], ACT.Copy).then_inc(op_hi, 1)

            for j in range(KB):
                act.wait_ge(ev("xT"), j + 1)
                A(x[:, j, 0:SEQ], ps[:, j % 4, :], ACT.Copy).then_inc(ev("xT_taken"), 1)
            act.wait_ge(ev("xsT"), 1)
            A(x[:, :, SEQ:T], ps[:, 4, :].rearrange("p (k n) -> p k n", k=KB), ACT.Copy).then_inc(ev("xT_taken"), 1)
            act.wait_ge(ev("xT_taken"), KB + 1)
            for s in range(2):
                split_high(PH["qkv"], s, s)
            for j in range(KB):
                A(xh[:, j, :], x[:, j, :], ACT.Copy).then_inc(op_hi, 1)
            act.wait_ge(ev("toep_taken"), 1)
            act.dma_start(scratch["table"], toep_sb[:]).then_inc(ev("table_out"), 16)
            act.wait_ge(ev("table_out"), 16)
            act.dma_start(scratch["spread"], bass.AP(tensor=scratch["table"].tensor, offset=0,
                                                     ap=[[TOEP, HEADS], [0, P], [1, TOEP]])).then_inc(ev("table_out"), 16)
            act.wait_ge(ev("table_out"), 32)
            act.wait_ge(ev("setup_taken"), 2)
            skew = scratch["spread"].tensor
            act.dma_start(biasT[:], bass.AP(tensor=skew, offset=WIN - 1, ap=[[TOEP - 1, P], [P * TOEP, HEADS], [1, 2 * WIN]])
                          ).then_inc(ev("bias_in"), 16)
            act.dma_start(bias_s[:], bass.AP(tensor=skew, offset=WIN - 1, ap=[[P * TOEP, HEADS], [TOEP - 1, DT], [1, KEYS]])
                          ).then_inc(ev("bias_in"), 16)
            act.wait_ge(op_ready, KB)
            scale_x(0, R_BO)
            for q, (new, old) in enumerate((("sk", "cache_win_k"), ("sv", "cache_win_v"))):
                act.dma_start(outs[new][0, :, 0:WIN - DT], ins[old][0, :, DT:WIN]).then_inc(stored, 16)
                outs_stored[0] += 1
            product("qkv")

            act.wait_ge(ev("kv_tok"), 1)
            A(kvnew[:], ps[0:NS, 4, :].rearrange("p (a n) -> p a n", a=2), ACT.Copy)
            A(ktok[:], ps[:, 5, 0:256], ACT.Copy)
            A(vtok[:, 0:2, :], ps[:, 6, :].rearrange("p (a n) -> p a n", a=2), ACT.Copy)
            A(vtok[:, 2:4, :], ps[:, 7, :].rearrange("p (a n) -> p a n", a=2), ACT.Copy).then_inc(ev("tok_taken"), 1)
            act.wait_ge(ev("tok_taken"), 1)
            act.dma_start(outs["pk"].rearrange("a b w h d -> w (a b) (h d)"), ktok[:].unsqueeze(1)).then_inc(ev("kv_kept"), 16)
            act.dma_start(outs["pv"].rearrange("a b w h d -> w (a b) (h d)"), vtok[:, 3:4, :]).then_inc(ev("kv_kept"), 16)
            for b in range(DB):
                act.dma_start(vnb[:, b, :], kvnew[b * DT:(b + 1) * DT, 1, :]).then_inc(ev("vnb_in"), 16)
                for q, name in enumerate(("sk", "sv")):
                    act.dma_start(outs[name][0, b, WIN - DT:WIN].rearrange("w h d -> w (h d)"), kvnew[b * DT:(b + 1) * DT, q, :]
                                  ).then_inc(ev("kv_kept"), 16)
            U = 4 * KV
            for t in range(U + 1):
                if t < U:
                    slot, W = t % 2, WIN if t < KV else 2 * WIN
                    act.wait_ge(ev("s_max"), t + 1)
                    for i in range(GROUP):
                        A(S[:, slot, i * W:(i + 1) * W], S[:, slot, i * W:(i + 1) * W], ACT.Exp,
                          bias=stat[:, slot, 0, i:i + 1], accum_out=stat[:, slot, 1, i:i + 1])
                    A(stat[:, slot, 3, 0:GROUP], stat[:, slot, 2, 0:GROUP], ACT.Exp).then_inc(ev("s_exp"), 1)
                if t >= 1:
                    u = t - 1
                    n_ = 1 if u < KV else 2
                    act.wait_ge(ev("pt_mm"), u + 1)
                    if u >= 2:
                        act.wait_ge(ev("o_mm"), u - 1)
                    A(PT[:, u % 2, 0:n_ * 512].rearrange("p (a n) -> p a n", a=n_), ps[:, 4:4 + n_, :], ACT.Copy).then_inc(ev("pt_taken"), 1)
            act.wait_ge(ev("ckT_mm"), 1)
            for G in range(2):
                for q in range(2):
                    out = A(ckT[:, G, 4 * q:4 * q + 4, 0:WIN], ps[:, 2 * G + q, :].rearrange("p (b n) -> p b n", b=4), ACT.Copy)
            out.then_inc(ev("ckT"), 1)
            act.wait_ge(ev("ss_max"), 1)
            for b in range(DB):
                A(S[:, 0, b * KEYS:(b + 1) * KEYS], S[:, 0, b * KEYS:(b + 1) * KEYS], ACT.Exp,
                  bias=stat[:, 0, 0, b:b + 1], accum_out=stat[:, 0, 1, b:b + 1])
            A(stat[:, 0, 3, :], stat[:, 0, 2, :], ACT.Exp).then_inc(ev("ss_exp"), 1)
            act.wait_ge(ev("spt_mm"), 1)
            act.wait_ge(ev("o_mm"), U)
            for q in range(2):
                A(PT[:, 0, q * 512:(q + 1) * 512], ps[:, q, :], ACT.Copy)
                out = A(PT[0:DT, 1, q * 512:(q + 1) * 512], ps[0:DT, 2 + q, :], ACT.Copy)
            out.then_inc(ev("spt"), 1)

            product("wo")
            norm(0, PH["wo"], R_LNG + 0, R_LNB + 0)
            act.wait_ge(op_ready, KB * 2)
            scale_x(1)
            act.wait_ge(ev("kv_kept"), KV_STORES)
            ffn(0)
            norm(1, PH["dn0"], R_LNG + 1, R_LNB + 1)

            act.wait_ge(ev("ln_x"), 2 * KB)
            act.dma_start(scratch["x"], x[:]).then_inc(ev("x_moved"), 16)
            act.dma_start(w1s, ins["rwkv_w1"].rearrange("a (k p) n -> p (a k) n", p=P)).then_inc(ev("lora_w_in"), 16)
            act.dma_start(a1s, ins["rwkv_a1"].rearrange("a (k p) n -> p (a k) n", p=P)).then_inc(ev("lora_w_in"), 16)
            act.dma_start(g1s, ins["rwkv_g1"].rearrange("a (k p) n -> p (a k) n", p=P)).then_inc(ev("lora_w_in"), 16)
            act.dma_start(wa2[top, :], ins["rwkv_w2"][0]).then_inc(ev("lora_w_in"), 16)
            act.dma_start(wa2[low, :], ins["rwkv_a2"][0]).then_inc(ev("lora_w_in"), 16)

            def mixed_high(step):
                for j in range(KB):
                    act.wait_ge(ev("mt"), KB * step + j + 1)
                    A(xh[:, j, :], mt[:, j % 2, :], ACT.Copy).then_inc(op_hi, 1)

            def take_into(dst):
                def take(blk, s):
                    A(two(dst[:, bass.ds(blk, 1), :]), acc(s), ACT.Copy).then_inc(acc_free, 1)
                return take

            mixed_high(0)
            act.wait_ge(ev("sh_mm"), 1)
            A(sho[:].rearrange("p (a n) -> p a n", a=2), ps[0:9, 6:8, :], ACT.Copy).then_inc(ev("sh_taken"), 1)
            act.wait_ge(ev("sh_taken"), 1)
            act.dma_start(outs["ps"].rearrange("a b d -> (a b) d"), sho[0:1, :]).then_inc(ev("shift_kept"), 16)
            act.dma_start(outs["ss"].rearrange("a b d -> (a b) d"), sho[1:9, :]).then_inc(ev("shift_kept"), 16)
            product("r", take_into(rr))
            mixed_high(1)
            act.wait_ge(ev("mf_used"), KB)
            A(twa[top].rearrange("p (h n) -> p h n", h=2), ps[top, 4:6, 0:TH], ACT.Tanh).then_inc(ev("lora_out"), 1)
            product("k", take_into(kx))
            mixed_high(2)
            act.wait_ge(ev("mf_used"), KB * 2)
            A(twa[low].rearrange("p (h n) -> p h n", h=2), ps[low, 4:6, 0:TH], ACT.Copy).then_inc(ev("lora_out"), 1)
            product("v", take_into(vv))
            act.wait_ge(ev("mf_used"), KB * 3)
            A(two(sg[:, 0:1, :]), ps[:, 4:6, 0:TH], ACT.Sigmoid)
            A(two(sg[0:L_GATE - P, 1:2, :]), ps[0:L_GATE - P, 6:8, 0:TH], ACT.Sigmoid).then_inc(ev("proj_taken"), 1)

            act.wait_ge(ev("cc_zero"), 1)
            for j in range(KB):
                act.wait_ge(ev("lora2_mm"), j + 1)
                b = 2 * (j % 2)
                A(cc[:, j, 0:PADP].rearrange("p (c n) -> p c n", n=CH + 1)[:, :, 1:], ps[:, b, :].rearrange("p (c n) -> p c n", n=CH),
                  ACT.Sigmoid, bias=col(R_W0, j))
                A(cc[:, j, PADP:].rearrange("p (c n) -> p c n", n=DT + 1)[:, :, 1:], ps[:, b + 1, 0:NS].rearrange("p (c n) -> p c n", n=DT),
                  ACT.Sigmoid, bias=col(R_W0, j)).then_inc(ev("lora2_taken"), 1)
            for j in range(KB):
                act.wait_ge(ev("lora2_mm"), KB + j + 1)
                b = 2 * (j % 2)
                A(bb[:, j, 0:SEQ], ps[:, b, :], ACT.Sigmoid, bias=col(R_A0, j))
                A(bb[:, j, SEQ:T], ps[:, b + 1, 0:NS], ACT.Sigmoid, bias=col(R_A0, j)).then_inc(ev("lora2_taken"), 1)
            act.wait_ge(ev("shift_kept"), 32)
            for t in range(KB + 1):
                if t < KB:
                    nc.scalar.mul(kk[:, t, :], kx[:, t, :], col(R_KK, t)).then_inc(ev("kk"), 1)
                    act.wait_ge(ev("kk"), t + 1)
                    if t >= 2:
                        act.wait_ge(ev("kk_sum"), t - 1)
                    A(ef2[:, t % 2, :], kk[:, t, :], ACT.Square).then_inc(ev("kk_sq"), 1)
                if t >= 1:
                    j = t - 1
                    act.wait_ge(ev("kk_sum"), j + 1)
                    if j >= 2:
                        act.wait_ge(ev("kk_norm"), j - 1)
                    A(nrm[j % 2].rearrange("p (h n) -> p h n", h=2), ps[:, 4 + 2 * (j % 2):6 + 2 * (j % 2), 0:TH], ACT.Sqrt
                      ).then_inc(ev("kk_root"), 1)

            def chunk_exp(c, sample):
                act.wait_ge(ev("c_kv"), c + 1)
                act.wait_ge(ev("sup"), 2 * c + 2)
                if sample:
                    v = cc[:, :, PADP:].rearrange("p k (b n) -> p k b n", n=DT + 1)
                    for j in range(KB):
                        o = ef[:, :, j, :].rearrange("p a (b t) -> p a b t", b=DB)
                        A(o[:, 0], v[:, j, :, 1:], ACT.Exp, scale=-KAPPA)
                        A(o[:, 1], v[:, j, :, 0:DT], ACT.Exp, scale=-KAPPA)
                        out = A(o[:, 2], v[:, j, :, 1:], ACT.Exp, scale=KAPPA)
                else:
                    A(ef[:, 0], cc[:, :, bass.ds(c * (CH + 1) + 1, CH)], ACT.Exp, scale=-KAPPA)
                    A(ef[:, 1], cc[:, :, bass.ds(c * (CH + 1), CH)], ACT.Exp, scale=-KAPPA)
                    out = A(ef[:, 2], cc[:, :, bass.ds(c * (CH + 1) + 1, CH)], ACT.Exp, scale=KAPPA)
                out.then_inc(ev("c_exp"), 1)

            def chunk(c, sample):
                levels = 3 if sample else LEVELS
                for dst, name, bank, taken in ((btm, "tb", 4, "tok_b"), (ktm, "tk", 6, "tok_k"), (vtm, "tv", 0, "tok_v")):
                    for g in range(2):
                        act.wait_ge(ev(name), 2 * c + (g + 1))
                        pr = slice(g * NP2, (g + 1) * NP2)
                        bk = ps[:, bank + g, :].rearrange("p (a n) -> p a n", a=NP2)
                        if name == "tv":
                            A(vtc[top, pr, :], bk[top, :, 0:HD], ACT.Copy)
                            A(vtc[low, pr, :], bk[low, :, HD:P], ACT.Copy)
                        A(dst[:, pr, :], bk, ACT.Copy).then_inc(ev(taken), 1)
                for level in range(levels):
                    if level >= 1:
                        for g in range(2):
                            act.wait_ge(ev(f"y{g}"), c * LEVELS + level + 1)
                            A(yc[:, g * NP2:(g + 1) * NP2, :], ps[:, 4 + g, 0:256].rearrange("p (a n) -> p a n", a=NP2),
                              ACT.Copy).then_inc(ev(f"yc{g}"), 1)
                    for g in range(2):
                        act.wait_ge(ev(f"xup{g}"), c * LEVELS + level + 1)
                        pr = slice(g * NP2, (g + 1) * NP2)
                        A(xtb[top, pr, 0, :], xc[top, g, 1], ACT.Copy)
                        A(xtb[low, pr, 1, :], xc[low, g, 1], ACT.Copy).then_inc(ev(f"xtb{g}"), 1)
                if sample:
                    return
                for g in range(2):
                    act.wait_ge(ev("sup"), 2 * c + (g + 3))
                    pr = slice(g * NP2, (g + 1) * NP2)
                    A(sbd[top, pr, 0, :], S_c[top, pr, :], ACT.Copy)
                    A(sbd[low, pr, 1, :], S_c[low, pr, :], ACT.Copy).then_inc(ev(f"sbd{g}"), 1)

            act.wait_ge(ev("prep"), KB)
            with nc.scalar.Fori(0, NCH) as c:
                chunk_exp(c, False)
                chunk(c, False)
            chunk_exp(NCH, True)
            act.wait_ge(ev("state_mm"), 1)
            A(stat_out[:], ps[:, 0, :].rearrange("p (a n) -> p a n", a=NPAIR), ACT.Copy).then_inc(ev("state_out"), 1)
            act.wait_ge(ev("state_out"), 1)
            for h, part in ((0, top), (1, low)):
                act.dma_start(outs["pw"].rearrange("a b (p h) v k -> h v (a b p) k", h=2)[h], stat_out[part]).then_inc(ev("state_kept"), 16)
            act.wait_ge(ev("n0_zero"), 1)
            for q in range(4):
                if q >= 1:
                    act.wait_ge(ev("s0_mm"), q)
                for a in range(2):
                    for h, part in ((0, top), (1, low)):
                        act.dma_start(n0bd[part, a, :, h, :],
                                      ins["state_wkv"][0, :, 2 * (2 * q + a) + h].rearrange("b v k -> v b k")).then_inc(ev("n0_in"), 16)
                act.wait_ge(ev("s0_mm"), q + 1)
                for a in range(2):
                    for b4 in range(2):
                        out = A(s0bd[:, a, 4 * b4:4 * b4 + 4, :], ps[:, 4 + 2 * a + b4, :].rearrange("p (b n) -> p b n", b=4), ACT.Copy)
                out.then_inc(ev("s0bd"), 1)
                act.wait_ge(ev("sp_mm"), q + 1)
                act.wait_ge(ev("zs_taken"), q + 1)
                A(spc[:, 2 * q:2 * q + 2], ps[:, 2:4, :].rearrange("p a (b n) -> p a b n", b=DB), ACT.Copy).then_inc(ev("s0_done"), 1)
            act.wait_ge(ev("wkv_zero"), 2)
            chunk(NCH, True)

            for p in range(NPAIR):
                act.wait_ge(ev("sst"), p + 1)
                for h, part in ((0, top), (1, low)):
                    act.dma_start(outs["sw"][0, :, 2 * p + h].rearrange("b v k -> v b k"), spc[part, p]).then_inc(ev("state_kept"), 16)
            act.wait_ge(ev("state_kept"), STATE_STORES)
            act.dma_start(g2a[:], ins["rwkv_g2"][0, 0:P]).then_inc(ev("g2_in"), 16)
            act.dma_start(g2b[:], ins["rwkv_g2"][0, P:L_GATE]).then_inc(ev("g2_in"), 16)
            for j in range(KB):
                act.wait_ge(ev("f_dev"), j + 1)
                A(fin[:, 2, :], fin[:, 1, :], ACT.Square).then_inc(ev("f_sq"), 1)
                act.wait_ge(ev("f_var"), j + 1)
                A(fin[:, 4, :].rearrange("p (h n) -> p h n", h=2), ps[:, 4:6, 0:TH], ACT.Sqrt, bias=const("eps")[:, 1:2],
                  scale=1.0 / HD).then_inc(ev("f_sd"), 1)
                act.wait_ge(ev("f_hat"), j + 1)
                A(fin[:, 3, :], fin[:, 3, :], ACT.Identity, bias=col(R_GB, j), scale=col(R_GW, j)).then_inc(ev("f_aff"), 1)
                act.wait_ge(ev("f_z"), j + 1)
                A(xh[:, j, :], fin[:, 3, :], ACT.Copy).then_inc(op_hi, 1)
            act.wait_ge(op_ready, KB * (OP["z"] + 1))
            act.dma_start(x[:], scratch["x"]).then_inc(ev("x_moved"), 16)
            act.wait_ge(ev("x_moved"), 32)
            scale_x(2)
            for s in range(2):
                split_high(PH["ro"], s, s)
            product("ro")
            norm(2, PH["ro"], R_LNG + 2, R_LNB + 2)
            act.wait_ge(op_ready, KB * (OP["f1"] + 1))
            scale_x(3)
            ffn(1)
            norm(3, PH["dn1"], R_LNG + 3, R_LNB + 3)
            for t in range(5):
                n_ = P if t < 4 else NS
                act.wait_ge(ev("y_mm"), t + 1)
                A(yout[0:n_, t, :].rearrange("p (a n) -> p a n", a=2), ps[0:n_, 2 * (t % 2):2 * (t % 2) + 2, :], ACT.Copy).then_inc(ev("y_taken"), 1)
                act.wait_ge(ev("y_taken"), t + 1)
                dst = outs["yp"][0, t * P:(t + 1) * P, :] if t < 4 else outs["ys"].rearrange("b t d -> (b t) d")
                act.dma_start(dst, yout[0:n_, t, :]).then_inc(stored, 16)
                outs_stored[0] += 1
            act.wait_ge(stored, 16 * outs_stored[0])

        @block.vector
        def _(dve):
            V = nc.vector
            dv = sem("dv")
            steps = [0]

            def link(ins_):
                steps[0] += 1
                ins_.then_inc(dv, 1)
                dve.wait_ge(dv, steps[0])

            def split_low(j):
                V.tensor_tensor(xl[:, j, :], x[:, j, :], xh[:, j, :].bitcast(F32), ALU.subtract).then_inc(op_ready, 1)

            def add_blocks(ph, i_x):
                per = 2 if ph.ffn_down else 1
                dve.wait_ge(ev("x_scaled"), i_x)
                with V.Fori(0, KB // 2) as i:
                    for a in range(2):
                        dve.wait_ge(wslot_free, i * (2 * per) + (ph.n0 + per * (a + 1) + 2))
                        blk = two(x[:, bass.ds(2 * i + a, 1), :])
                        V.tensor_tensor(blk, blk, acc(a), ALU.add).then_inc(acc_free, 1)

            def norm(i_ln):
                mean, var, tmp = lnw[:, 0, :], lnw[:, 1, :], lnw[:, 2, :]
                dve.wait_ge(ev("ln_mean"), i_ln + 1)
                link(V.tensor_copy(mean.rearrange("p (h n) -> p h n", h=2), ps[:, 4:6, 0:TH]))
                link(V.tensor_tensor(tmp, mean, mean, ALU.mult))
                dve.wait_ge(ev("ln_sum"), KB * (i_ln + 1))
                V.tensor_tensor(var.rearrange("p (h n) -> p h n", h=2), ps[:, 6:8, 0:TH],
                                tmp.rearrange("p (h n) -> p h n", h=2), ALU.subtract).then_inc(ev("ln_var"), 1)
                dve.wait_ge(ev("ln_sd"), i_ln + 1)
                link(V.reciprocal(tmp, var))
                for j in range(KB):
                    link(V.tensor_tensor(x[:, j, :], x[:, j, :], mean, ALU.subtract))
                    V.tensor_tensor(x[:, j, :], x[:, j, :], tmp, ALU.mult).then_inc(ev("ln_hat"), 1)
                    if i_ln in (0, 2) and j >= 1:
                        dve.wait_ge(op_hi, KB * OP["f0" if i_ln == 0 else "f1"] + j)
                        split_low(j - 1)
                if i_ln in (0, 2):
                    dve.wait_ge(op_hi, KB * (OP["f0" if i_ln == 0 else "f1"] + 1))
                    split_low(KB - 1)

            def take_state(p):
                dve.wait_ge(ev("sst_mm"), p + 1)
                V.tensor_tensor(spc[:, p], spc[:, p], ps[:, 6 + p % 2, :].rearrange("p (b k) -> p b k", b=DB), ALU.add
                                ).then_inc(ev("sst"), 1)

            def ffn(i_ffn):
                up = PH[f"gu{i_ffn}"]
                with V.Fori(0, FB // 2) as i:
                    for q in range(2):
                        dve.wait_ge(wslot_free, 4 * i + (up.n0 + 2 * q + 4))
                        dve.wait_ge(gate_free, 2 * i + (up.g0 + q + 3))
                        dve.wait_ge(hid_hi, 2 * i + (up.g0 + q + 1))
                        V.tensor_tensor(hbuf[:, q, :].rearrange("p (h n) -> p h n", h=2),
                                        gbuf[:, q, :].rearrange("p (h n) -> p h n", h=2), acc(2 * q + 1), ALU.mult
                                        ).then_inc(up_free, 1)
                        dve.wait_ge(up_free, 2 * i + (up.g0 + q + 3))
                        dve.wait_ge(hid_hi, 2 * i + (up.g0 + q + 3))
                        V.tensor_tensor(hl[:, bass.ds(2 * i + q, 1), :], hbuf[:, q:q + 1, :],
                                        hh[:, bass.ds(2 * i + q, 1), :].bitcast(F32), ALU.subtract).then_inc(hid_lo, 1)
                add_blocks(PH[f"dn{i_ffn}"], 2 * i_ffn + 2)

            dve.wait_ge(ev("pT"), 1)
            link(V.tensor_copy(prm[:], ps[:, 5, 0:KB * NROW].rearrange("p (k n) -> p k n", k=KB)))
            V.tensor_copy(bqkv[:, 0:KB], prm[:, :, R_BQ])
            V.tensor_copy(bqkv[:, KB:QB], prm[:, 0:4, R_BKV])
            V.tensor_scalar(omka[:], prm[:, :, R_KA], -1.0, 1.0, ALU.mult, ALU.add).then_inc(ev("setup_taken"), 1)
            dve.wait_ge(ev("toep"), 1)
            V.tensor_copy(toep_sb[:], ps[0:HEADS, 6, 0:TOEP]).then_inc(ev("toep_taken"), 1)
            dve.wait_ge(ev("s_in"), 32)
            V.tensor_scalar(sink[:], sink[:], -1.0, None, ALU.mult)
            V.tensor_scalar(sink_s[:], sink_s[:], -1.0, None, ALU.mult).then_inc(ev("setup_taken"), 1)
            dve.wait_ge(ev("xT_taken"), KB + 1)
            for j in range(KB):
                dve.wait_ge(op_hi, j + 1)
                split_low(j)
            dve.wait_ge(ev("table_out"), 16)
            dve.wait_ge(ev("setup_taken"), 2)
            with V.Fori(0, QB // 2) as i:
                for a in range(2):
                    dve.wait_ge(wslot_free, 2 * i + (a + 3))
                    V.tensor_scalar(two(qkvT[:, bass.ds(2 * i + a, 1), :]), acc(a), bqkv[:, bass.ds(2 * i + a, 1)], None,
                                    ALU.add).then_inc(acc_free, 1)

            dve.wait_ge(ev("bias_in"), 32)
            units = [(qb, g) for qb in range(SEQ // WIN) for g in range(KV)]
            U = len(units)
            for t in range(U + 3):
                if t < U:
                    qb, g = units[t]
                    slot, W = t % 2, WIN if qb == 0 else 2 * WIN
                    dve.wait_ge(ev("s_mm"), t + 1)
                    if t >= 2:
                        dve.wait_ge(ev("pt_mm"), t - 1)
                    sc = S[:, slot, 0:GROUP * W].rearrange("p (i w) -> p i w", w=W)
                    banks = ps[:, 2 * slot:2 * slot + 2, 0:2 * W].rearrange("p a (i w) -> p a i w", w=W)
                    for a in range(2):
                        out = V.scalar_tensor_tensor(sc[:, 2 * a:2 * a + 2, :], banks[:, a], HD ** -0.5,
                                                     biasT[:, g * GROUP + 2 * a:g * GROUP + 2 * a + 2, 2 * WIN - W:2 * WIN],
                                                     ALU.mult, ALU.add)
                    out.then_inc(ev("s_taken"), 1)
                    dve.wait_ge(ev("s_taken"), t + 1)
                    st = stat[:, slot]
                    link(V.tensor_reduce(st[:, 4, 0:GROUP], sc, AX_X, ALU.max))
                    link(V.scalar_tensor_tensor(st[:, 0, 0:GROUP], st[:, 4, 0:GROUP], -1.0, sink[:, g * GROUP:(g + 1) * GROUP],
                                                ALU.mult, ALU.min))
                    V.tensor_tensor(st[:, 2, 0:GROUP], st[:, 0, 0:GROUP], sink[:, g * GROUP:(g + 1) * GROUP],
                                    ALU.subtract).then_inc(ev("s_max"), 1)
                if 1 <= t <= U:
                    u = t - 1
                    slot, W = u % 2, WIN if units[u][0] == 0 else 2 * WIN
                    sc = S[:, slot, 0:GROUP * W].rearrange("p (i w) -> p i w", w=W)
                    st = stat[:, slot]
                    dve.wait_ge(ev("s_exp"), u + 1)
                    link(V.tensor_tensor(st[:, 4, 0:GROUP], st[:, 1, 0:GROUP], st[:, 3, 0:GROUP], ALU.add))
                    link(V.reciprocal(st[:, 4, 0:GROUP], st[:, 4, 0:GROUP]))
                    V.tensor_tensor(sc, sc, st[:, 4, 0:GROUP].unsqueeze(2).to_broadcast([P, GROUP, W]), ALU.mult
                                    ).then_inc(ev("probs"), 1)
                if t >= 4 and t % 2 == 0:
                    pair = (t - 4) // 2
                    qb, G = pair // 2, pair % 2
                    blk, tok = slice(G * GROUP, (G + 1) * GROUP), slice(qb * WIN, (qb + 1) * WIN)
                    bank = ps[:, 6 + pair % 2, :].rearrange("p (i q) -> p i q", i=GROUP)
                    dve.wait_ge(ev("o_mm"), 2 * pair + 2)
                    link(V.tensor_copy(xh[:, blk, tok], bank))
                    V.tensor_tensor(xl[:, blk, tok], bank, xh[:, blk, tok].bitcast(F32), ALU.subtract).then_inc(ev("o_taken"), 1)
            for G in range(2):
                V.tensor_copy(qs[:, G].rearrange("p b (i t) -> p i b t", i=GROUP),
                              qkvT[:, G * GROUP:(G + 1) * GROUP, SEQ:T].rearrange("p i (b t) -> p i b t", b=DB))
                out = V.tensor_copy(ckT[:, G, :, WIN:KEYS], qkvT[:, KB + G, SEQ:T].rearrange("p (b t) -> p b t", b=DB))
            out.then_inc(ev("ckT_new"), 1)
            dve.wait_ge(ev("ss_mm"), 1)
            st = stat[:, 0]
            sc = S[:, 0, :].rearrange("p (b w) -> p b w", b=DB)
            for q in range(3):
                n_ = 3 if q < 2 else 2
                out = V.scalar_tensor_tensor(sc[:, 3 * q:3 * q + n_, :],
                                             ps[:, 4 + q, 0:n_ * KEYS].rearrange("p (b w) -> p b w", w=KEYS), HD ** -0.5,
                                             bias_s[:].unsqueeze(1).to_broadcast([P, n_, KEYS]), ALU.mult, ALU.add)
            link(out)
            link(V.tensor_reduce(st[:, 4, :], sc, AX_X, ALU.max))
            link(V.tensor_scalar(st[:, 0, :], st[:, 4, :], -1.0, sink_s[:], ALU.mult, ALU.min))
            V.tensor_scalar(st[:, 2, :], st[:, 0, :], sink_s[:], None, ALU.subtract).then_inc(ev("ss_max"), 1)
            dve.wait_ge(ev("ss_exp"), 1)
            link(V.tensor_tensor(st[:, 4, :], st[:, 1, :], st[:, 3, :], ALU.add))
            link(V.reciprocal(st[:, 4, :], st[:, 4, :]))
            V.tensor_tensor(sc, sc, st[:, 4, :].unsqueeze(2).to_broadcast([P, DB, KEYS]), ALU.mult).then_inc(ev("s_probs"), 1)
            dve.wait_ge(ev("so_mm"), 1)
            bank = ps[:, 7, :].rearrange("p (k n) -> p k n", k=KB)
            link(V.tensor_copy(xh[:, :, SEQ:T], bank))
            V.tensor_tensor(xl[:, :, SEQ:T], bank, xh[:, :, SEQ:T].bitcast(F32), ALU.subtract).then_inc(ev("att_ready"), 1)

            add_blocks(PH["wo"], 1)
            norm(0)
            dve.wait_ge(ev("kv_kept"), KV_STORES)
            ffn(0)
            norm(1)

            dve.wait_ge(ev("ln_x"), 2 * KB)
            V.tensor_copy(shc[:, :, 0:1], x[:, :, SEQ - 1:SEQ])
            V.tensor_copy(shc[:, :, 1:9], x[:, :, SEQ:T].rearrange("p k (b t) -> p k b t", t=DT)[:, :, :, DT - 1]
                          ).then_inc(ev("shc"), 1)
            V.tensor_tensor(xx[:, :, 1:T], x[:, :, 0:T - 1], x[:, :, 1:T], ALU.subtract)
            link(V.tensor_scalar(xx[:, :, 0:1], x[:, :, 0:1], -1.0, None, ALU.mult))
            for j in range(KB):
                out = V.tensor_tensor(xx[:, j, SEQ:T].rearrange("p (b t) -> p b t", t=DT)[:, :, 0],
                                      prm[:, j, R_SHIFT:R_SHIFT + DB],
                                      x[:, j, SEQ:T].rearrange("p (b t) -> p b t", t=DT)[:, :, 0], ALU.subtract)
            link(out)

            def mix_operand(step, c):
                if step:
                    dve.wait_ge(wslot_free, PH[("", "r", "k")[step]].n1 + 2)
                for j in range(KB + 1):
                    if j < KB:
                        V.scalar_tensor_tensor(mt[:, j % 2, :], xx[:, j, :], col(R_MIX + c, j), x[:, j, :], ALU.mult, ALU.add
                                               ).then_inc(ev("mt"), 1)
                    if j >= 1:
                        dve.wait_ge(op_hi, KB * (2 + step) + j)
                        dve.wait_ge(ev("mt"), KB * step + j)
                        V.tensor_tensor(xl[:, j - 1, :], mt[:, (j - 1) % 2, :], xh[:, j - 1, :].bitcast(F32), ALU.subtract
                                        ).then_inc(op_ready, 1)
                        dve.wait_ge(op_ready, KB * (2 + step) + j)

            def mix_plain(step, c):
                for j in range(KB):
                    if step or j >= 2:
                        dve.wait_ge(ev("mf_used"), KB * step + j - 1)
                    V.scalar_tensor_tensor(mf[:, j % 2, :], xx[:, j, :], col(R_MIX + c, j), x[:, j, :], ALU.mult, ALU.add
                                           ).then_inc(ev("mf"), 1)

            mix_operand(0, 0)
            mix_plain(0, 1)
            mix_operand(1, 2)
            mix_plain(1, 4)
            mix_operand(2, 3)
            mix_plain(2, 5)

            dve.wait_ge(ev("proj_taken"), 1)
            dve.wait_ge(acc_free, PH["v"].m1 + 2)
            dve.wait_ge(ev("x_moved"), 16)
            V.memset(cc[:], 0.0).then_inc(ev("cc_zero"), 1)
            dve.wait_ge(ev("lora2_taken"), KB)
            for j in range(KB):
                V.tensor_tensor_scan(cc[:, j, :], const("reset"), cc[:, j, :], 0.0, ALU.mult, ALU.add)
            for j in range(KB):
                nr = nrm[j % 2]
                dve.wait_ge(ev("kk_root"), j + 1)
                link(V.tensor_scalar(nr, nr, 1e-12, None, ALU.max))
                link(V.reciprocal(nr, nr))
                V.tensor_tensor(kk[:, j, :], kk[:, j, :], nr, ALU.mult).then_inc(ev("kk_norm"), 1)
            dve.wait_ge(ev("lora2_taken"), 2 * KB)
            dve.wait_ge(ev("kk_norm"), KB)
            for j in range(KB):
                nr = nrm[j % 2]
                link(V.tensor_scalar(nr, bb[:, j, :], col(R_KA, j), omka[:, j:j + 1], ALU.mult, ALU.add))
                V.tensor_tensor(kx[:, j, :], kx[:, j, :], nr, ALU.mult)
                V.tensor_tensor(bb[:, j, :], kk[:, j, :], bb[:, j, :], ALU.mult).then_inc(ev("prep"), 1)

            CHAIN = [sem("zr_done"), sem("bd_done")]

            def chunk_pre(c, sample):
                tok = bass.ds(c * CH, CH)
                dve.wait_ge(ev("c_exp"), c + 1)
                V.tensor_tensor(zr[:, :, 1, :], rr[:, :, tok], ef[:, 0], ALU.mult)
                V.scalar_tensor_tensor(zr[:, :, 0, :], kk[:, :, tok], -1.0, ef[:, 1], ALU.mult, ALU.mult
                                       ).then_inc(CHAIN[0], 1)
                if sample:
                    V.tensor_copy(pc[:], ef[:, 0].rearrange("p k (b t) -> p k b t", t=DT)[:, :, :, DT - 1])
                else:
                    V.tensor_copy(pc[:, :, 0:1], ef[:, 0, :, CH - 1:CH])
                for h, part in ((0, top), (1, low)):
                    V.tensor_tensor(bbd[part, :, h, :], bb[part, :, tok], ef[part, 2], ALU.mult)
                dve.wait_ge(CHAIN[0], c + 1)
                V.tensor_copy(zbd[top, :, 0, :], zr[top, :, 0, :])
                V.tensor_copy(zbd[low, :, 1, :], zr[low, :, 0, :]).then_inc(ev("c_pre"), 1)

            def chunk(c, sample):
                levels = 3 if sample else LEVELS
                kind = "s" if sample else "p"
                strict, incl = const("strict_" + kind), const("incl_" + kind)
                for src, full, comp, name in ((0, lzb, lrb, "b"), (2, lzk, lrk, "k")):
                    for g in range(2):
                        dve.wait_ge(ev("g" + name), 2 * c + (g + 1))
                        pr = slice(g * NP2, (g + 1) * NP2)
                        gram = ps[:, src + g, :].rearrange("p (a z t) -> p a z t", a=NP2, z=2)
                        V.tensor_tensor(comp[:, pr, :], gram[:, :, 1, :], incl.unsqueeze(1).to_broadcast([P, NP2, CH]), ALU.mult)
                        if name == "b":
                            V.tensor_tensor(xc[:, g, 1], gram[:, :, 0, :],
                                            const("level0").unsqueeze(1).to_broadcast([P, NP2, CH]), ALU.mult
                                            ).then_inc(ev("x0"), 1)
                        for h in range(2):
                            out = V.tensor_tensor(full[:, pr, h, :], gram[:, :, 0, :],
                                                  strict[:, h * CH:(h + 1) * CH].unsqueeze(1).to_broadcast([P, NP2, CH]), ALU.mult)
                        out.then_inc(ev("gram_" + name), 1)
                if sample:
                    for t in (bbd, kbd):
                        for p in range(NPAIR):
                            out = V.tensor_tensor(t[:, p].rearrange("p h (b t) -> p h b t", t=DT),
                                                  t[:, p].rearrange("p h (b t) -> p h b t", t=DT),
                                                  pc[:, p, :].unsqueeze(1).unsqueeze(3).to_broadcast([P, 2, DB, DT]), ALU.mult)
                    out.then_inc(ev("hats"), 1)
                eye = const("ident2").unsqueeze(1).to_broadcast([P, NP2, CH])
                for g in range(2):
                    dve.wait_ge(ev("x0"), 2 * c + (g + 1))
                    V.tensor_tensor(xc[:, g, 1], xc[:, g, 1], eye, ALU.add)
                    dve.wait_ge(ev(f"y{g}"), c * LEVELS + 1)
                    V.tensor_tensor(xc[:, g, 0], ps[:, 4 + g, 0:256].rearrange("p (a t) -> p a t", a=NP2), eye, ALU.add
                                    ).then_inc(ev(f"xup{g}"), 1)
                for level in range(1, levels):
                    for g in range(2):
                        pr = slice(g * NP2, (g + 1) * NP2)
                        dve.wait_ge(ev(f"yc{g}"), c * (LEVELS - 1) + level)
                        V.tensor_copy(ybd[top, pr, 0, :], yc[top, pr, :])
                        V.tensor_copy(ybd[low, pr, 1, :], yc[low, pr, :]).then_inc(ev(f"ybd{g}"), 1)
                    for g in range(2):
                        half = 1 if level == levels - 1 else 0
                        dve.wait_ge(ev(f"xm{g}"), c * (LEVELS - 1) + level)
                        cur = xc[:, g, half:].rearrange("p x a t -> p (x a) t")
                        V.tensor_tensor(cur, cur, ps[:, 6 + g, half * 256:].rearrange("p (a t) -> p a t", t=CH), ALU.add
                                        ).then_inc(ev(f"xup{g}"), 1)
                for g in range(2):
                    pr = slice(g * NP2, (g + 1) * NP2)
                    dve.wait_ge(ev("u"), 2 * c + (g + 1))
                    V.tensor_copy(uc[:, pr, :], ps[:, 2 + g, 0:256].rearrange("p (a t) -> p a t", a=NP2)).then_inc(ev("uc"), 1)
                for g in range(2):
                    pr = slice(g * NP2, (g + 1) * NP2)
                    dve.wait_ge(ev("sa"), 2 * c + (g + 1))
                    bank = ps[:, g, 0:256].rearrange("p (a t) -> p a t", a=NP2)
                    V.tensor_copy(sac[:, pr, :], bank)
                    V.tensor_copy(sabd[top, pr, 0, :], bank[top])
                    V.tensor_copy(sabd[low, pr, 1, :], bank[low]).then_inc(ev("sac"), 1)
                for g in range(2):
                    pr = slice(g * NP2, (g + 1) * NP2)
                    dve.wait_ge(ev("o"), 2 * c + (g + 1))
                    bank = ps[:, 4 + g, 0:256].rearrange("p (a t) -> p a t", a=NP2)
                    if sample:
                        V.tensor_tensor(kk[:, pr, bass.ds(c * CH, CH)], bank, ef[:, 0, pr, :], ALU.add)
                    else:
                        V.tensor_scalar(kk[:, pr, bass.ds(c * CH, CH)], bank, 1.0, None, ALU.mult)
                if sample:
                    return
                for g in range(2):
                    pr = slice(g * NP2, (g + 1) * NP2)
                    dve.wait_ge(ev("st"), 2 * c + (g + 1))
                    V.tensor_tensor(S_c[:, pr, :], S_c[:, pr, :], ps[:, 6 + g, 0:256].rearrange("p (a t) -> p a t", a=NP2), ALU.add
                                    ).then_inc(ev("sadd"), 1)
                for g in range(2):
                    pr = slice(g * NP2, (g + 1) * NP2)
                    dve.wait_ge(ev("sadd"), 2 * c + (g + 1))
                    V.tensor_tensor(S_c[:, pr, :], S_c[:, pr, :], pc[:, pr, 0:1].to_broadcast([P, NP2, HD]), ALU.mult
                                    ).then_inc(ev("sup"), 1)

            dve.wait_ge(ev("wkv_zero"), 1)
            with V.Fori(0, NCH) as c:
                chunk_pre(c, False)
                chunk(c, False)
            chunk_pre(NCH, True)
            dve.wait_ge(ev("n0_zero"), 1)
            for q in range(4):
                if q == 0:
                    dve.wait_ge(CHAIN[0], NCH + 1)
                    dve.wait_ge(ev("c_pre"), NCH + 1)
                else:
                    dve.wait_ge(ev("sp_mm"), q)
                for a in range(2):
                    out = V.tensor_tensor(dpc[:, a], const("ident2").unsqueeze(1).to_broadcast([P, DB, HD]),
                                          pc[:, 2 * q + a, :].unsqueeze(2).to_broadcast([P, DB, HD]), ALU.mult)
                out.then_inc(ev("dpc"), 1)
                dve.wait_ge(ev("zs_mm"), q + 1)
                for a in range(2):
                    p = 2 * q + a
                    bank = ps[:, 1, a * P:(a + 1) * P].rearrange("p (b z t) -> p b z t", b=DB, z=2)
                    V.tensor_copy(sbd[top, p, 0, :].rearrange("p (b t) -> p b t", b=DB), bank[top, :, 0, :])
                    V.tensor_copy(sbd[low, p, 1, :].rearrange("p (b t) -> p b t", b=DB), bank[low, :, 0, :])
                    out = V.tensor_copy(ef[:, 0, p, :].rearrange("p (b t) -> p b t", b=DB), bank[:, :, 1, :])
                out.then_inc(ev("zs_taken"), 1)
            chunk(NCH, True)
            for p in range(NPAIR):
                if p >= 2:
                    dve.wait_ge(ev("sst_mm"), p - 1)
                for which, src in ((0, btm), (1, ktm)):
                    for h, part in ((0, top), (1, low)):
                        out = V.tensor_tensor(bkm(p, which)[part], src[part, p, h * HD:(h + 1) * HD].unsqueeze(1).to_broadcast([HD, DB, HD]),
                                              const("seqmask")[part].unsqueeze(2).to_broadcast([HD, DB, HD]), ALU.mult)
                out.then_inc(ev("bkm"), 1)
                if p >= 1:
                    take_state(p - 1)
            take_state(NPAIR - 1)
            dve.wait_ge(ev("state_kept"), STATE_STORES)

            for j in range(KB):
                V.scalar_tensor_tensor(fin[:, 0, :], rr[:, j, :], col(R_RK, j), kx[:, j, :], ALU.mult, ALU.mult
                                       ).then_inc(ev("f_rk"), 1)
                dve.wait_ge(ev("f_sums"), j + 1)
                h2 = lambda k: fin[:, k, :].rearrange("p (h n) -> p h n", h=2)
                V.scalar_tensor_tensor(h2(1), ps[:, 2:4, 0:TH], -1.0 / HD, kk[:, j, :].rearrange("p (h n) -> p h n", h=2),
                                       ALU.mult, ALU.add).then_inc(ev("f_dev"), 1)
                V.tensor_tensor(h2(5), ps[:, 0:2, 0:TH], vv[:, j, :].rearrange("p (h n) -> p h n", h=2), ALU.mult)
                dve.wait_ge(ev("f_sd"), j + 1)
                link(V.reciprocal(fin[:, 4, :], fin[:, 4, :]))
                V.tensor_tensor(fin[:, 3, :], fin[:, 1, :], fin[:, 4, :], ALU.mult).then_inc(ev("f_hat"), 1)
                dve.wait_ge(ev("f_aff"), j + 1)
                link(V.tensor_tensor(fin[:, 3, :], fin[:, 3, :], fin[:, 5, :], ALU.add))
                dve.wait_ge(ev("f_gate"), j + 1)
                V.tensor_tensor(h2(3), ps[:, 6:8, 0:TH], h2(3), ALU.mult).then_inc(ev("f_z"), 1)
                dve.wait_ge(op_hi, KB * OP["z"] + j + 1)
                dve.wait_ge(ev("f_z"), j + 1)
                V.tensor_tensor(xl[:, j, :], fin[:, 3, :], xh[:, j, :].bitcast(F32), ALU.subtract).then_inc(op_ready, 1)
                dve.wait_ge(op_ready, KB * OP["z"] + j + 1)

            add_blocks(PH["ro"], 3)
            norm(2)
            ffn(1)
            norm(3)


OUTPUTS = [("yp", (1, SEQ, D)), ("ys", (DB, DT, D)), ("pk", (1, 1, WIN, KV, HD)), ("pv", (1, 1, WIN, KV, HD)),
           ("ps", (1, 1, D)), ("pw", (1, 1, HEADS, HD, HD)), ("sk", (1, DB, WIN, KV, HD)), ("sv", (1, DB, WIN, KV, HD)),
           ("ss", (1, DB, D)), ("sw", (1, DB, HEADS, HD, HD))]
INPUTS = ["x_prompt", "x_sample", "cache_win_k", "cache_win_v", "state_shift", "state_wkv", "rel_bias", "ln_g", "ln_b",
          "attn_w_qkv", "attn_b_qkv", "attn_w_o", "attn_b_o", "attn_sinks", "rwkv_mix", "rwkv_w_rkv", "rwkv_w0",
          "rwkv_w1", "rwkv_w2", "rwkv_a0", "rwkv_a1", "rwkv_a2", "rwkv_g1", "rwkv_g2", "rwkv_k_k", "rwkv_k_a",
          "rwkv_r_k", "rwkv_ln_w", "rwkv_ln_b", "rwkv_w_o", "ffn_w_gu", "ffn_w_down"]


def kernel(**inputs):
    import concourse.bacc as bacc
    from concourse.bass_utils import run_bass_kernel_spmd

    nc = bacc.Bacc("TRN2", target_bir_lowering=False, num_devices=1)
    arrays, ins = {}, {}
    for name in INPUTS:
        arrays["in_" + name] = np.ascontiguousarray(inputs[name])
        ins[name] = nc.dram_tensor("in_" + name, inputs[name].shape, F32, kind="ExternalInput").ap()
    arrays["in_constants"] = constants()
    ins["constants"] = nc.dram_tensor("in_constants", arrays["in_constants"].shape, F32, kind="ExternalInput").ap()
    arrays["in_onehot"] = bucket_table()
    ins["onehot"] = nc.dram_tensor("in_onehot", arrays["in_onehot"].shape, F32, kind="ExternalInput").ap()
    outs = {name: nc.dram_tensor("out_" + name, shape, F32, kind="ExternalOutput").ap() for name, shape in OUTPUTS}
    scratch = {"table": nc.dram_tensor("table", (HEADS, TOEP), F32, kind="Internal").ap(),
               "spread": nc.dram_tensor("spread", (HEADS, P, TOEP), F32, kind="Internal").ap(),
               "x": nc.dram_tensor("x_kept", (P, KB, T), F32, kind="Internal").ap()}
    build_program(nc, ins, outs, scratch)
    r = run_bass_kernel_spmd(nc, [arrays], core_ids=[0])
    return tuple(r.results[0]["out_" + name] for name, _ in OUTPUTS)
```

```python
from contextlib import ExitStack

import numpy as np

import concourse.bass as bass
from concourse import mybir
from concourse.alu_op_type import AluOpType as ALU

F32 = mybir.dt.float32
F32R = mybir.dt.float32r
ACT = mybir.ActivationFunctionType
AX_X = mybir.AxisListType.X

P = 128
D = 1024
KB = D // P
SEQ = 512
DB, DT = 8, 8
NS = DB * DT
T = SEQ + NS
TH = T // 2
HEADS = 16
KV = 4
GROUP = HEADS // KV
HD = 64
WIN = 128
NBUCKET = 32
FF = 2816
FB = FF // P
QKV = (HEADS + 2 * KV) * HD
QB = QKV // P
KEYS = WIN + DT
CH = 64
NCH = SEQ // CH
PADP = NCH * (CH + 1)
PADT = PADP + DB * (DT + 1)
NPAIR = HEADS // 2
LEVELS = 6
L_DECAY, L_AAA, L_GATE = 64, 64, 160
ALPHA = 4 ** 0.25
KAPPA = float(np.exp(-0.5))
NEG = -1e30
TOEP = 384

(R_LNG, R_LNB, R_BQ, R_BKV, R_BO, R_MIX, R_W0, R_A0, R_KK, R_KA, R_RK, R_GW, R_GB, R_SHIFT) = (
    0, 4, 8, 9, 10, 11, 17, 18, 19, 20, 21, 22, 23, 24)
NROW = 32


def constant_layout():
    sizes = [("ident", P), ("ident2", HD), ("bdones", P), ("mean", P), ("strict_p", P), ("incl_p", HD),
             ("strict_s", P), ("incl_s", HD), ("levels", LEVELS * P), ("level0", HD), ("seqmask", DB), ("headmask", 2),
             ("eps", 2)]
    at, out = 0, {}
    for name, n in sizes:
        out[name] = (at, at + n)
        at += n
    return out, at


def t5_bucket(d):
    exact = NBUCKET // 2
    df = np.maximum(d, 1).astype(np.float32)
    large = exact + (np.log(df / np.float32(exact)) / np.float32(np.log(WIN / exact))
                     * np.float32(NBUCKET - exact)).astype(np.int32)
    return np.where(d < exact, d, np.minimum(large, NBUCKET - 1))


def constants():
    cols, width = constant_layout()
    c = np.zeros((P, width), np.float32)

    def put(name, a):
        lo, hi = cols[name]
        c[:a.shape[0], lo:hi] = a.reshape(a.shape[0], -1)

    p, q = np.arange(P)[:, None], np.arange(P)[None, :]
    s, t = p % HD, q % HD
    same_head = (p // HD) == (q // HD)
    same_seq = (s // DT) == (t // DT)
    tc = np.arange(HD)[None, :]
    put("ident", np.eye(P))
    put("ident2", (s == tc))
    put("bdones", same_head)
    put("mean", np.full((P, P), 1.0 / D))
    put("strict_p", same_head & (s < t))
    put("incl_p", s <= tc)
    put("strict_s", same_head & (s < t) & same_seq)
    put("incl_s", (s <= tc) & ((s // DT) == (tc // DT)))
    lv = np.zeros((P, LEVELS, P))
    for level in range(LEVELS):
        b = 1 << level
        lv[:, level] = same_head & (s // (2 * b) == t // (2 * b)) & ((s // b) % 2 == 0) & ((t // b) % 2 == 1)
    put("levels", lv)
    put("level0", (s // 2 == tc // 2) & (s % 2 == 0) & (tc % 2 == 1))
    put("seqmask", (s // DT) == np.arange(DB)[None, :])
    put("headmask", (p // HD) == np.arange(2)[None, :])
    put("eps", np.tile([1e-5, 64e-5], (P, 1)))
    return c


def scan_resets():
    reset = np.ones(PADT, np.float32)
    reset[0:PADP:CH + 1] = 0
    reset[PADP:PADT:DT + 1] = 0
    return np.tile(reset, (P, 1))


def bucket_table():
    onehot = np.zeros((NBUCKET + 1, TOEP), np.float32)
    for y in range(TOEP):
        d = 2 * WIN - 1 - y
        onehot[t5_bucket(np.array(d)) if 0 <= d < WIN else NBUCKET, y] = 1
    return onehot


def build_program(nc, ins, outs, scratch):
    cols, width = constant_layout()
    ctx = ExitStack()
    with ctx:
        def sb(name, shape, dt=F32):
            return ctx.enter_context(nc.sbuf_tensor(name, shape, dt))

        def sem(name):
            return ctx.enter_context(nc.semaphore(name))

        def region(*tensors):
            with ExitStack() as scope:
                return [scope.enter_context(nc.sbuf_tensor(n, s, d)) for n, s, d in tensors]

        cst = sb("cst", [P, width])

        def const(name):
            lo, hi = cols[name]
            return cst[:, lo:hi]

        prm = sb("prm", [P, KB, NROW])
        bqkv = sb("bqkv", [P, QB])
        sink = sb("sink", [P, HEADS])
        sink_s = sb("sink_s", [P, 1])
        credit = sb("credit", [P, 6])
        omka = sb("omka", [P, KB])

        KMAX = FB // 2
        dense = [("x", [P, KB, T], F32), ("raw", [P, 2, KMAX, P], F32), ("wh", [P, 2, KMAX, P], F32R),
                 ("wl", [P, 2, KMAX, P], F32R), ("xh", [P, KB, T], F32R), ("xl", [P, KB, T], F32R),
                 ("lnw", [P, 5, T], F32)]
        NP2 = NPAIR // 2
        wkv1 = [("kk", [P, KB, T], F32), ("bb", [P, KB, T], F32), ("cc", [P, KB, PADT], F32),
                ("zr0", [P, NPAIR, 2, CH], F32), ("zbd0", [P, NPAIR, 2, CH], F32), ("bbd", [P, NPAIR, 2, CH], F32),
                ("kbd", [P, NPAIR, 2, CH], F32), ("vbd", [P, NPAIR, 2, CH], F32),
                ("btm", [P, NPAIR, P], F32), ("ktm", [P, NPAIR, P], F32), ("vtm", [P, NPAIR, P], F32),
                ("vtc", [P, NPAIR, CH], F32), ("lzb", [P, NPAIR, 2, CH], F32), ("lzk", [P, NPAIR, 2, CH], F32),
                ("pc0", [P, NPAIR, DB], F32), ("pc1", [P, NPAIR, DB], F32)]
        kk, bb, cc, zr0, zbd0, bbd, kbd, vbd, btm, ktm, vtm, vtc, lzb, lzk, pc0, pc1 = region(*wkv1)
        x, raw, wh, wl, xh, xl, lnw = [ctx.enter_context(nc.sbuf_tensor(n, s, d)) for n, s, d in dense]
        w1s, a1s, g1s = lnw[:, 0, 0:512].rearrange("p (k n) -> p k n", k=KB), \
            lnw[:, 1, 0:512].rearrange("p (k n) -> p k n", k=KB), \
            lnw[:, 2:5, :].rearrange("p a n -> p (a n)")[:, 0:KB * L_GATE].rearrange("p (k n) -> p k n", k=KB)

        vnb = lnw.rearrange("p a n -> p (a n)")[0:DT, 0:DB * KV * HD].rearrange("p (b n) -> p b n", b=DB)

        xnat, prow, relb, onehot, toep_sb = region(("xnat", [P, 5, D], F32), ("prow", [P, D], F32),
                                           ("relb", [P, HEADS], F32), ("onehot", [NBUCKET + 1, TOEP], F32), ("toep_sb", [HEADS, TOEP], F32))
        (qkvT, biasT, bias_s, S, PT, vtok, ktok, kvnew, ck, cv, ckT, qs, stat) = region(
            ("qkvT", [P, QB, T], F32), ("biasT", [P, HEADS, 2 * WIN], F32), ("bias_s", [P, KEYS], F32),
            ("S", [P, 2, 8 * KEYS], F32), ("PT", [P, 2, 8 * P], F32), ("vtok", [P, 4, KV * HD], F32),
            ("ktok", [P, KV * HD], F32), ("kvnew", [NS, 2, KV * HD], F32), ("ck", [P, DB, KV * HD], F32),
            ("cv", [P, DB, KV * HD], F32), ("ckT", [P, 2, DB, KEYS], F32), ("qs", [P, 2, DB, GROUP * DT], F32), ("stat", [P, 2, 5, 8], F32))
        hh, hl = region(("hh", [P, FB, T], F32R), ("hl", [P, FB, T], F32R))
        gbuf, hbuf = lnw[:, 0:2, :], lnw[:, 2:4, :]
        yout, = region(("yout", [P, 5, D], F32))
        rr, kx, vv = [ctx.enter_context(nc.sbuf_tensor(n, s, F32)) for n, s in (
            ("rr", [P, KB, T]), ("kx", [P, KB, T]), ("vv", [P, KB, T]))]
        xx, mf, mt, twa, wa2, shc, sho, sg, reset = region(
            ("xx", [P, KB, T], F32), ("mf", [P, 2, T], F32), ("mt", [P, 2, T], F32), ("twa", [P, T], F32),
            ("wa2", [P, D], F32), ("shc", [P, KB, 9], F32), ("sho", [9, D], F32),
            ("sg", [P, 2, T], F32), ("reset", [P, PADT], F32))
        g2a, g2b, sg_back, f_rk, f_dev, f_sq, f_sd, f_bon, f_gt = region(
            ("g2a", [P, D], F32), ("g2b", [L_GATE - P, D], F32), ("sg_back", [P, 2, T], F32), ("f_rk", [P, 2, T], F32), ("f_dev", [P, 3, T], F32),
            ("f_sq", [P, 2, T], F32), ("f_sd", [P, 2, T], F32), ("f_bon", [P, 3, T], F32), ("f_gt", [P, 2, T], F32))
        ef, lrb0, lrb1, lrk0, lrk1, zr1, zbd1 = [ctx.enter_context(nc.sbuf_tensor(n, s, F32)) for n, s in (
            ("ef", [P, 3, KB, CH]), ("lrb0", [P, NPAIR, CH]), ("lrb1", [P, NPAIR, CH]), ("lrk0", [P, NPAIR, CH]),
            ("lrk1", [P, NPAIR, CH]), ("zr1", [P, NPAIR, 2, CH]), ("zbd1", [P, NPAIR, 2, CH]))]
        lm, xc, xtb, yc, ybd = region(
            ("lm", [P, NPAIR, P], F32R), ("xc", [P, 2, 2, NP2, CH], F32R), ("xtb", [P, NPAIR, 2, CH], F32R),
            ("yc", [P, NPAIR, CH], F32R), ("ybd", [P, NPAIR, 2, CH], F32R))
        lm0, _, xtf, uc, imx, S_c, sbd = region(
            ("lm0", [P, NPAIR, P], F32), ("xc_pad", [P, 2, 2, NP2, CH], F32), ("xtf", [P, NPAIR, 2, CH], F32),
            ("uc", [P, NPAIR, CH], F32), ("imx", [P, NPAIR, 2, CH], F32), ("S_c", [P, NPAIR, HD], F32),
            ("sbd", [P, NPAIR, 2, HD], F32))
        zr, zbd, pc, lrb, lrk = (zr0, zr1), (zbd0, zbd1), (pc0, pc1), (lrb0, lrb1), (lrk0, lrk1)
        xf, sac, sabd = lm0, uc, imx
        kt = lm0.rearrange("p a n -> p (a n)")[:, 0:NPAIR * CH].rearrange("p (a n) -> p a n", a=NPAIR)
        s0bd = [t.rearrange("p a h n -> p (a h n)").rearrange("p (b n) -> p b n", b=DB) for t in (zr1, zbd1)]
        dpc, stat_out = lrk1, lrb1
        spc = bb[:, :, 0:SEQ].rearrange("p a (b k) -> p a b k", b=DB)
        ef2 = ef[:].rearrange("p a k n -> p (a k n)")[:, 0:2 * T].rearrange("p (a n) -> p a n", a=2)
        nrm = [t.rearrange("p a b -> p (a b)")[:, 0:T] for t in (lm0[:], xtf[:].rearrange("p a h n -> p a (h n)"))]

        def n0(p, b):
            at = (b % 4) * P
            return cc[:, 2 * (p % 4) + b // 4, at:at + P]

        def bkm(p, which):
            return cc[:, 2 * (p % 2) + which, 0:DB * HD]

        ps = ctx.enter_context(nc.psum_tensor("ps", [P, 8, 512], F32))
        halves = [(0, 0), (1, TH)]
        top, low = slice(0, HD), slice(HD, P)

        def two(ap):
            return ap.rearrange("p a (h n) -> p (a h) n", h=2)

        def acc(a):
            return ps[:, 2 * a:2 * a + 2, 0:TH]

        def col(row, j):
            return prm[:, j, row:row + 1]

        class Phase:
            def __init__(self, name, slabs, kblocks, dmas=1):
                self.name, self.slabs, self.kb, self.dmas = name, slabs, kblocks, dmas
                self.ffn_up, self.ffn_down = name.startswith("gu"), name.startswith("dn")

        PH = {p.name: p for p in (
            Phase("qkv", QB, KB, 2), Phase("wo", KB, KB, 4), Phase("gu0", 2 * FB, KB), Phase("dn0", 2 * KB, KMAX),
            Phase("r", KB, KB), Phase("k", KB, KB), Phase("v", KB, KB),
            Phase("ro", KB, KB), Phase("gu1", 2 * FB, KB), Phase("dn1", 2 * KB, KMAX))}
        order = list(PH.values())
        n = m = g = r = 0
        for ph in order:
            ph.n0, ph.m0, ph.g0, ph.r0 = n, m, g, r
            n += ph.slabs
            r += 16 * ph.dmas * (ph.slabs // 2)
            if ph.ffn_up:
                g += FB
            else:
                m += ph.slabs // (2 if ph.ffn_down else 1)
            ph.n1, ph.m1 = n, m

        def after(name):
            return order[[p.name for p in order].index(name) + 1]

        raw_in = [sem("raw_in0"), sem("raw_in1")]
        raw_free = sem("raw_free")
        hi_done = sem("hi_done")
        wslot_free = sem("wslot_free")
        acc_free = sem("acc_free")
        gate_free = sem("gate_free")
        up_free = sem("up_free")
        hid_hi = sem("hid_hi")
        hid_lo = sem("hid_lo")
        op_hi = sem("op_hi")
        op_ready = sem("op_ready")
        stored = sem("stored")
        sems = {}

        def ev(name):
            if name not in sems:
                sems[name] = sem(name)
            return sems[name]

        KV_STORES = 16 * (2 + 2 * DB)
        STATE_STORES = 16 * (2 + 2 * NPAIR)
        outs_stored = [0]
        OP = {"x0": 0, "f0": 1, "r": 2, "k": 3, "v": 4, "z": 5, "f1": 6}
        block = ctx.enter_context(nc.Block())

        @block.sync
        def _(sp):
            sp.dma_start(xnat[:, 0:4, :], ins["x_prompt"].rearrange("o (t p) d -> p (o t) d", p=P)).then_inc(ev("x_in"), 16)
            sp.dma_start(xnat[0:NS, 4, :], ins["x_sample"].rearrange("b t d -> (b t) d")).then_inc(ev("x_in"), 16)
            sp.dma_start(cst[:], ins["constants"]).then_inc(ev("c_in"), 16)
            sp.wait_ge(ev("row_zero"), 2)
            rows = [(R_LNG, 4, ins["ln_g"].rearrange("a b d -> (a b) d")), (R_LNB, 4, ins["ln_b"].rearrange("a b d -> (a b) d")),
                    (R_BO, 1, ins["attn_b_o"]), (R_MIX, 6, ins["rwkv_mix"].rearrange("a c d -> (a c) d")),
                    (R_W0, 1, ins["rwkv_w0"]), (R_A0, 1, ins["rwkv_a0"]), (R_KK, 1, ins["rwkv_k_k"]),
                    (R_KA, 1, ins["rwkv_k_a"]), (R_RK, 1, ins["rwkv_r_k"].rearrange("a h d -> a (h d)")),
                    (R_GW, 1, ins["rwkv_ln_w"]), (R_GB, 1, ins["rwkv_ln_b"]),
                    (R_SHIFT, DB, ins["state_shift"].rearrange("a b d -> (a b) d"))]
            for at, count, src in rows:
                sp.dma_start(prow[at:at + count, :], src).then_inc(ev("p_in"), 16)
            for G in range(2):
                sp.dma_start(prow[R_BQ:R_BQ + 1, G * 512:(G + 1) * 512].rearrange("p (i h d) -> p i h d", i=GROUP, h=2),
                             ins["attn_b_qkv"][:, G * 512:(G + 1) * 512].rearrange("a (h i d) -> a i h d", h=2, i=GROUP)
                             ).then_inc(ev("p_in"), 16)
            sp.dma_start(prow[R_BKV:R_BKV + 1, 0:512], ins["attn_b_qkv"][:, D:QKV]).then_inc(ev("p_in"), 16)
            sp.dma_start(relb[0:NBUCKET, :], ins["rel_bias"]).then_inc(ev("b_in"), 16)
            sp.dma_start(onehot[:], ins["onehot"]).then_inc(ev("b_in"), 16)
            sp.dma_start(sink[:], bass.AP(tensor=ins["attn_sinks"].tensor, offset=0, ap=[[0, P], [1, HEADS]])).then_inc(ev("s_in"), 16)
            sp.dma_start(sink_s[:], bass.AP(tensor=ins["attn_sinks"].tensor, offset=0, ap=[[1, HEADS], [0, DT], [1, 1]])
                         ).then_inc(ev("s_in"), 16)

            sp.dma_start(ck[:], ins["cache_win_k"].rearrange("a b w h d -> w (a b) (h d)")).then_inc(ev("cache_in"), 16)
            sp.dma_start(cv[:], ins["cache_win_v"].rearrange("a b w h d -> w (a b) (h d)")).then_inc(ev("cache_in"), 16)

            wq = ins["attn_w_qkv"].rearrange("a (k p) n -> p (a k) n", p=P)
            for G in range(2):
                heads = wq[:, :, G * 512:(G + 1) * 512].rearrange("p k (h i d) -> p k h (i d)", h=2, i=GROUP)
                with nc.sync.Fori(0, 2) as i:
                    for s in range(2):
                        sp.wait_ge(raw_free, 2 * i + (4 * G + s + 1))
                        for h in range(2):
                            sp.dma_start(raw[:, s, 0:KB, h * HD:(h + 1) * HD],
                                         heads[:, :, h, bass.ds((2 * i + s) * HD, HD)]).then_inc(raw_in[s], 16)
            with nc.sync.Fori(0, 2) as i:
                for s in range(2):
                    sp.wait_ge(raw_free, 2 * i + (KB + s + 1))
                    for h in range(2):
                        sp.dma_start(raw[:, s, 0:KB, h * HD:(h + 1) * HD],
                                     wq[:, :, bass.ds((2 * i + s) * P + (D + h * HD), HD)]).then_inc(raw_in[s], 16)

            wo = ins["attn_w_o"].rearrange("a (G h i d) n -> h d (a G) i n", G=2, h=2, i=GROUP)
            with nc.sync.Fori(0, KB // 2) as i:
                for s in range(2):
                    sp.wait_ge(raw_free, 2 * i + (PH["wo"].n0 + s + 1))
                    for h in range(2):
                        for G in range(2):
                            sp.dma_start(raw[h * HD:(h + 1) * HD, s, G * GROUP:(G + 1) * GROUP, :],
                                         wo[h, :, G, :, bass.ds((2 * i + s) * P, P)]).then_inc(raw_in[s], 16)

            def ffn(up, down, layer):
                wgu = ins["ffn_w_gu"][layer].rearrange("(k p) (u n) -> u p k n", p=P, u=2)
                with nc.sync.Fori(0, FB) as i:
                    for s in range(2):
                        sp.wait_ge(raw_free, 2 * i + (up.n0 + s + 1))
                        sp.dma_start(raw[:, s, 0:KB, :], wgu[s, :, :, bass.ds(i * P, P)]).then_inc(raw_in[s], 16)
                wd = ins["ffn_w_down"][layer].rearrange("(u k p) n -> u p k n", p=P, u=2)
                with nc.sync.Fori(0, KB) as i:
                    for s in range(2):
                        sp.wait_ge(raw_free, 2 * i + (down.n0 + s + 1))
                        sp.dma_start(raw[:, s, :, :], wd[s, :, :, bass.ds(i * P, P)]).then_inc(raw_in[s], 16)

            ffn(PH["gu0"], PH["dn0"], 0)

            def square(ph, w, x_back=False):
                v = w.rearrange("(k p) n -> p k n", p=P)

                def two_slabs(i):
                    for s in range(2):
                        sp.wait_ge(raw_free, 2 * i + (ph.n0 + s + 1))
                        sp.dma_start(raw[:, s, 0:KB, :], v[:, :, bass.ds((2 * i + s) * P, P)]).then_inc(raw_in[s], 16)
                if x_back:
                    two_slabs(0)
                    for j in range(KB):
                        sp.wait_ge(ev("bon"), j + 1)
                        sp.dma_start(x[:, j, :], scratch["x"][:, j, :]).then_inc(ev("x_moved"), 16)
                with nc.sync.Fori(int(x_back), KB // 2) as i:
                    two_slabs(i)

            for name, c in (("r", 0), ("k", 1), ("v", 2)):
                square(PH[name], ins["rwkv_w_rkv"][0, c])
            sp.wait_ge(ev("n0_zero"), 1)
            for p in range(NPAIR):
                if p >= 4:
                    sp.wait_ge(ev("s0_mm"), p - 3)
                for h, part in ((0, top), (1, low)):
                    for q in range(2):
                        sp.dma_start(cc[part, 2 * (p % 4) + q, 0:4 * P].rearrange("p (b x) -> p b x", b=4)[:, :, h * HD:(h + 1) * HD],
                                     ins["state_wkv"][0, 4 * q:4 * q + 4, 2 * p + h].rearrange("b v k -> v b k")).then_inc(ev(f"n0_in{p % 4}"), 16)
            sp.wait_ge(ev("state_kept"), STATE_STORES)
            square(PH["ro"], ins["rwkv_w_o"][0], x_back=True)
            ffn(PH["gu1"], PH["dn1"], 1)

        @block.gpsimd
        def _(pool):
            nc.gpsimd.memset(prow[:], 0.0).then_inc(ev("row_zero"), 1)
            nc.gpsimd.memset(relb[:], NEG).then_inc(ev("row_zero"), 1)
            for at, free in enumerate((raw_free, wslot_free, acc_free, gate_free, up_free, hid_hi)):
                nc.gpsimd.memset(credit[:, at:at + 1], 0.0).then_inc(free, 2)

            ident = const("ident")

            def split_low(ph):
                with nc.gpsimd.Fori(0, ph.slabs // 2) as i:
                    for s in range(2):
                        pool.wait_ge(hi_done, 2 * i + (ph.n0 + s + 1))
                        nc.gpsimd.tensor_tensor(wl[:, s, 0:ph.kb, :], raw[:, s, 0:ph.kb, :],
                                                wh[:, s, 0:ph.kb, :].bitcast(F32), ALU.subtract).then_inc(raw_free, 1)

            for name in ("qkv", "wo", "gu0", "dn0", "r", "k", "v"):
                split_low(PH[name])

            pool.wait_ge(ev("prep"), KB)
            pool.wait_ge(ev("shift_kept"), 64)
            for t in (bbd, zbd[0], zbd[1], S_c):
                nc.gpsimd.memset(t[:], 0.0)
            for g in range(2):
                nc.gpsimd.memset(sbd[:, g * NP2:(g + 1) * NP2], 0.0).then_inc(ev("sbd"), 1)
            nc.gpsimd.memset(pc[0][:], 0.0).then_inc(ev("wkv_zero"), 1)

            def keys_values(n, first=False):
                tok = bass.ds(n * CH, CH)
                own = const("headmask").unsqueeze(1).unsqueeze(3).to_broadcast([P, NPAIR, 2, CH])
                pool.wait_ge(ev("c_exp"), n + 1)
                nc.gpsimd.tensor_tensor(vbd[:], vv[:, :, tok].unsqueeze(2).to_broadcast([P, NPAIR, 2, CH]), own, ALU.mult)
                if not first:
                    pool.wait_ge(ev("fix"), 2 * n)
                nc.gpsimd.tensor_tensor(kt, kx[:, :, tok], ef[:, 2], ALU.mult).then_inc(ev("kt"), 1)
                pool.wait_ge(ev("kt"), n + 1)
                nc.gpsimd.tensor_tensor(kbd[:], kt.unsqueeze(2).to_broadcast([P, NPAIR, 2, CH]), own, ALU.mult
                                        ).then_inc(ev("c_kv"), 1)

            def clear():
                nc.gpsimd.memset(xtb[:].bitcast(F32), 0.0)
                nc.gpsimd.memset(ybd[:].bitcast(F32), 0.0).then_inc(ev("cleared"), 1)

            def level_masks(c, levels):
                pool.wait_ge(ev("c_kv"), c + 1)
                for level in range(levels):
                    for g in range(2):
                        if level == 0:
                            pool.wait_ge(ev("gram_b"), 2 * c + (g + 1))
                        else:
                            pool.wait_ge(ev("y"), (c * LEVELS + level) * 2 + (g - 1))
                        pr = slice(g * NP2, (g + 1) * NP2)
                        nc.gpsimd.tensor_tensor(
                            (lm if level else lm0)[:, pr, :], lzb[:, pr].rearrange("p a h t -> p a (h t)"),
                            const("levels")[:, level * P:(level + 1) * P].unsqueeze(1).to_broadcast([P, NP2, P]),
                            ALU.mult).then_inc(ev("lm"), 1)
                eye = ident.unsqueeze(1).to_broadcast([P, NP2, P])
                for g in range(2):
                    pr = slice(g * NP2, (g + 1) * NP2)
                    pool.wait_ge(ev("xf"), 2 * c + (g + 1))
                    nc.gpsimd.tensor_tensor(imx[:, pr].rearrange("p a h t -> p a (h t)"), eye, xf[:, pr, :], ALU.subtract
                                            ).then_inc(ev("imx"), 1)

            def step(c):
                level_masks(c, LEVELS)
                keys_values(c + 1)
                pool.wait_ge(ev("cleared"), 1)
                pool.wait_ge(ev("st"), 2 * c + 2)
                clear()

            clear()
            keys_values(0, first=True)
            with nc.gpsimd.Fori(0, NCH) as c:
                step(c)
            nc.gpsimd.memset(cc[:, :, 0:SEQ], 0.0).then_inc(ev("n0_zero"), 1)
            level_masks(NCH, 3)

            for t in range(KB + 1):
                if t < KB:
                    pool.wait_ge(ev("affine"), t + 1)
                    nc.gpsimd.tensor_tensor(f_dev[:, t % 3, :], f_dev[:, t % 3, :], f_bon[:, t % 3, :], ALU.add
                                            ).then_inc(ev("bonused"), 1)
                if t >= 1:
                    pool.wait_ge(op_hi, KB * OP["z"] + t)
                    nc.gpsimd.tensor_tensor(xl[:, t - 1, :], f_dev[:, (t - 1) % 3, :], xh[:, t - 1, :].bitcast(F32), ALU.subtract
                                            ).then_inc(op_ready, 1)

            for name in ("ro", "gu1", "dn1"):
                split_low(PH[name])

        @block.tensor
        def _(pe):
            mm = nc.tensor.matmul
            ident = const("ident")

            def slab(a, s, kb, high, low_, k0, first, last):
                for k in range(kb):
                    for w, o in ((wh, high), (wh, low_), (wl, high)):
                        for b, t0 in halves:
                            out = mm(ps[:, 2 * a + b, 0:TH], w[:, s, k, :], o[:, k0 + k, t0:t0 + TH],
                                     start=(first and k == 0 and w is wh and o is high),
                                     stop=(last and k == kb - 1 and w is wl))
                out.then_inc(wslot_free, 1)

            def product(name, high, low_):
                ph = PH[name]
                with nc.tensor.Fori(0, ph.slabs // 2) as i:
                    for s in range(2):
                        pe.wait_ge(raw_free, 2 * i + (ph.n0 + s + 3))
                        pe.wait_ge(acc_free, 2 * i + (ph.m0 + s + 1))
                        slab(s, s, ph.kb, high, low_, 0, True, True)

            def operand(name):
                pe.wait_ge(op_ready, KB * (OP[name] + 1))

            def ffn(i_ffn):
                up, down = PH[f"gu{i_ffn}"], PH[f"dn{i_ffn}"]
                operand(f"f{i_ffn}")
                with nc.tensor.Fori(0, FB // 2) as i:
                    for q in range(2):
                        for s, free in ((0, gate_free), (1, up_free)):
                            pe.wait_ge(raw_free, 4 * i + (up.n0 + 2 * q + s + 3))
                            pe.wait_ge(free, 2 * i + (up.g0 + q + 1))
                            slab(2 * q + s, s, KB, xh, xl, 0, True, True)
                pe.wait_ge(hid_lo, FB * (i_ffn + 1))
                with nc.tensor.Fori(0, KB // 2) as i:
                    for q in range(2):
                        pe.wait_ge(acc_free, 2 * i + (down.m0 + q + 1))
                        for s in range(2):
                            pe.wait_ge(raw_free, 4 * i + (down.n0 + 2 * q + s + 3))
                            slab(q, s, KMAX, hh, hl, s * KMAX, s == 0, s == 1)

            def norm(i_ln, ph):
                pe.wait_ge(acc_free, ph.m1 + 2)
                for j in range(KB):
                    for b, t0 in halves:
                        out = mm(ps[:, 4 + b, 0:TH], const("mean"), x[:, j, t0:t0 + TH], start=(j == 0), stop=(j == KB - 1))
                out.then_inc(ev("ln_mean"), 1)
                for j in range(KB):
                    pe.wait_ge(ev("ln_sq"), KB * i_ln + j + 1)
                    for b, t0 in halves:
                        out = mm(ps[:, 6 + b, 0:TH], const("mean"), lnw[:, 3 + j % 2, t0:t0 + TH], start=(j == 0), stop=(j == KB - 1))
                    out.then_inc(ev("ln_sum"), 1)

            pe.wait_ge(ev("c_in"), 16)
            pe.wait_ge(ev("x_in"), 32)
            for j in range(KB):
                if j >= 4:
                    pe.wait_ge(ev("xT_taken"), j - 3)
                for t in range(4):
                    out = nc.tensor.transpose(ps[:, j % 4, t * P:(t + 1) * P], xnat[:, t, j * P:(j + 1) * P], ident)
                out.then_inc(ev("xT"), 1)
            for j in range(KB):
                out = nc.tensor.transpose(ps[:, 4, j * NS:(j + 1) * NS], xnat[0:NS, 4, j * P:(j + 1) * P], ident[0:NS, 0:NS])
            out.then_inc(ev("xT"), 1)
            pe.wait_ge(ev("p_in"), 16 * 15)
            for j in range(KB):
                out = nc.tensor.transpose(ps[:, 5, j * NROW:(j + 1) * NROW], prow[0:NROW, j * P:(j + 1) * P], ident[0:NROW, 0:NROW])
            out.then_inc(ev("pT"), 1)
            pe.wait_ge(ev("b_in"), 32)
            mm(ps[0:HEADS, 6, 0:TOEP], relb[0:NBUCKET + 1, :], onehot[:],
               start=True, stop=True).then_inc(ev("pT"), 1)

            pe.wait_ge(ev("setup_taken"), 3)
            operand("x0")
            product("qkv", xh, xl)

            pe.wait_ge(acc_free, PH["qkv"].m1 + 2)
            for G in range(2):
                for kv in range(2):
                    nc.tensor.transpose(ps[0:NS, 4, (kv * 2 + G) * P:(kv * 2 + G + 1) * P],
                                        qkvT[:, KB + 2 * kv + G, SEQ:T], ident)
            for G in range(2):
                out = nc.tensor.transpose(ps[:, 5, G * P:(G + 1) * P], qkvT[:, KB + G, SEQ - WIN:SEQ], ident)
            for t in range(4):
                for G in range(2):
                    out = nc.tensor.transpose(ps[:, 6 + t // 2, (t % 2) * 256 + G * P:(t % 2) * 256 + (G + 1) * P],
                                              qkvT[:, KB + 2 + G, t * P:(t + 1) * P], ident)
            out.then_inc(ev("kv_tok"), 1)

            units = [(qb, g) for qb in range(SEQ // WIN) for g in range(KV)]
            U = len(units)
            pe.wait_ge(ev("tok_taken"), 1)
            for t in range(U + 2):
                if t < U:
                    qb, g = units[t]
                    W = WIN if qb == 0 else 2 * WIN
                    part, G = (top, low)[g % 2], g // 2
                    if t >= 2:
                        pe.wait_ge(ev("s_taken"), t - 1)
                    for i in range(GROUP):
                        out = mm(ps[:, 2 * (t % 2) + i // 2, (i % 2) * W:(i % 2 + 1) * W],
                                 qkvT[part, G * GROUP + i, qb * WIN:(qb + 1) * WIN],
                                 qkvT[part, KB + G, (qb + 1) * WIN - W:(qb + 1) * WIN], start=True, stop=True)
                    out.then_inc(ev("s_mm"), 1)
                if 1 <= t <= U:
                    u = t - 1
                    nkb = 1 if units[u][0] == 0 else 2
                    pe.wait_ge(ev("probs"), u + 1)
                    if u >= 1:
                        pe.wait_ge(ev("pt_taken"), u)
                    for kb in range(nkb):
                        for i in range(GROUP):
                            W = nkb * WIN
                            out = nc.tensor.transpose(ps[:, 4 + kb, i * P:(i + 1) * P],
                                                      S[:, u % 2, i * W + kb * P:i * W + (kb + 1) * P], ident)
                    out.then_inc(ev("pt_mm"), 1)
                if t >= 2:
                    u = t - 2
                    qb, g = units[u]
                    nkb = 1 if qb == 0 else 2
                    part, pair = (top, low)[g % 2], u // 2
                    pe.wait_ge(ev("pt_taken"), u + 1)
                    if g % 2 == 0 and pair >= 2:
                        pe.wait_ge(ev("o_taken"), pair - 1)
                    for kb in range(nkb):
                        out = mm(ps[part, 6 + pair % 2, :], vtok[:, qb - nkb + 1 + kb, g * HD:(g + 1) * HD],
                                 PT[:, u % 2, kb * 512:(kb + 1) * 512], start=(kb == 0), stop=(kb == nkb - 1))
                    out.then_inc(ev("o_mm"), 1)

            pe.wait_ge(ev("cache_in"), 32)
            pe.wait_ge(ev("s_taken"), U)
            for G in range(2):
                for b in range(DB):
                    out = nc.tensor.transpose(ps[:, 2 * G + b // 4, (b % 4) * P:(b % 4 + 1) * P], ck[:, b, G * P:(G + 1) * P], ident)
            out.then_inc(ev("ckT_mm"), 1)
            pe.wait_ge(ev("ckT"), 1)
            pe.wait_ge(ev("ckT_new"), 1)
            pe.wait_ge(ev("o_taken"), U // 2)
            for b in range(DB):
                for g in range(KV):
                    part, G = (top, low)[g % 2], g // 2
                    out = mm(ps[32 * g:32 * (g + 1), 4 + b // 3, (b % 3) * KEYS:(b % 3 + 1) * KEYS],
                             qs[part, G, b, :],
                             ckT[part, G, b, :], start=True, stop=True)
            out.then_inc(ev("ss_mm"), 1)
            pe.wait_ge(ev("s_probs"), 1)
            for b in range(DB):
                nc.tensor.transpose(ps[:, b // 4, (b % 4) * P:(b % 4 + 1) * P], S[:, 0, b * KEYS:b * KEYS + WIN], ident)
                out = nc.tensor.transpose(ps[0:DT, 2 + b // 4, (b % 4) * P:(b % 4 + 1) * P],
                                          S[:, 0, b * KEYS + WIN:(b + 1) * KEYS], ident)
            out.then_inc(ev("spt_mm"), 1)
            pe.wait_ge(ev("spt"), 1)
            pe.wait_ge(ev("vnb_in"), 16 * DB)
            o_s = ps[:, 7, :].rearrange("p (G i b t) -> p G i b t", G=2, i=GROUP, b=DB)
            for b in range(DB):
                for g in range(KV):
                    part, G = (top, low)[g % 2], g // 2
                    mm(o_s[part, G, :, b, :], cv[:, b, g * HD:(g + 1) * HD], PT[:, 0, b * P + 32 * g:b * P + 32 * (g + 1)],
                       start=True, stop=False)
                    out = mm(o_s[part, G, :, b, :], vnb[:, b, g * HD:(g + 1) * HD],
                             PT[0:DT, 1, b * P + 32 * g:b * P + 32 * (g + 1)], start=False, stop=True)
            out.then_inc(ev("so_mm"), 1)
            pe.wait_ge(ev("att_ready"), 1)
            product("wo", xh, xl)

            norm(0, PH["wo"])
            ffn(0)
            norm(1, PH["dn0"])

            def lora_in(step, products):
                for k in range(KB):
                    pe.wait_ge(ev("mf"), KB * step + k + 1)
                    for w, part, bank in products:
                        for b, t0 in halves:
                            out = mm(ps[part, bank + b, 0:TH], w(k), mf[:, k % 2, t0:t0 + TH], start=(k == 0), stop=(k == KB - 1))
                    out.then_inc(ev("mf_used"), 1)

            pe.wait_ge(ev("shc"), 1)
            for j in range(KB):
                out = nc.tensor.transpose(ps[0:9, 6 + j // 4, (j % 4) * P:(j % 4 + 1) * P], shc[:, j, :], ident)
            out.then_inc(ev("sh_mm"), 1)
            operand("r")
            product("r", xh, xl)
            pe.wait_ge(ev("lora_w_in"), 16 * 6)
            lora_in(0, [(lambda k: w1s[:, k, :], top, 4)])
            operand("k")
            product("k", xh, xl)
            pe.wait_ge(ev("lora_out"), 1)
            lora_in(1, [(lambda k: a1s[:, k, :], low, 4)])
            operand("v")
            product("v", xh, xl)
            pe.wait_ge(ev("lora_out"), 2)
            pe.wait_ge(ev("sh_taken"), 1)
            lora_in(2, [(lambda k: g1s[:, k, 0:P], slice(0, P), 4), (lambda k: g1s[:, k, P:L_GATE], slice(0, L_GATE - P), 6)])

            pe.wait_ge(ev("proj_taken"), 1)
            pe.wait_ge(acc_free, PH["v"].m1 + 2)
            for i_l, part in enumerate((top, low)):
                for j in range(KB):
                    q = i_l * KB + j
                    if q >= 2:
                        pe.wait_ge(ev("lora2_taken"), q - 1)
                    b = 2 * (j % 2)
                    mm(ps[:, b, :], wa2[part, j * P:(j + 1) * P], twa[part, 0:SEQ], start=True, stop=True)
                    mm(ps[:, b + 1, 0:NS], wa2[part, j * P:(j + 1) * P], twa[part, SEQ:T], start=True, stop=True).then_inc(ev("lora2_mm"), 1)
            for j in range(KB):
                pe.wait_ge(ev("kk_sq"), j + 1)
                if j >= 2:
                    pe.wait_ge(ev("kk_norm"), j - 1)
                for b, t0 in halves:
                    out = mm(ps[:, 4 + 2 * (j % 2) + b, 0:TH], const("bdones"), ef2[:, j % 2, t0:t0 + TH], start=True, stop=True)
                out.then_inc(ev("kk_sum"), 1)

            pairs = [range(g * NP2, (g + 1) * NP2) for g in range(2)]

            def flat(ap):
                return ap.rearrange("p h t -> p (h t)")

            def gram_b(n, q):
                pe.wait_ge(ev("c_pre"), n + 1)
                for g in range(2):
                    for n_, p in enumerate(pairs[g]):
                        out = mm(ps[:, g, n_ * P:(n_ + 1) * P], flat(bbd[:, p]), flat(zr[q][:, p]), start=True, stop=True)
                    out.then_inc(ev("gb"), 1)

            def gram_k(n, q):
                pe.wait_ge(ev("c_kv"), n + 1)
                for g in range(2):
                    for n_, p in enumerate(pairs[g]):
                        out = mm(ps[:, 2 + g, n_ * P:(n_ + 1) * P], flat(kbd[:, p]), flat(zr[q][:, p]), start=True, stop=True)
                    out.then_inc(ev("gk"), 1)

            def token_major(n, first=False):
                for src, bank, name in ((vbd, 0, "tv"), (bbd, 4, "tb"), (kbd, 6, "tk")):
                    if name == "tb" and not first:
                        pe.wait_ge(ev("sadd"), 2 * n)
                    for g in range(2):
                        if name == "tv":
                            pe.wait_ge(ev("gram_b"), 2 * n + (g + 1))
                        for n_, p in enumerate(pairs[g]):
                            out = nc.tensor.transpose(ps[:, bank + g, n_ * P:(n_ + 1) * P], flat(src[:, p]), ident)
                        out.then_inc(ev(name), 1)

            def invert(c, levels):
                for level in range(levels):
                    for g in range(2):
                        pe.wait_ge(ev("lm"), (c * LEVELS + level + 1) * 2 + (g - 1))
                        if level == 0:
                            pe.wait_ge(ev("tok_b"), 2 * c + g + 1)
                        else:
                            pe.wait_ge(ev("xup"), (c * LEVELS + level) * 2 + (g - 1))
                            if level > 1:
                                pe.wait_ge(ev("yc"), (c * (LEVELS - 1) + level - 1) * 2 + (g - 1))
                        for n_, p in enumerate(pairs[g]):
                            out = mm(ps[:, 4 + g, n_ * CH:(n_ + 1) * CH], (lm if level else lm0)[:, p, :],
                                     xc[:, g, 0, n_, :] if level else const("ident2"), start=True, stop=True)
                        out.then_inc(ev("y"), 1)
                    if level == 0:
                        continue
                    for g in range(2):
                        pe.wait_ge(ev("yc"), (c * (LEVELS - 1) + level) * 2 + (g - 1))
                        pe.wait_ge(ev("ybd"), (c * (LEVELS - 1) + level) * 2 + (g - 1))
                        pe.wait_ge(ev("xtb"), (c * LEVELS + level) * 2 + (g - 1))
                        if level == 1:
                            pe.wait_ge(ev("tok_k"), 2 * c + g + 1)
                        for n_, p in enumerate(pairs[g]):
                            if level < levels - 1:
                                mm(ps[:, 6 + g, n_ * CH:(n_ + 1) * CH], flat(xtb[:, p]), yc[:, p, :], start=True, stop=True)
                            out = mm(ps[:, 6 + g, 256 + n_ * CH:256 + (n_ + 1) * CH], flat(ybd[:, p]),
                                     xc[:, g, 1, n_, :], start=True, stop=True)
                        out.then_inc(ev("xm"), 1)
                for g in range(2):
                    pe.wait_ge(ev("xtb"), (c * LEVELS + levels) * 2 + (g - 1))
                    for n_, p in enumerate(pairs[g]):
                        out = nc.tensor.transpose(ps[:, 4 + g, n_ * P:(n_ + 1) * P], flat(xtb[:, p]).bitcast(F32), ident)
                    out.then_inc(ev("xx_mm"), 1)
                for g in range(2):
                    pe.wait_ge(ev("xf"), 2 * c + (g + 1))
                    for n_, p in enumerate(pairs[g]):
                        out = mm(ps[:, 6 + g, n_ * P:(n_ + 1) * P], flat(lzb[:, p]), xf[:, p, :], start=True, stop=True)
                    out.then_inc(ev("lx"), 1)

            def refine(c):
                for g in range(2):
                    pe.wait_ge(ev("res"), 2 * c + (g + 1))
                    for n_, p in enumerate(pairs[g]):
                        out = mm(ps[:, 6 + g, n_ * P:(n_ + 1) * P], lm[:, p, :], flat(xtb[:, p]), start=True, stop=True)
                    out.then_inc(ev("fix"), 1)

            def state_step(c, q, levels, sample=False, ahead_b=None, ahead_k=None):
                for g in range(2):
                    pe.wait_ge(ev("gram_k"), 2 * c + (g + 1))
                    pe.wait_ge(ev("tok_v"), 2 * c + g + 1)
                    pe.wait_ge(ev("sbd"), (c + 1) * 2 + (g - 1))
                    for n_, p in enumerate(pairs[g]):
                        o = ps[:, 4 + g, 256 + n_ * HD:256 + (n_ + 1) * HD]
                        if sample:
                            mm(o, flat(sbd[:, p]), const("ident2"), start=True, stop=False)
                        else:
                            mm(o, flat(zbd[q][:, p]), S_c[:, p, :], start=True, stop=False)
                        out = mm(o, flat(lzk[:, p]), vtc[:, p, :], start=False, stop=True)
                    out.then_inc(ev("u"), 1)
                refine(c)
                if ahead_b:
                    ahead_b()
                for g in range(2):
                    pe.wait_ge(ev("uc"), 2 * c + (g + 1))
                    pe.wait_ge(ev("xtf"), 2 * c + (g + 1))
                    for n_, p in enumerate(pairs[g]):
                        out = mm(ps[:, 6 + g, n_ * HD:(n_ + 1) * HD], flat(xtf[:, p]), uc[:, p, :], start=True, stop=True)
                    out.then_inc(ev("sa"), 1)
                if ahead_k:
                    ahead_k()
                for g in range(2):
                    pe.wait_ge(ev("sac"), 2 * c + (g + 1))
                    for n_, p in enumerate(pairs[g]):
                        o = ps[:, 4 + g, n_ * CH:(n_ + 1) * CH]
                        if not sample:
                            mm(o, flat(sbd[:, p]), zr[q][:, p, 1, :], start=True, stop=False)
                        mm(o, flat(sabd[:, p]), lrb[q][:, p, :], start=sample, stop=False)
                        out = mm(o, vtm[:, p, :], lrk[q][:, p, :], start=False, stop=True)
                    out.then_inc(ev("o"), 1)
                if sample:
                    return
                for g in range(2):
                    for n_, p in enumerate(pairs[g]):
                        o = ps[:, 6 + g, 256 + n_ * HD:256 + (n_ + 1) * HD]
                        mm(o, btm[:, p, :], sac[:, p, :], start=True, stop=False)
                        out = mm(o, ktm[:, p, :], vtc[:, p, :], start=False, stop=True)
                    out.then_inc(ev("st"), 1)

            def step(c, q, transposes=True):
                invert(c, LEVELS)
                state_step(c, q, LEVELS, ahead_b=lambda: gram_b(c + 1, 1 - q), ahead_k=lambda: gram_k(c + 1, 1 - q))
                if transposes:
                    token_major(c + 1)

            pe.wait_ge(ev("wkv_zero"), 1)
            gram_b(0, 0)
            gram_k(0, 0)
            token_major(0, first=True)
            with nc.tensor.Fori(0, NCH // 2 - 1) as i:
                for q in range(2):
                    step(2 * i + q, q)
            step(NCH - 2, 0)
            step(NCH - 1, 1, transposes=False)
            pe.wait_ge(ev("hats"), 1)
            token_major(NCH)
            pe.wait_ge(ev("tok_v"), 2 * NCH + 2)
            for g in range(2):
                pe.wait_ge(ev("sbd"), 2 * (NCH + 1) - 1 + g)
            for p in range(NPAIR):
                out = mm(ps[:, 0, p * HD:(p + 1) * HD], flat(sbd[:, p]), const("ident2"), start=True, stop=True)
            out.then_inc(ev("state_mm"), 1)
            pe.wait_ge(ev("tok_b"), 2 * NCH + 2)
            pe.wait_ge(ev("tok_k"), 2 * NCH + 2)
            pe.wait_ge(ev("state_out"), 1)
            for t in range(NPAIR + 1):
                if t < NPAIR:
                    pe.wait_ge(ev(f"n0_in{t % 4}"), 64 * (t // 4 + 1))
                    if t >= 2:
                        pe.wait_ge(ev("s0bd"), t - 1)
                    for b in range(DB):
                        out = nc.tensor.transpose(ps[:, 4 + 2 * (t % 2) + b // 4, (b % 4) * P:(b % 4 + 1) * P], n0(t, b), ident)
                    out.then_inc(ev("s0_mm"), 1)
                if t >= 1:
                    p = t - 1
                    pe.wait_ge(ev("s0bd"), p + 1)
                    if p >= 2:
                        pe.wait_ge(ev("zs_taken"), p - 1)
                    for b in range(DB):
                        at = b * 2 * DT
                        out = mm(ps[:, p % 2, at:at + 2 * DT].rearrange("p (z t) -> p z t", z=2),
                                 s0bd[p % 2][:, b, :], zr[0][:, p, :, b * DT:(b + 1) * DT], start=True, stop=True)
                    out.then_inc(ev("zs_mm"), 1)
                    pe.wait_ge(ev("dpc"), p + 1)
                    if p >= 2:
                        pe.wait_ge(ev("s0_done"), p - 1)
                    for b in range(DB):
                        out = mm(ps[:, 2 + p % 2, b * HD:(b + 1) * HD], s0bd[p % 2][:, b, :], dpc[:, b, :], start=True, stop=True)
                    out.then_inc(ev("sp_mm"), 1)
            pe.wait_ge(ev("zs_taken"), NPAIR)
            invert(NCH, 3)
            state_step(NCH, 0, 3, sample=True)
            for p in range(NPAIR):
                pe.wait_ge(ev("bkm"), p + 1)
                if p >= 2:
                    pe.wait_ge(ev("sst"), p - 1)
                o = ps[:, 6 + p % 2, :]
                mm(o, sabd[:, p].rearrange("p h v -> p (h v)"), bkm(p, 0), start=True, stop=False)
                mm(o, vtm[:, p, :], bkm(p, 1), start=False, stop=True).then_inc(ev("sst_mm"), 1)

            pe.wait_ge(ev("g2_in"), 64)
            for t in range(KB + 1):
                if t < KB:
                    pe.wait_ge(ev("rk"), t + 1)
                    if t >= 1:
                        pe.wait_ge(ev("bon"), t)
                    for src, bank in ((f_rk[:, t % 2], 0), (kk[:, t], 2)):
                        for b, t0 in halves:
                            out = mm(ps[:, bank + b, 0:TH], const("bdones"), src[:, t0:t0 + TH], start=True, stop=True)
                    out.then_inc(ev("f_sums"), 1)
                    if t >= 1:
                        pe.wait_ge(ev("gate"), t)
                    for b, t0 in halves:
                        mm(ps[:, 6 + b, 0:TH], g2a[:, t * P:(t + 1) * P], sg_back[:, 0, t0:t0 + TH], start=True, stop=False)
                        out = mm(ps[:, 6 + b, 0:TH], g2b[:, t * P:(t + 1) * P], sg_back[0:L_GATE - P, 1, t0:t0 + TH], start=False, stop=True)
                    out.then_inc(ev("gate_mm"), 1)
                if t >= 1:
                    pe.wait_ge(ev("dev_sq"), t)
                    if t >= 2:
                        pe.wait_ge(ev("sd"), t - 1)
                    for b, t0 in halves:
                        out = mm(ps[:, 4 + b, 0:TH], const("bdones"), f_sq[:, (t - 1) % 2, t0:t0 + TH], start=True, stop=True)
                    out.then_inc(ev("var_mm"), 1)

            operand("z")
            product("ro", xh, xl)
            norm(2, PH["ro"])
            ffn(1)
            norm(3, PH["dn1"])
            for t in range(5):
                n_ = P if t < 4 else NS
                if t == 0:
                    pe.wait_ge(ev("ln_x"), 4 * KB)
                if t >= 2:
                    pe.wait_ge(ev("y_taken"), t - 1)
                for j in range(KB):
                    out = nc.tensor.transpose(ps[0:n_, 2 * (t % 2) + j // 4, (j % 4) * P:(j % 4 + 1) * P],
                                              x[:, j, t * P:t * P + n_], ident)
                out.then_inc(ev("y_mm"), 1)

        @block.scalar
        def _(act):
            A = nc.scalar.activation

            def split_high(ph, t, s):
                act.wait_ge(raw_in[s], ph.r0 + 16 * ph.dmas * (t // 2 + 1) if isinstance(t, int)
                            else (t - s) * (8 * ph.dmas) + (ph.r0 + 16 * ph.dmas))
                act.wait_ge(wslot_free, t + (ph.n0 + 1))
                nc.scalar.copy(wh[:, s, 0:ph.kb, :], raw[:, s, 0:ph.kb, :]).then_inc(hi_done, 1)

            def high_ahead(ph, t, s, last):
                if last:
                    if ph.name in ("v", "dn1"):
                        return
                    split_high(after(ph.name), s, s)
                else:
                    split_high(ph, t + 2, s)

            def product(name, take=None):
                ph = PH[name]
                rounds = ph.slabs // 2

                def body(i, last):
                    for s in range(2):
                        high_ahead(ph, 2 * i + s, s, last)
                        if take:
                            act.wait_ge(wslot_free, 2 * i + (ph.n0 + s + 3))
                            take(2 * i + s, s)
                with nc.scalar.Fori(0, rounds - 1) as i:
                    body(i, False)
                body(rounds - 1, True)

            def ffn(i_ffn):
                up = PH[f"gu{i_ffn}"]

                def body(i, last):
                    for q in range(2):
                        for s in range(2):
                            high_ahead(up, 4 * i + 2 * q + s, s, last and q == 1)
                            if s == 0:
                                act.wait_ge(wslot_free, 4 * i + (up.n0 + 2 * q + 3))
                                act.wait_ge(up_free, 2 * i + (up.g0 + q + 1))
                                A(gbuf[:, q, :].rearrange("p (h n) -> p h n", h=2), acc(2 * q), ACT.Silu).then_inc(gate_free, 1)
                        act.wait_ge(up_free, 2 * i + (up.g0 + q + 3))
                        A(hh[:, bass.ds(2 * i + q, 1), :], hbuf[:, q:q + 1, :], ACT.Copy).then_inc(hid_hi, 1)
                with nc.scalar.Fori(0, FB // 2 - 1) as i:
                    body(i, False)
                body(FB // 2 - 1, True)
                product(f"dn{i_ffn}")

            def scale_x(i, bias=None):
                if bias is None:
                    nc.scalar.mul(x[:], x[:], ALPHA).then_inc(ev("x_scaled"), 1)
                else:
                    for j in range(KB):
                        out = A(x[:, j, :], x[:, j, :], ACT.Identity, bias=col(bias, j), scale=ALPHA)
                    out.then_inc(ev("x_scaled"), 1)

            def norm(i_ln, ph, gain, shift_row):
                act.wait_ge(acc_free, ph.m1 + 2)
                for j in range(KB):
                    if i_ln or j >= 2:
                        act.wait_ge(ev("ln_sum"), KB * i_ln + j - 1 if j >= 2 else KB * i_ln)
                    A(lnw[:, 3 + j % 2, :], x[:, j, :], ACT.Square).then_inc(ev("ln_sq"), 1)
                act.wait_ge(ev("ln_var"), i_ln + 1)
                A(lnw[:, 1, :], lnw[:, 1, :], ACT.Sqrt, bias=const("eps")[:, 0:1]).then_inc(ev("ln_sd"), 1)
                for j in range(KB):
                    act.wait_ge(ev("ln_hat"), KB * i_ln + j + 1)
                    A(x[:, j, :], x[:, j, :], ACT.Identity, bias=col(shift_row, j), scale=col(gain, j)).then_inc(ev("ln_x"), 1)
                    if i_ln in (0, 2):
                        act.wait_ge(ev("ln_x"), KB * i_ln + j + 1)
                        A(xh[:, j, :], x[:, j, :], ACT.Copy).then_inc(op_hi, 1)

            for j in range(KB):
                act.wait_ge(ev("xT"), j + 1)
                A(x[:, j, 0:SEQ], ps[:, j % 4, :], ACT.Copy).then_inc(ev("xT_taken"), 1)
            act.wait_ge(ev("xT"), KB + 1)
            A(x[:, :, SEQ:T], ps[:, 4, :].rearrange("p (k n) -> p k n", k=KB), ACT.Copy).then_inc(ev("xT_taken"), 1)
            act.wait_ge(ev("xT_taken"), KB + 1)
            for s in range(2):
                split_high(PH["qkv"], s, s)
            for j in range(KB):
                A(xh[:, j, :], x[:, j, :], ACT.Copy).then_inc(op_hi, 1)
            act.wait_ge(ev("setup_taken"), 2)
            act.dma_start(scratch["table"], toep_sb[:]).then_inc(ev("table_out"), 16)
            act.wait_ge(ev("table_out"), 16)
            act.dma_start(scratch["spread"], bass.AP(tensor=scratch["table"].tensor, offset=0,
                                                     ap=[[TOEP, HEADS], [0, P], [1, TOEP]])).then_inc(ev("table_out"), 16)
            act.wait_ge(ev("table_out"), 32)
            act.wait_ge(ev("setup_taken"), 3)
            skew = scratch["spread"].tensor
            act.dma_start(biasT[:], bass.AP(tensor=skew, offset=WIN - 1, ap=[[TOEP - 1, P], [P * TOEP, HEADS], [1, 2 * WIN]])
                          ).then_inc(ev("bias_in"), 16)
            act.dma_start(bias_s[:], bass.AP(tensor=skew, offset=WIN - 1, ap=[[P * TOEP, HEADS], [TOEP - 1, DT], [1, KEYS]])
                          ).then_inc(ev("bias_in"), 16)
            act.wait_ge(op_ready, KB)
            scale_x(0, R_BO)
            for q, (new, old) in enumerate((("sk", "cache_win_k"), ("sv", "cache_win_v"))):
                act.dma_start(outs[new][0, :, 0:WIN - DT], ins[old][0, :, DT:WIN]).then_inc(stored, 16)
                outs_stored[0] += 1
            product("qkv")

            act.wait_ge(ev("kv_tok"), 1)
            A(kvnew[:], ps[0:NS, 4, :].rearrange("p (a n) -> p a n", a=2), ACT.Copy)
            A(ktok[:], ps[:, 5, 0:256], ACT.Copy)
            A(vtok[:, 0:2, :], ps[:, 6, :].rearrange("p (a n) -> p a n", a=2), ACT.Copy)
            A(vtok[:, 2:4, :], ps[:, 7, :].rearrange("p (a n) -> p a n", a=2), ACT.Copy).then_inc(ev("tok_taken"), 1)
            act.wait_ge(ev("tok_taken"), 1)
            act.dma_start(outs["pk"].rearrange("a b w h d -> w (a b) (h d)"), ktok[:].unsqueeze(1)).then_inc(ev("kv_kept"), 16)
            act.dma_start(outs["pv"].rearrange("a b w h d -> w (a b) (h d)"), vtok[:, 3:4, :]).then_inc(ev("kv_kept"), 16)
            for b in range(DB):
                act.dma_start(vnb[:, b, :], kvnew[b * DT:(b + 1) * DT, 1, :]).then_inc(ev("vnb_in"), 16)
                for q, name in enumerate(("sk", "sv")):
                    act.dma_start(outs[name][0, b, WIN - DT:WIN].rearrange("w h d -> w (h d)"), kvnew[b * DT:(b + 1) * DT, q, :]
                                  ).then_inc(ev("kv_kept"), 16)
            U = 4 * KV
            for t in range(U + 1):
                if t < U:
                    slot, W = t % 2, WIN if t < KV else 2 * WIN
                    act.wait_ge(ev("s_max"), t + 1)
                    for i in range(GROUP):
                        A(S[:, slot, i * W:(i + 1) * W], S[:, slot, i * W:(i + 1) * W], ACT.Exp,
                          bias=stat[:, slot, 0, i:i + 1], accum_out=stat[:, slot, 1, i:i + 1])
                    A(stat[:, slot, 3, 0:GROUP], stat[:, slot, 2, 0:GROUP], ACT.Exp).then_inc(ev("s_exp"), 1)
                if t >= 1:
                    u = t - 1
                    n_ = 1 if u < KV else 2
                    act.wait_ge(ev("pt_mm"), u + 1)
                    if u >= 2:
                        act.wait_ge(ev("o_mm"), u - 1)
                    A(PT[:, u % 2, 0:n_ * 512].rearrange("p (a n) -> p a n", a=n_), ps[:, 4:4 + n_, :], ACT.Copy).then_inc(ev("pt_taken"), 1)
            act.wait_ge(ev("ckT_mm"), 1)
            for G in range(2):
                for q in range(2):
                    out = A(ckT[:, G, 4 * q:4 * q + 4, 0:WIN], ps[:, 2 * G + q, :].rearrange("p (b n) -> p b n", b=4), ACT.Copy)
            out.then_inc(ev("ckT"), 1)
            act.wait_ge(ev("ss_max"), 1)
            for b in range(DB):
                A(S[:, 0, b * KEYS:(b + 1) * KEYS], S[:, 0, b * KEYS:(b + 1) * KEYS], ACT.Exp,
                  bias=stat[:, 0, 0, b:b + 1], accum_out=stat[:, 0, 1, b:b + 1])
            A(stat[:, 0, 3, :], stat[:, 0, 2, :], ACT.Exp).then_inc(ev("ss_exp"), 1)
            act.wait_ge(ev("spt_mm"), 1)
            act.wait_ge(ev("o_mm"), U)
            for q in range(2):
                A(PT[:, 0, q * 512:(q + 1) * 512], ps[:, q, :], ACT.Copy)
                out = A(PT[0:DT, 1, q * 512:(q + 1) * 512], ps[0:DT, 2 + q, :], ACT.Copy)
            out.then_inc(ev("spt"), 1)

            product("wo")
            norm(0, PH["wo"], R_LNG + 0, R_LNB + 0)
            act.wait_ge(op_ready, KB * 2)
            scale_x(1)
            act.wait_ge(ev("kv_kept"), KV_STORES)
            ffn(0)
            norm(1, PH["dn0"], R_LNG + 1, R_LNB + 1)

            act.wait_ge(ev("ln_x"), 2 * KB)
            act.dma_start(scratch["x"], x[:]).then_inc(ev("x_moved"), 16)
            act.dma_start(reset[:], ins["reset"]).then_inc(ev("lora_w_in"), 16)
            act.dma_start(w1s, ins["rwkv_w1"].rearrange("a (k p) n -> p (a k) n", p=P)).then_inc(ev("lora_w_in"), 16)
            act.dma_start(a1s, ins["rwkv_a1"].rearrange("a (k p) n -> p (a k) n", p=P)).then_inc(ev("lora_w_in"), 16)
            act.dma_start(g1s, ins["rwkv_g1"].rearrange("a (k p) n -> p (a k) n", p=P)).then_inc(ev("lora_w_in"), 16)
            act.dma_start(wa2[top, :], ins["rwkv_w2"][0]).then_inc(ev("lora_w_in"), 16)
            act.dma_start(wa2[low, :], ins["rwkv_a2"][0]).then_inc(ev("lora_w_in"), 16)

            def mixed_high(step):
                for j in range(KB):
                    act.wait_ge(ev("mt"), KB * step + j + 1)
                    A(xh[:, j, :], mt[:, j % 2, :], ACT.Copy).then_inc(op_hi, 1)

            def take_into(dst):
                def take(blk, s):
                    A(two(dst[:, bass.ds(blk, 1), :]), acc(s), ACT.Copy).then_inc(acc_free, 1)
                return take

            mixed_high(0)
            act.wait_ge(ev("sh_mm"), 1)
            A(sho[:].rearrange("p (a n) -> p a n", a=2), ps[0:9, 6:8, :], ACT.Copy).then_inc(ev("sh_taken"), 1)
            act.wait_ge(ev("sh_taken"), 1)
            act.dma_start(outs["ps"].rearrange("a b d -> (a b) d"), sho[0:1, :]).then_inc(ev("shift_kept"), 16)
            act.dma_start(outs["ss"].rearrange("a b d -> (a b) d"), sho[1:9, :]).then_inc(ev("shift_kept"), 16)
            product("r", take_into(rr))
            mixed_high(1)
            act.wait_ge(ev("mf_used"), KB)
            A(twa[top].rearrange("p (h n) -> p h n", h=2), ps[top, 4:6, 0:TH], ACT.Tanh).then_inc(ev("lora_out"), 1)
            product("k", take_into(kx))
            mixed_high(2)
            act.wait_ge(ev("mf_used"), KB * 2)
            A(twa[low].rearrange("p (h n) -> p h n", h=2), ps[low, 4:6, 0:TH], ACT.Copy).then_inc(ev("lora_out"), 1)
            product("v", take_into(vv))
            act.wait_ge(ev("mf_used"), KB * 3)
            A(two(sg[:, 0:1, :]), ps[:, 4:6, 0:TH], ACT.Sigmoid)
            A(two(sg[0:L_GATE - P, 1:2, :]), ps[0:L_GATE - P, 6:8, 0:TH], ACT.Sigmoid).then_inc(ev("proj_taken"), 1)

            act.wait_ge(ev("proj_taken"), 1)
            act.dma_start(scratch["sg"][:, 0], sg[:, 0, :]).then_inc(ev("shift_kept"), 16)
            act.dma_start(scratch["sg"][0:L_GATE - P, 1], sg[0:L_GATE - P, 1, :]).then_inc(ev("shift_kept"), 16)

            act.wait_ge(ev("cc_zero"), 1)
            for j in range(KB):
                act.wait_ge(ev("lora2_mm"), j + 1)
                b = 2 * (j % 2)
                A(cc[:, j, 0:PADP].rearrange("p (c n) -> p c n", n=CH + 1)[:, :, 1:], ps[:, b, :].rearrange("p (c n) -> p c n", n=CH),
                  ACT.Sigmoid, bias=col(R_W0, j))
                A(cc[:, j, PADP:].rearrange("p (c n) -> p c n", n=DT + 1)[:, :, 1:], ps[:, b + 1, 0:NS].rearrange("p (c n) -> p c n", n=DT),
                  ACT.Sigmoid, bias=col(R_W0, j)).then_inc(ev("lora2_taken"), 1)
            for j in range(KB):
                act.wait_ge(ev("lora2_mm"), KB + j + 1)
                b = 2 * (j % 2)
                A(bb[:, j, 0:SEQ], ps[:, b, :], ACT.Sigmoid, bias=col(R_A0, j))
                A(bb[:, j, SEQ:T], ps[:, b + 1, 0:NS], ACT.Sigmoid, bias=col(R_A0, j)).then_inc(ev("lora2_taken"), 1)
            act.wait_ge(ev("shift_kept"), 64)
            for t in range(KB + 1):
                if t < KB:
                    nc.scalar.mul(kk[:, t, :], kx[:, t, :], col(R_KK, t)).then_inc(ev("kk"), 1)
                    act.wait_ge(ev("kk"), t + 1)
                    if t >= 2:
                        act.wait_ge(ev("kk_sum"), t - 1)
                    A(ef2[:, t % 2, :], kk[:, t, :], ACT.Square).then_inc(ev("kk_sq"), 1)
                if t >= 1:
                    j = t - 1
                    act.wait_ge(ev("kk_sum"), j + 1)
                    if j >= 2:
                        act.wait_ge(ev("kk_norm"), j - 1)
                    A(nrm[j % 2].rearrange("p (h n) -> p h n", h=2), ps[:, 4 + 2 * (j % 2):6 + 2 * (j % 2), 0:TH], ACT.Sqrt
                      ).then_inc(ev("kk_root"), 1)

            def chunk_exp(c, sample=False, first=False):
                if not first:
                    act.wait_ge(ev("c_pre"), c)
                    act.wait_ge(ev("c_kv"), c)
                if sample:
                    v = cc[:, :, PADP:].rearrange("p k (b n) -> p k b n", n=DT + 1)
                    for j in range(KB):
                        o = ef[:, :, j, :].rearrange("p a (b t) -> p a b t", b=DB)
                        A(o[:, 0], v[:, j, :, 1:], ACT.Exp, scale=-KAPPA)
                        A(o[:, 1], v[:, j, :, 0:DT], ACT.Exp, scale=-KAPPA)
                        out = A(o[:, 2], v[:, j, :, 1:], ACT.Exp, scale=KAPPA)
                else:
                    A(ef[:, 0], cc[:, :, bass.ds(c * (CH + 1) + 1, CH)], ACT.Exp, scale=-KAPPA)
                    A(ef[:, 1], cc[:, :, bass.ds(c * (CH + 1), CH)], ACT.Exp, scale=-KAPPA)
                    out = A(ef[:, 2], cc[:, :, bass.ds(c * (CH + 1) + 1, CH)], ACT.Exp, scale=KAPPA)
                out.then_inc(ev("c_exp"), 1)

            def token_major(n):
                for dst, name, bank, taken in ((vtm, "tv", 0, "tok_v"), (btm, "tb", 4, "tok_b"), (ktm, "tk", 6, "tok_k")):
                    for g in range(2):
                        act.wait_ge(ev(name), 2 * n + (g + 1))
                        pr = slice(g * NP2, (g + 1) * NP2)
                        bk = ps[:, bank + g, :].rearrange("p (a n) -> p a n", a=NP2)
                        if name == "tv":
                            A(vtc[top, pr, :], bk[top, :, 0:HD], ACT.Copy)
                            A(vtc[low, pr, :], bk[low, :, HD:P], ACT.Copy)
                        A(dst[:, pr, :], bk, ACT.Copy).then_inc(ev(taken), 1)

            def invert(c, levels, ahead=None):
                for level in range(levels):
                    if level >= 1:
                        for g in range(2):
                            act.wait_ge(ev("y"), (c * LEVELS + level + 1) * 2 + (g - 1))
                            A(yc[:, g * NP2:(g + 1) * NP2, :], ps[:, 4 + g, 0:256].rearrange("p (a n) -> p a n", a=NP2),
                              ACT.Copy).then_inc(ev("yc"), 1)
                    for g in range(2):
                        act.wait_ge(ev("xup"), (c * LEVELS + level + 1) * 2 + (g - 1))
                        pr = slice(g * NP2, (g + 1) * NP2)
                        if level == 0:
                            act.wait_ge(ev("cleared"), c + 1)
                        A(xtb[top, pr, 0, :], xc[top, g, 1].bitcast(F32), ACT.Copy)
                        A(xtb[low, pr, 1, :], xc[low, g, 1].bitcast(F32), ACT.Copy).then_inc(ev("xtb"), 1)
                    if level == 1 and ahead:
                        ahead()
                for g in range(2):
                    act.wait_ge(ev("xx_mm"), 2 * c + (g + 1))
                    A(xf[:, g * NP2:(g + 1) * NP2, :], ps[:, 4 + g, :].rearrange("p (a n) -> p a n", a=NP2), ACT.Copy
                      ).then_inc(ev("xf"), 1)

            def step(c, sample_next=False):
                invert(c, LEVELS, lambda: chunk_exp(c + 1, sample_next))
                token_major(c + 1)
                for g in range(2):
                    act.wait_ge(ev("sup"), 2 * c + (g + 1))
                    pr = slice(g * NP2, (g + 1) * NP2)
                    A(sbd[top, pr, 0, :], S_c[top, pr, :], ACT.Copy)
                    A(sbd[low, pr, 1, :], S_c[low, pr, :], ACT.Copy).then_inc(ev("sbd"), 1)

            act.wait_ge(ev("prep"), KB)
            chunk_exp(0, first=True)
            token_major(0)
            with nc.scalar.Fori(0, NCH - 1) as c:
                step(c)
            step(NCH - 1, sample_next=True)
            act.wait_ge(ev("state_mm"), 1)
            A(stat_out[:], ps[:, 0, :].rearrange("p (a n) -> p a n", a=NPAIR), ACT.Copy).then_inc(ev("state_out"), 1)
            act.wait_ge(ev("state_out"), 1)
            for h, part in ((0, top), (1, low)):
                act.dma_start(outs["pw"].rearrange("a b (p h) v k -> h v (a b p) k", h=2)[h], stat_out[part]).then_inc(ev("state_kept"), 16)
            for t in range(NPAIR + 1):
                if t < NPAIR:
                    act.wait_ge(ev("s0_mm"), t + 1)
                    if t >= 2:
                        act.wait_ge(ev("sp_mm"), t - 1)
                    A(s0bd[t % 2].rearrange("p (q b) n -> p q (b n)", q=2), ps[:, 4 + 2 * (t % 2):6 + 2 * (t % 2), :], ACT.Copy
                      ).then_inc(ev("s0bd"), 1)
                if t >= 1:
                    act.wait_ge(ev("sp_mm"), t)
                    A(spc[:, t - 1], ps[:, 2 + (t - 1) % 2, :].rearrange("p (b n) -> p b n", b=DB), ACT.Copy).then_inc(ev("s0_done"), 1)
            invert(NCH, 3)
            for p in range(NPAIR):
                act.wait_ge(ev("sst"), p + 1)
                for h, part in ((0, top), (1, low)):
                    act.dma_start(outs["sw"][0, :, 2 * p + h].rearrange("b v k -> v b k"), spc[part, p]).then_inc(ev("state_kept"), 16)

            act.wait_ge(ev("state_kept"), STATE_STORES)
            act.dma_start(g2a[:], ins["rwkv_g2"][0, 0:P]).then_inc(ev("g2_in"), 16)
            act.dma_start(g2b[:], ins["rwkv_g2"][0, P:L_GATE]).then_inc(ev("g2_in"), 16)
            act.dma_start(sg_back[:, 0, :], scratch["sg"][:, 0]).then_inc(ev("g2_in"), 16)
            act.dma_start(sg_back[0:L_GATE - P, 1, :], scratch["sg"][0:L_GATE - P, 1]).then_inc(ev("g2_in"), 16)
            for s in range(2):
                split_high(PH["ro"], s, s)
            h2 = lambda ap: ap.rearrange("p (h n) -> p h n", h=2)
            for t in range(KB + 2):
                if t < KB:
                    act.wait_ge(ev("dev"), t + 1)
                    if t >= 2:
                        act.wait_ge(ev("var_mm"), t - 1)
                    A(f_sq[:, t % 2, :], f_dev[:, t % 3, :], ACT.Square).then_inc(ev("dev_sq"), 1)
                    act.wait_ge(ev("gate_mm"), t + 1)
                    if t >= 2:
                        act.wait_ge(ev("z"), t - 1)
                    A(h2(f_gt[:, t % 2, :]), ps[:, 6:8, 0:TH], ACT.Copy).then_inc(ev("gate"), 1)
                    act.wait_ge(ev("var_mm"), t + 1)
                    if t >= 2:
                        act.wait_ge(ev("hat"), t - 1)
                    A(h2(f_sd[:, t % 2, :]), ps[:, 4:6, 0:TH], ACT.Sqrt, bias=const("eps")[:, 1:2], scale=1.0 / HD).then_inc(ev("sd"), 1)
                if 1 <= t <= KB:
                    act.wait_ge(ev("hat"), t)
                    o = f_dev[:, (t - 1) % 3, :]
                    A(o, o, ACT.Identity, bias=col(R_GB, t - 1), scale=col(R_GW, t - 1)).then_inc(ev("affine"), 1)
                if t >= 2:
                    act.wait_ge(ev("z"), t - 1)
                    A(xh[:, t - 2, :], f_dev[:, (t - 2) % 3, :], ACT.Copy).then_inc(op_hi, 1)
            act.wait_ge(ev("x_moved"), 16 * (KB + 1))
            scale_x(2)
            product("ro")
            norm(2, PH["ro"], R_LNG + 2, R_LNB + 2)
            act.wait_ge(op_ready, KB * (OP["f1"] + 1))
            scale_x(3)
            ffn(1)
            norm(3, PH["dn1"], R_LNG + 3, R_LNB + 3)
            for t in range(5):
                n_ = P if t < 4 else NS
                act.wait_ge(ev("y_mm"), t + 1)
                A(yout[0:n_, t, :].rearrange("p (a n) -> p a n", a=2), ps[0:n_, 2 * (t % 2):2 * (t % 2) + 2, :], ACT.Copy).then_inc(ev("y_taken"), 1)
                act.wait_ge(ev("y_taken"), t + 1)
                dst = outs["yp"][0, t * P:(t + 1) * P, :] if t < 4 else outs["ys"].rearrange("b t d -> (b t) d")
                act.dma_start(dst, yout[0:n_, t, :]).then_inc(stored, 16)
                outs_stored[0] += 1
            act.wait_ge(stored, 16 * outs_stored[0])

        @block.vector
        def _(dve):
            V = nc.vector
            dv = sem("dv")
            steps = [0]

            def link(ins_):
                steps[0] += 1
                ins_.then_inc(dv, 1)
                dve.wait_ge(dv, steps[0])

            def split_low(j):
                V.tensor_tensor(xl[:, j, :], x[:, j, :], xh[:, j, :].bitcast(F32), ALU.subtract).then_inc(op_ready, 1)

            def add_blocks(ph, i_x):
                per = 2 if ph.ffn_down else 1
                dve.wait_ge(ev("x_scaled"), i_x)
                with V.Fori(0, KB // 2) as i:
                    for a in range(2):
                        dve.wait_ge(wslot_free, i * (2 * per) + (ph.n0 + per * (a + 1) + 2))
                        blk = two(x[:, bass.ds(2 * i + a, 1), :])
                        V.tensor_tensor(blk, blk, acc(a), ALU.add).then_inc(acc_free, 1)

            def norm(i_ln):
                mean, var, tmp = lnw[:, 0, :], lnw[:, 1, :], lnw[:, 2, :]
                dve.wait_ge(ev("ln_mean"), i_ln + 1)
                link(V.tensor_copy(mean.rearrange("p (h n) -> p h n", h=2), ps[:, 4:6, 0:TH]))
                link(V.tensor_tensor(tmp, mean, mean, ALU.mult))
                dve.wait_ge(ev("ln_sum"), KB * (i_ln + 1))
                V.tensor_tensor(var.rearrange("p (h n) -> p h n", h=2), ps[:, 6:8, 0:TH],
                                tmp.rearrange("p (h n) -> p h n", h=2), ALU.subtract).then_inc(ev("ln_var"), 1)
                dve.wait_ge(ev("ln_sd"), i_ln + 1)
                link(V.reciprocal(tmp, var))
                for j in range(KB):
                    link(V.tensor_tensor(x[:, j, :], x[:, j, :], mean, ALU.subtract))
                    V.tensor_tensor(x[:, j, :], x[:, j, :], tmp, ALU.mult).then_inc(ev("ln_hat"), 1)
                    if i_ln in (0, 2) and j >= 1:
                        dve.wait_ge(op_hi, KB * OP["f0" if i_ln == 0 else "f1"] + j)
                        split_low(j - 1)
                if i_ln in (0, 2):
                    dve.wait_ge(op_hi, KB * (OP["f0" if i_ln == 0 else "f1"] + 1))
                    split_low(KB - 1)

            def take_state(p):
                dve.wait_ge(ev("sst_mm"), p + 1)
                V.tensor_tensor(spc[:, p], spc[:, p], ps[:, 6 + p % 2, :].rearrange("p (b k) -> p b k", b=DB), ALU.add
                                ).then_inc(ev("sst"), 1)

            def ffn(i_ffn):
                up = PH[f"gu{i_ffn}"]
                with V.Fori(0, FB // 2) as i:
                    for q in range(2):
                        dve.wait_ge(wslot_free, 4 * i + (up.n0 + 2 * q + 4))
                        dve.wait_ge(gate_free, 2 * i + (up.g0 + q + 3))
                        dve.wait_ge(hid_hi, 2 * i + (up.g0 + q + 1))
                        V.tensor_tensor(hbuf[:, q, :].rearrange("p (h n) -> p h n", h=2),
                                        gbuf[:, q, :].rearrange("p (h n) -> p h n", h=2), acc(2 * q + 1), ALU.mult
                                        ).then_inc(up_free, 1)
                        dve.wait_ge(up_free, 2 * i + (up.g0 + q + 3))
                        dve.wait_ge(hid_hi, 2 * i + (up.g0 + q + 3))
                        V.tensor_tensor(hl[:, bass.ds(2 * i + q, 1), :], hbuf[:, q:q + 1, :],
                                        hh[:, bass.ds(2 * i + q, 1), :].bitcast(F32), ALU.subtract).then_inc(hid_lo, 1)
                add_blocks(PH[f"dn{i_ffn}"], 2 * i_ffn + 2)

            dve.wait_ge(ev("pT"), 1)
            link(V.tensor_copy(prm[:], ps[:, 5, 0:KB * NROW].rearrange("p (k n) -> p k n", k=KB)))
            V.tensor_copy(bqkv[:, 0:KB], prm[:, :, R_BQ])
            V.tensor_copy(bqkv[:, KB:QB], prm[:, 0:4, R_BKV])
            V.tensor_scalar(omka[:], prm[:, :, R_KA], -1.0, 1.0, ALU.mult, ALU.add).then_inc(ev("setup_taken"), 1)
            dve.wait_ge(ev("pT"), 2)
            V.tensor_copy(toep_sb[:], ps[0:HEADS, 6, 0:TOEP]).then_inc(ev("setup_taken"), 1)
            dve.wait_ge(ev("s_in"), 32)
            V.tensor_scalar(sink[:], sink[:], -1.0, None, ALU.mult)
            V.tensor_scalar(sink_s[:], sink_s[:], -1.0, None, ALU.mult).then_inc(ev("setup_taken"), 1)
            dve.wait_ge(ev("xT_taken"), KB + 1)
            for j in range(KB):
                dve.wait_ge(op_hi, j + 1)
                split_low(j)
            dve.wait_ge(ev("table_out"), 16)
            dve.wait_ge(ev("setup_taken"), 3)
            with V.Fori(0, QB // 2) as i:
                for a in range(2):
                    dve.wait_ge(wslot_free, 2 * i + (a + 3))
                    V.tensor_scalar(two(qkvT[:, bass.ds(2 * i + a, 1), :]), acc(a), bqkv[:, bass.ds(2 * i + a, 1)], None,
                                    ALU.add).then_inc(acc_free, 1)

            dve.wait_ge(ev("bias_in"), 32)
            units = [(qb, g) for qb in range(SEQ // WIN) for g in range(KV)]
            U = len(units)
            for t in range(U + 3):
                if t < U:
                    qb, g = units[t]
                    slot, W = t % 2, WIN if qb == 0 else 2 * WIN
                    dve.wait_ge(ev("s_mm"), t + 1)
                    if t >= 2:
                        dve.wait_ge(ev("pt_mm"), t - 1)
                    sc = S[:, slot, 0:GROUP * W].rearrange("p (i w) -> p i w", w=W)
                    banks = ps[:, 2 * slot:2 * slot + 2, 0:2 * W].rearrange("p a (i w) -> p a i w", w=W)
                    for a in range(2):
                        out = V.scalar_tensor_tensor(sc[:, 2 * a:2 * a + 2, :], banks[:, a], HD ** -0.5,
                                                     biasT[:, g * GROUP + 2 * a:g * GROUP + 2 * a + 2, 2 * WIN - W:2 * WIN],
                                                     ALU.mult, ALU.add)
                    out.then_inc(ev("s_taken"), 1)
                    dve.wait_ge(ev("s_taken"), t + 1)
                    st = stat[:, slot]
                    link(V.tensor_reduce(st[:, 4, 0:GROUP], sc, AX_X, ALU.max))
                    link(V.scalar_tensor_tensor(st[:, 0, 0:GROUP], st[:, 4, 0:GROUP], -1.0, sink[:, g * GROUP:(g + 1) * GROUP],
                                                ALU.mult, ALU.min))
                    V.tensor_tensor(st[:, 2, 0:GROUP], st[:, 0, 0:GROUP], sink[:, g * GROUP:(g + 1) * GROUP],
                                    ALU.subtract).then_inc(ev("s_max"), 1)
                if 1 <= t <= U:
                    u = t - 1
                    slot, W = u % 2, WIN if units[u][0] == 0 else 2 * WIN
                    sc = S[:, slot, 0:GROUP * W].rearrange("p (i w) -> p i w", w=W)
                    st = stat[:, slot]
                    dve.wait_ge(ev("s_exp"), u + 1)
                    link(V.tensor_tensor(st[:, 4, 0:GROUP], st[:, 1, 0:GROUP], st[:, 3, 0:GROUP], ALU.add))
                    link(V.reciprocal(st[:, 4, 0:GROUP], st[:, 4, 0:GROUP]))
                    V.tensor_tensor(sc, sc, st[:, 4, 0:GROUP].unsqueeze(2).to_broadcast([P, GROUP, W]), ALU.mult
                                    ).then_inc(ev("probs"), 1)
                if t >= 4 and t % 2 == 0:
                    pair = (t - 4) // 2
                    qb, G = pair // 2, pair % 2
                    blk, tok = slice(G * GROUP, (G + 1) * GROUP), slice(qb * WIN, (qb + 1) * WIN)
                    bank = ps[:, 6 + pair % 2, :].rearrange("p (i q) -> p i q", i=GROUP)
                    dve.wait_ge(ev("o_mm"), 2 * pair + 2)
                    link(V.tensor_copy(xh[:, blk, tok], bank))
                    V.tensor_tensor(xl[:, blk, tok], bank, xh[:, blk, tok].bitcast(F32), ALU.subtract).then_inc(ev("o_taken"), 1)
            for G in range(2):
                V.tensor_copy(qs[:, G].rearrange("p b (i t) -> p i b t", i=GROUP),
                              qkvT[:, G * GROUP:(G + 1) * GROUP, SEQ:T].rearrange("p i (b t) -> p i b t", b=DB))
                out = V.tensor_copy(ckT[:, G, :, WIN:KEYS], qkvT[:, KB + G, SEQ:T].rearrange("p (b t) -> p b t", b=DB))
            out.then_inc(ev("ckT_new"), 1)
            dve.wait_ge(ev("ss_mm"), 1)
            st = stat[:, 0]
            sc = S[:, 0, :].rearrange("p (b w) -> p b w", b=DB)
            for q in range(3):
                n_ = 3 if q < 2 else 2
                out = V.scalar_tensor_tensor(sc[:, 3 * q:3 * q + n_, :],
                                             ps[:, 4 + q, 0:n_ * KEYS].rearrange("p (b w) -> p b w", w=KEYS), HD ** -0.5,
                                             bias_s[:].unsqueeze(1).to_broadcast([P, n_, KEYS]), ALU.mult, ALU.add)
            link(out)
            link(V.tensor_reduce(st[:, 4, :], sc, AX_X, ALU.max))
            link(V.tensor_scalar(st[:, 0, :], st[:, 4, :], -1.0, sink_s[:], ALU.mult, ALU.min))
            V.tensor_scalar(st[:, 2, :], st[:, 0, :], sink_s[:], None, ALU.subtract).then_inc(ev("ss_max"), 1)
            dve.wait_ge(ev("ss_exp"), 1)
            link(V.tensor_tensor(st[:, 4, :], st[:, 1, :], st[:, 3, :], ALU.add))
            link(V.reciprocal(st[:, 4, :], st[:, 4, :]))
            V.tensor_tensor(sc, sc, st[:, 4, :].unsqueeze(2).to_broadcast([P, DB, KEYS]), ALU.mult).then_inc(ev("s_probs"), 1)
            dve.wait_ge(ev("so_mm"), 1)
            bank = ps[:, 7, :].rearrange("p (k n) -> p k n", k=KB)
            link(V.tensor_copy(xh[:, :, SEQ:T], bank))
            V.tensor_tensor(xl[:, :, SEQ:T], bank, xh[:, :, SEQ:T].bitcast(F32), ALU.subtract).then_inc(ev("att_ready"), 1)

            add_blocks(PH["wo"], 1)
            norm(0)
            dve.wait_ge(ev("kv_kept"), KV_STORES)
            ffn(0)
            norm(1)

            dve.wait_ge(ev("ln_x"), 2 * KB)
            V.tensor_copy(shc[:, :, 0:1], x[:, :, SEQ - 1:SEQ])
            V.tensor_copy(shc[:, :, 1:9], x[:, :, SEQ:T].rearrange("p k (b t) -> p k b t", t=DT)[:, :, :, DT - 1]
                          ).then_inc(ev("shc"), 1)
            V.tensor_tensor(xx[:, :, 1:T], x[:, :, 0:T - 1], x[:, :, 1:T], ALU.subtract)
            link(V.tensor_scalar(xx[:, :, 0:1], x[:, :, 0:1], -1.0, None, ALU.mult))
            for j in range(KB):
                out = V.tensor_tensor(xx[:, j, SEQ:T].rearrange("p (b t) -> p b t", t=DT)[:, :, 0],
                                      prm[:, j, R_SHIFT:R_SHIFT + DB],
                                      x[:, j, SEQ:T].rearrange("p (b t) -> p b t", t=DT)[:, :, 0], ALU.subtract)
            link(out)

            def mix_operand(step, c):
                if step:
                    dve.wait_ge(wslot_free, PH[("", "r", "k")[step]].n1 + 2)
                for j in range(KB + 1):
                    if j < KB:
                        V.scalar_tensor_tensor(mt[:, j % 2, :], xx[:, j, :], col(R_MIX + c, j), x[:, j, :], ALU.mult, ALU.add
                                               ).then_inc(ev("mt"), 1)
                    if j >= 1:
                        dve.wait_ge(op_hi, KB * (2 + step) + j)
                        dve.wait_ge(ev("mt"), KB * step + j)
                        V.tensor_tensor(xl[:, j - 1, :], mt[:, (j - 1) % 2, :], xh[:, j - 1, :].bitcast(F32), ALU.subtract
                                        ).then_inc(op_ready, 1)
                        dve.wait_ge(op_ready, KB * (2 + step) + j)

            def mix_plain(step, c):
                for j in range(KB):
                    if step or j >= 2:
                        dve.wait_ge(ev("mf_used"), KB * step + j - 1)
                    V.scalar_tensor_tensor(mf[:, j % 2, :], xx[:, j, :], col(R_MIX + c, j), x[:, j, :], ALU.mult, ALU.add
                                           ).then_inc(ev("mf"), 1)

            mix_operand(0, 0)
            mix_plain(0, 1)
            mix_operand(1, 2)
            mix_plain(1, 4)
            mix_operand(2, 3)
            mix_plain(2, 5)

            dve.wait_ge(ev("proj_taken"), 1)
            dve.wait_ge(acc_free, PH["v"].m1 + 2)
            dve.wait_ge(ev("x_moved"), 16)
            V.memset(cc[:], 0.0).then_inc(ev("cc_zero"), 1)
            dve.wait_ge(ev("lora2_taken"), KB)
            dve.wait_ge(ev("lora_w_in"), 16 * 6)
            for j in range(KB):
                V.tensor_tensor_scan(cc[:, j, :], reset[:], cc[:, j, :], 0.0, ALU.mult, ALU.add)
            for j in range(KB):
                nr = nrm[j % 2]
                dve.wait_ge(ev("kk_root"), j + 1)
                link(V.tensor_scalar(nr, nr, 1e-12, None, ALU.max))
                link(V.reciprocal(nr, nr))
                V.tensor_tensor(kk[:, j, :], kk[:, j, :], nr, ALU.mult).then_inc(ev("kk_norm"), 1)
            dve.wait_ge(ev("lora2_taken"), 2 * KB)
            dve.wait_ge(ev("kk_norm"), KB)
            for j in range(KB):
                nr = nrm[j % 2]
                link(V.tensor_scalar(nr, bb[:, j, :], col(R_KA, j), omka[:, j:j + 1], ALU.mult, ALU.add))
                V.tensor_tensor(kx[:, j, :], kx[:, j, :], nr, ALU.mult)
                V.tensor_tensor(bb[:, j, :], kk[:, j, :], bb[:, j, :], ALU.mult).then_inc(ev("prep"), 1)

            def chunk_pre(c, q, sample=False):
                tok = bass.ds(c * CH, CH)
                dve.wait_ge(ev("c_exp"), c + 1)
                V.tensor_tensor(zr[q][:, :, 1, :], rr[:, :, tok], ef[:, 0], ALU.mult)
                V.scalar_tensor_tensor(zr[q][:, :, 0, :], kk[:, :, tok], -1.0, ef[:, 1], ALU.mult, ALU.mult
                                       ).then_inc(ev("z_done"), 1)
                if sample:
                    V.tensor_copy(pc[q][:], ef[:, 0].rearrange("p k (b t) -> p k b t", t=DT)[:, :, :, DT - 1])
                else:
                    V.tensor_copy(pc[q][:, :, 0:1], ef[:, 0, :, CH - 1:CH])
                for h, part in ((0, top), (1, low)):
                    V.tensor_tensor(bbd[part, :, h, :], bb[part, :, tok], ef[part, 2], ALU.mult)
                dve.wait_ge(ev("z_done"), c + 1)
                V.tensor_copy(zbd[q][top, :, 0, :], zr[q][top, :, 0, :])
                V.tensor_copy(zbd[q][low, :, 1, :], zr[q][low, :, 0, :]).then_inc(ev("c_pre"), 1)

            def gram_masks(n, q, src, full, comp, name, sample=False, first=False):
                kind = "s" if sample else "p"
                strict, incl = const("strict_" + kind), const("incl_" + kind)
                for g in range(2):
                    dve.wait_ge(ev("g" + name), 2 * n + (g + 1))
                    pr = slice(g * NP2, (g + 1) * NP2)
                    gram = ps[:, src + g, :].rearrange("p (a z t) -> p a z t", a=NP2, z=2)
                    V.tensor_tensor(comp[q][:, pr, :], gram[:, :, 1, :], incl.unsqueeze(1).to_broadcast([P, NP2, CH]), ALU.mult)
                    if name == "b":
                        if not first:
                            dve.wait_ge(ev("xtb"), (n * LEVELS) * 2 + (g - 1))
                        V.tensor_tensor(xc[:, g, 1], gram[:, :, 0, :],
                                        const("level0").unsqueeze(1).to_broadcast([P, NP2, CH]), ALU.mult
                                        ).then_inc(ev("x0"), 1)
                    for h in range(2):
                        out = V.tensor_tensor(full[:, pr, h, :], gram[:, :, 0, :],
                                              strict[:, h * CH:(h + 1) * CH].unsqueeze(1).to_broadcast([P, NP2, CH]), ALU.mult)
                    out.then_inc(ev("gram_" + name), 1)

            def invert(c, levels, ahead=None):
                eye = const("ident2").unsqueeze(1).to_broadcast([P, NP2, CH])
                for g in range(2):
                    dve.wait_ge(ev("x0"), 2 * c + (g + 1))
                    V.tensor_tensor(xc[:, g, 1], xc[:, g, 1].bitcast(F32), eye, ALU.add)
                    dve.wait_ge(ev("y"), (c * LEVELS + 1) * 2 + (g - 1))
                    V.tensor_tensor(xc[:, g, 0], ps[:, 4 + g, 0:256].rearrange("p (a t) -> p a t", a=NP2), eye, ALU.add
                                    ).then_inc(ev("xup"), 1)
                for level in range(1, levels):
                    for g in range(2):
                        pr = slice(g * NP2, (g + 1) * NP2)
                        dve.wait_ge(ev("yc"), (c * (LEVELS - 1) + level) * 2 + (g - 1))
                        V.tensor_copy(ybd[top, pr, 0, :], yc[top, pr, :].bitcast(F32))
                        V.tensor_copy(ybd[low, pr, 1, :], yc[low, pr, :].bitcast(F32)).then_inc(ev("ybd"), 1)
                    for g in range(2):
                        half = 1 if level == levels - 1 else 0
                        dve.wait_ge(ev("xm"), (c * (LEVELS - 1) + level) * 2 + (g - 1))
                        cur = xc[:, g, half:].rearrange("p x a t -> p (x a) t")
                        V.tensor_tensor(cur, cur.bitcast(F32), ps[:, 6 + g, half * 256:].rearrange("p (a t) -> p a t", t=CH), ALU.add
                                        ).then_inc(ev("xup"), 1)
                    if level == 3 and ahead:
                        ahead()
                for g in range(2):
                    pr = slice(g * NP2, (g + 1) * NP2)
                    dve.wait_ge(ev("lx"), 2 * c + (g + 1))
                    dve.wait_ge(ev("imx"), 2 * c + (g + 1))
                    V.tensor_tensor(lm[:, pr, :], ps[:, 6 + g, :].rearrange("p (a n) -> p a n", a=NP2),
                                    imx[:, pr].rearrange("p a h t -> p a (h t)"), ALU.add).then_inc(ev("res"), 1)

            def state_step(c, q, sample=False, ahead_b=None, ahead_k=None):
                def quarter(bank, half, g):
                    return ps[:, bank + g, half * 256:(half + 1) * 256].rearrange("p (a t) -> p a t", a=NP2)
                prs = [slice(g * NP2, (g + 1) * NP2) for g in range(2)]
                for g, pr in enumerate(prs):
                    dve.wait_ge(ev("u"), 2 * c + (g + 1))
                    V.tensor_copy(uc[:, pr, :], quarter(4, 1, g)).then_inc(ev("uc"), 1)
                for g, pr in enumerate(prs):
                    dve.wait_ge(ev("fix"), 2 * c + (g + 1))
                    V.tensor_tensor(xtf[:, pr].rearrange("p a h t -> p a (h t)"), xtb[:, pr].rearrange("p a h t -> p a (h t)").bitcast(F32),
                                    ps[:, 6 + g, :].rearrange("p (a n) -> p a n", a=NP2), ALU.add).then_inc(ev("xtf"), 1)
                if ahead_b:
                    ahead_b()
                for g, pr in enumerate(prs):
                    dve.wait_ge(ev("sa"), 2 * c + (g + 1))
                    bank = quarter(6, 0, g)
                    V.tensor_copy(sac[:, pr, :], bank)
                    V.tensor_copy(sabd[top, pr, 0, :], bank[top])
                    V.tensor_copy(sabd[low, pr, 1, :], bank[low]).then_inc(ev("sac"), 1)
                if ahead_k:
                    ahead_k()
                for g, pr in enumerate(prs):
                    dve.wait_ge(ev("o"), 2 * c + (g + 1))
                    if sample:
                        V.tensor_tensor(kk[:, pr, bass.ds(c * CH, CH)], quarter(4, 0, g), ef[:, 0, pr, :], ALU.add)
                    else:
                        V.tensor_scalar(kk[:, pr, bass.ds(c * CH, CH)], quarter(4, 0, g), 1.0, None, ALU.mult)
                if sample:
                    return
                for g, pr in enumerate(prs):
                    dve.wait_ge(ev("st"), 2 * c + (g + 1))
                    V.tensor_tensor(S_c[:, pr, :], S_c[:, pr, :], quarter(6, 1, g), ALU.add).then_inc(ev("sadd"), 1)
                for g, pr in enumerate(prs):
                    dve.wait_ge(ev("sadd"), 2 * c + (g + 1))
                    V.tensor_tensor(S_c[:, pr, :], S_c[:, pr, :], pc[q][:, pr, 0:1].to_broadcast([P, NP2, HD]), ALU.mult
                                    ).then_inc(ev("sup"), 1)

            def step(c, q, sample_next=False):
                invert(c, LEVELS, lambda: chunk_pre(c + 1, 1 - q, sample_next))
                state_step(c, q,
                           ahead_b=lambda: gram_masks(c + 1, 1 - q, 0, lzb, lrb, "b", sample_next),
                           ahead_k=lambda: gram_masks(c + 1, 1 - q, 2, lzk, lrk, "k", sample_next))

            dve.wait_ge(ev("wkv_zero"), 1)
            chunk_pre(0, 0)
            gram_masks(0, 0, 0, lzb, lrb, "b", first=True)
            gram_masks(0, 0, 2, lzk, lrk, "k", first=True)
            with V.Fori(0, NCH // 2 - 1) as i:
                for q in range(2):
                    step(2 * i + q, q)
            step(NCH - 2, 0)
            step(NCH - 1, 1, sample_next=True)
            for t in (bbd, kbd):
                for p in range(NPAIR):
                    out = V.tensor_tensor(t[:, p].rearrange("p h (b t) -> p h b t", t=DT),
                                          t[:, p].rearrange("p h (b t) -> p h b t", t=DT),
                                          pc[0][:, p, :].unsqueeze(1).unsqueeze(3).to_broadcast([P, 2, DB, DT]), ALU.mult)
            out.then_inc(ev("hats"), 1)
            for p in range(NPAIR):
                if p >= 1:
                    dve.wait_ge(ev("sp_mm"), p)
                V.tensor_tensor(dpc[:], const("ident2").unsqueeze(1).to_broadcast([P, DB, HD]),
                                pc[0][:, p, :].unsqueeze(2).to_broadcast([P, DB, HD]), ALU.mult).then_inc(ev("dpc"), 1)
                dve.wait_ge(ev("zs_mm"), p + 1)
                bank = ps[:, p % 2, 0:P].rearrange("p (b z t) -> p b z t", b=DB, z=2)
                V.tensor_copy(sbd[top, p, 0, :].rearrange("p (b t) -> p b t", b=DB), bank[top, :, 0, :])
                V.tensor_copy(sbd[low, p, 1, :].rearrange("p (b t) -> p b t", b=DB), bank[low, :, 0, :])
                V.tensor_copy(ef[:, 0, p, :].rearrange("p (b t) -> p b t", b=DB), bank[:, :, 1, :]).then_inc(ev("zs_taken"), 1)
            invert(NCH, 3)
            state_step(NCH, 0, sample=True)
            for p in range(NPAIR):
                if p >= 2:
                    dve.wait_ge(ev("sst_mm"), p - 1)
                for which, src in ((0, btm), (1, ktm)):
                    for h, part in ((0, top), (1, low)):
                        out = V.tensor_tensor(bkm(p, which)[part].rearrange("p (b k) -> p b k", b=DB), src[part, p, h * HD:(h + 1) * HD].unsqueeze(1).to_broadcast([HD, DB, HD]),
                                              const("seqmask")[part].unsqueeze(2).to_broadcast([HD, DB, HD]), ALU.mult)
                out.then_inc(ev("bkm"), 1)
                if p >= 1:
                    take_state(p - 1)
            take_state(NPAIR - 1)
            dve.wait_ge(ev("state_kept"), STATE_STORES)

            h2 = lambda ap: ap.rearrange("p (h n) -> p h n", h=2)
            for t in range(KB + 3):
                if t < KB:
                    V.scalar_tensor_tensor(f_rk[:, t % 2, :], rr[:, t, :], col(R_RK, t), kx[:, t, :], ALU.mult, ALU.mult
                                           ).then_inc(ev("rk"), 1)
                if 1 <= t <= KB:
                    u = t - 1
                    dve.wait_ge(ev("f_sums"), u + 1)
                    if u >= 3:
                        dve.wait_ge(op_ready, KB * OP["z"] + u - 2)
                    V.scalar_tensor_tensor(h2(f_dev[:, u % 3, :]), ps[:, 2:4, 0:TH], -1.0 / HD, h2(kk[:, u, :]), ALU.mult, ALU.add
                                           ).then_inc(ev("dev"), 1)
                    V.tensor_tensor(h2(f_bon[:, u % 3, :]), ps[:, 0:2, 0:TH], h2(vv[:, u, :]), ALU.mult).then_inc(ev("bon"), 1)
                if 2 <= t <= KB + 1:
                    u = t - 2
                    dve.wait_ge(ev("sd"), u + 1)
                    link(V.reciprocal(f_sd[:, u % 2, :], f_sd[:, u % 2, :]))
                    V.tensor_tensor(f_dev[:, u % 3, :], f_dev[:, u % 3, :], f_sd[:, u % 2, :], ALU.mult).then_inc(ev("hat"), 1)
                if t >= 3:
                    u = t - 3
                    dve.wait_ge(ev("bonused"), u + 1)
                    dve.wait_ge(ev("gate"), u + 1)
                    V.tensor_tensor(f_dev[:, u % 3, :], f_dev[:, u % 3, :], f_gt[:, u % 2, :], ALU.mult).then_inc(ev("z"), 1)

            add_blocks(PH["ro"], 3)
            norm(2)
            ffn(1)
            norm(3)


OUTPUTS = [("yp", (1, SEQ, D)), ("ys", (DB, DT, D)), ("pk", (1, 1, WIN, KV, HD)), ("pv", (1, 1, WIN, KV, HD)),
           ("ps", (1, 1, D)), ("pw", (1, 1, HEADS, HD, HD)), ("sk", (1, DB, WIN, KV, HD)), ("sv", (1, DB, WIN, KV, HD)),
           ("ss", (1, DB, D)), ("sw", (1, DB, HEADS, HD, HD))]
INPUTS = ["x_prompt", "x_sample", "cache_win_k", "cache_win_v", "state_shift", "state_wkv", "rel_bias", "ln_g", "ln_b",
          "attn_w_qkv", "attn_b_qkv", "attn_w_o", "attn_b_o", "attn_sinks", "rwkv_mix", "rwkv_w_rkv", "rwkv_w0",
          "rwkv_w1", "rwkv_w2", "rwkv_a0", "rwkv_a1", "rwkv_a2", "rwkv_g1", "rwkv_g2", "rwkv_k_k", "rwkv_k_a",
          "rwkv_r_k", "rwkv_ln_w", "rwkv_ln_b", "rwkv_w_o", "ffn_w_gu", "ffn_w_down"]


def kernel(**inputs):
    import concourse.bacc as bacc
    from concourse.bass_utils import run_bass_kernel_spmd

    nc = bacc.Bacc("TRN2", target_bir_lowering=False, num_devices=1)
    arrays, ins = {}, {}
    for name in INPUTS:
        arrays["in_" + name] = np.ascontiguousarray(inputs[name])
        ins[name] = nc.dram_tensor("in_" + name, inputs[name].shape, F32, kind="ExternalInput").ap()
    arrays["in_constants"] = constants()
    ins["constants"] = nc.dram_tensor("in_constants", arrays["in_constants"].shape, F32, kind="ExternalInput").ap()
    for name, table in (("onehot", bucket_table()), ("reset", scan_resets())):
        arrays["in_" + name] = table
        ins[name] = nc.dram_tensor("in_" + name, table.shape, F32, kind="ExternalInput").ap()
    outs = {name: nc.dram_tensor("out_" + name, shape, F32, kind="ExternalOutput").ap() for name, shape in OUTPUTS}
    scratch = {"table": nc.dram_tensor("table", (HEADS, TOEP), F32, kind="Internal").ap(),
               "spread": nc.dram_tensor("spread", (HEADS, P, TOEP), F32, kind="Internal").ap(),
               "sg": nc.dram_tensor("sg_kept", (P, 2, T), F32, kind="Internal").ap(),
               "x": nc.dram_tensor("x_kept", (P, KB, T), F32, kind="Internal").ap()}
    build_program(nc, ins, outs, scratch)
    r = run_bass_kernel_spmd(nc, [arrays], core_ids=[0])
    return tuple(r.results[0]["out_" + name] for name, _ in OUTPUTS)
```
